# Optimizing a Trainium2 kernel written in Bass

```python
import math
import jax
import jax.numpy as jnp
from jax import lax
import numpy as np

D_MODEL = 1024
BATCH = 1
SEQ = 1024
DEPTH = 1
DEC_BATCH = 8
DEC_SEQ = 1
PAST_LEN = 1024
PAGE_SIZE = 128

HEAD_DIM = 64
NSA_HEADS = 8
CMP_BLOCK = 32
SEL_BLOCK = 64
TOP_N = 16
WINDOW = 512
DIFF_HEADS = 4
DIFF_KV_HEADS = 2
DIFF_GROUP = DIFF_HEADS // DIFF_KV_HEADS
DIFF_VDIM = 2 * HEAD_DIM
NSA_WIDTH = NSA_HEADS * HEAD_DIM
DIFF_WIDTH = DIFF_HEADS * DIFF_VDIM
D_FF = ((8 * D_MODEL + 3 * 256 - 1) // (3 * 256)) * 256
Q_BLOCK = 128
CACHE_SIZES = (HEAD_DIM, HEAD_DIM, HEAD_DIM, HEAD_DIM, DIFF_KV_HEADS * 2 * HEAD_DIM, DIFF_KV_HEADS * DIFF_VDIM)
CACHE_W = sum(CACHE_SIZES)
WIN_W = 2 * HEAD_DIM
IN_SIZES = (NSA_WIDTH, CACHE_W, WIN_W, 3 * NSA_HEADS, DIFF_HEADS * 2 * HEAD_DIM, 2 * D_MODEL)
IN_W = sum(IN_SIZES)
FORCE_SCORE = 1e9
NEG_INF = -1e30
EPS = 1e-6

kernel_name = 'nsa_diffattn_gated_merge_step'

def _offsets(sizes):
    out, acc = [], 0
    for s in sizes[:-1]:
        acc += s
        out.append(acc)
    return out

def _w_buf():
    return min(WINDOW, PAST_LEN)

def _rms(x, g):
    xf = x.astype(jnp.float32)
    y = xf * lax.rsqrt(jnp.mean(xf * xf, axis=-1, keepdims=True) + EPS)
    return (y * g.astype(jnp.float32)).astype(x.dtype)

def _alibi(n):
    return 2.0 ** (-8.0 * jnp.arange(1, n + 1, dtype=jnp.float32) / n)

def _masked_softmax(s, mask):
    s = jnp.where(mask, s, NEG_INF)
    m = jnp.max(s, axis=-1, keepdims=True)
    e = jnp.where(mask, jnp.exp(s - m), 0.0)
    return e / jnp.maximum(jnp.sum(e, axis=-1, keepdims=True), 1e-30)

def _sdpa(q, k, v, dist, mask, slopes):
    s = jnp.einsum('...qhd,...kd->...hqk', q, k, preferred_element_type=jnp.float32) * (HEAD_DIM ** -0.5)
    s = s - slopes[:, None, None] * dist.astype(jnp.float32)[..., None, :, :]
    p = _masked_softmax(s, mask[..., None, :, :])
    o = jnp.einsum('...hqk,...kv->...qhv', p.astype(v.dtype), v)
    return o, p

def _map_query_blocks(fn, q_pos, q):
    B, T = q.shape[:2]
    qb = min(Q_BLOCK, T)
    nb = -(-T // qb)
    pad = nb * qb - T
    pos_b = jnp.pad(q_pos, (0, pad), mode='edge').reshape(nb, qb)
    q_b = jnp.pad(q, [(0, 0), (0, pad)] + [(0, 0)] * (q.ndim - 2))
    q_b = jnp.moveaxis(q_b.reshape(B, nb, qb, *q.shape[2:]), 1, 0)
    out = lax.map(lambda args: fn(*args), (pos_b, q_b))
    out = jnp.moveaxis(out, 0, 1)
    return out.reshape(B, nb * qb, *out.shape[3:])[:, :T]

def _append(past, new, total):
    parts = [new] if past is None else [past, new]
    k = sum(p.shape[1] for p in parts)
    if total > k:
        parts.append(jnp.zeros((new.shape[0], total - k, new.shape[2]), new.dtype))
    return jnp.concatenate(parts, axis=1) if len(parts) > 1 else parts[0]

def _window_banded(q, k, v, slopes):
    B, T, H, D = q.shape
    qb = min(Q_BLOCK, T)
    nb = T // qb
    span = qb + WINDOW
    kp = jnp.pad(k, ((0, 0), (WINDOW, 0), (0, 0)))
    vp = jnp.pad(v, ((0, 0), (WINDOW, 0), (0, 0)))
    idx = jnp.arange(nb)[:, None] * qb + jnp.arange(span)[None, :]
    kpos = idx - WINDOW
    qpos = jnp.arange(T).reshape(nb, qb)
    dist = qpos[:, :, None] - kpos[:, None, :]
    mask = (dist >= 0) & (dist < WINDOW) & (kpos[:, None, :] >= 0)
    o, _ = _sdpa(q.reshape(B, nb, qb, H, D), kp[:, idx], vp[:, idx], dist, mask, slopes)
    return o.reshape(B, T, H, v.shape[-1])

def _layer(x, c, past_parts, past_win, pos0, lam_init, w):
    B, T, _ = x.shape
    f32 = jnp.float32
    mod = jnp.einsum('bd,de->be', jax.nn.silu(c), w['w_ada']) + w['b_ada']
    sh1, sc1, ga1, sh2, sc2, ga2 = jnp.split(mod[:, None, :], 6, axis=-1)

    h = _rms(x, w['norm1_g']) * (1.0 + sc1) + sh1
    z = h @ w['w_in']
    q_nsa, kv_new, win_new, nsa_gl, q_dif, merge_l = jnp.split(z, _offsets(IN_SIZES), axis=-1)
    q_pos = pos0 + jnp.arange(T)
    new_parts = jnp.split(kv_new, _offsets(CACHE_SIZES), axis=-1)
    pasts = [None] * len(CACHE_SIZES) if past_parts is None else past_parts
    K = T + (0 if past_parts is None else past_parts[0].shape[1])
    k_pos = jnp.arange(K)

    slopes_a = _alibi(NSA_HEADS)
    knorm = w['nsa_k_norm']
    qn = _rms(q_nsa.reshape(B, T, NSA_HEADS, HEAD_DIM), w['nsa_q_norm'])
    Kp = -(-K // SEL_BLOCK) * SEL_BLOCK
    ck, cv, sk, sv = [_append(p, n, Kp) for p, n in zip(pasts[:4], new_parts[:4])]
    n_cmp, n_sel = Kp // CMP_BLOCK, Kp // SEL_BLOCK
    n_top = min(TOP_N, n_sel)
    kc = jnp.einsum('bnld,l->bnd', ck.reshape(B, n_cmp, CMP_BLOCK, HEAD_DIM) + w['nsa_cmp_pe'], w['nsa_cmp_wk'])
    vc = jnp.einsum('bnld,l->bnd', cv.reshape(B, n_cmp, CMP_BLOCK, HEAD_DIM), w['nsa_cmp_wv'])
    kc = _rms(kc, knorm[0])
    cmp_end = jnp.arange(n_cmp) * CMP_BLOCK + (CMP_BLOCK - 1)
    ks = _rms(sk, knorm[1]).reshape(B, n_sel, SEL_BLOCK, HEAD_DIM)
    vs = sv.reshape(B, n_sel, SEL_BLOCK, HEAD_DIM)
    blk = jnp.arange(n_sel)

    def nsa_block(qp, qb):
        nq = qp.shape[0]
        dist_c = qp[:, None] - cmp_end[None, :]
        o_c, p_c = _sdpa(qb, kc, vc, dist_c, dist_c >= 0, slopes_a)
        imp = p_c.sum(axis=1).reshape(B, nq, n_sel, SEL_BLOCK // CMP_BLOCK).sum(-1)
        forced = (blk[None, :] == (qp // SEL_BLOCK)[:, None]) | (blk[None, :] == 0)
        score = jnp.where(forced, FORCE_SCORE, imp)
        score = jnp.where(blk[None, :] * SEL_BLOCK <= qp[:, None], score, -1.0)
        _, idx = lax.top_k(score, n_top)
        kg = jax.vmap(lambda a, i: a[i])(ks, idx).reshape(B, nq, n_top * SEL_BLOCK, HEAD_DIM)
        vg = jax.vmap(lambda a, i: a[i])(vs, idx).reshape(B, nq, n_top * SEL_BLOCK, HEAD_DIM)
        pos_g = (idx[..., None] * SEL_BLOCK + jnp.arange(SEL_BLOCK)).reshape(B, nq, n_top * SEL_BLOCK)
        dist_s = (qp[None, :, None] - pos_g)[:, :, None, :]
        o_s, _ = _sdpa(qb[:, :, None], kg, vg, dist_s, dist_s >= 0, slopes_a)
        return jnp.stack([o_c, o_s[:, :, 0]], axis=-2)

    o_cs = _map_query_blocks(nsa_block, q_pos, qn)

    w_buf = _w_buf() if past_win is None else past_win.shape[1]
    base = jnp.zeros((B, w_buf, WIN_W), x.dtype) if past_win is None else past_win
    win_all = jnp.concatenate([base, win_new], axis=1)
    win_state = win_all[:, -w_buf:]
    kw, vw = jnp.split(win_all, 2, axis=-1)
    kw = _rms(kw, knorm[2])
    if past_win is None:
        o_w = _window_banded(qn, kw[:, w_buf:], vw[:, w_buf:], slopes_a)
    else:
        wpos = pos0 - w_buf + jnp.arange(w_buf + T)
        dist_w = q_pos[:, None] - wpos[None, :]
        mask_w = (dist_w >= 0) & (dist_w < WINDOW) & (wpos[None, :] >= 0)
        o_w, _ = _sdpa(qn, kw, vw, dist_w, mask_w, slopes_a)
    g = jax.nn.sigmoid(nsa_gl.reshape(B, T, NSA_HEADS, 3, 1))
    o_a = g[..., 0, :] * o_cs[..., 0, :] + g[..., 1, :] * o_cs[..., 1, :] + g[..., 2, :] * o_w
    y_a = o_a.reshape(B, T, NSA_WIDTH) @ w['w_br_nsa']

    slopes_b = _alibi(DIFF_HEADS).reshape(DIFF_KV_HEADS, DIFF_GROUP)
    dk, dv = [_append(p, n, K) for p, n in zip(pasts[4:], new_parts[4:])]
    qd = _rms(q_dif.reshape(B, T, DIFF_KV_HEADS, DIFF_GROUP, 2, HEAD_DIM), w['diff_q_norm'])
    kd = _rms(dk.reshape(B, K, DIFF_KV_HEADS, 2, HEAD_DIM), w['diff_k_norm'])
    vd = dv.reshape(B, K, DIFF_KV_HEADS, DIFF_VDIM)
    lq1, lk1, lq2, lk2 = [w['diff_lambda'][i].astype(f32) for i in range(4)]
    lam = jnp.exp(jnp.sum(lq1 * lk1)) - jnp.exp(jnp.sum(lq2 * lk2)) + lam_init

    def diff_block(qp, qb):
        dist = qp[:, None] - k_pos[None, :]
        s = jnp.einsum('bqngmd,bknmd->bngmqk', qb, kd, preferred_element_type=f32) * (HEAD_DIM ** -0.5)
        s = s - slopes_b[:, :, None, None, None] * dist.astype(f32)
        p = _masked_softmax(s, dist >= 0)
        a = p[:, :, :, 0] - lam * p[:, :, :, 1]
        return jnp.einsum('bngqk,bknv->bqngv', a.astype(vd.dtype), vd)

    o_b = _map_query_blocks(diff_block, q_pos, qd)
    o_b = _rms(o_b, w['diff_subln']) * (1.0 - lam_init)
    y_b = o_b.reshape(B, T, DIFF_WIDTH) @ w['w_br_diff']

    g_a, g_b = jnp.split(jax.nn.sigmoid(merge_l), 2, axis=-1)
    x = x + ga1 * ((g_a * y_a + g_b * y_b) @ w['w_out'])

    h2 = _rms(x, w['norm2_g']) * (1.0 + sc2) + sh2
    u_gate, u_val = jnp.split(h2 @ w['w_ffn_in'], 2, axis=-1)
    x = x + ga2 * ((jax.nn.silu(u_gate) * u_val) @ w['w_ffn_out'])
    return x, kv_new, win_state

def setup_inputs(seed: int = 0) -> dict:
    key = jax.random.key(seed)
    ks = jax.random.split(key, 26)
    f32 = jnp.float32
    n_pages = PAST_LEN // PAGE_SIZE
    n_used = DEC_BATCH * n_pages
    n_phys = n_used + n_used // 4
    w_buf = min(WINDOW, PAST_LEN)
    L = DEPTH

    def nrm(k, shape, scale):
        return scale * jax.random.normal(k, shape, f32)

    def gain(k, shape):
        return 1.0 + 0.05 * jax.random.normal(k, shape, f32)

    page_table = jax.random.permutation(ks[4], n_phys)[:n_used].reshape(DEC_BATCH, n_pages).astype(jnp.int32)
    return {
        'x_prompt': nrm(ks[0], (BATCH, SEQ, D_MODEL), 1.0),
        'x_sample': nrm(ks[1], (DEC_BATCH, DEC_SEQ, D_MODEL), 1.0),
        'cache_kv': nrm(ks[2], (L, n_phys, PAGE_SIZE, CACHE_W), 1.0),
        'state_win_kv': nrm(ks[3], (L, DEC_BATCH, w_buf, WIN_W), 1.0),
        'page_table': page_table,
        'c_prompt': nrm(ks[5], (BATCH, D_MODEL), 1.0),
        'c_sample': nrm(ks[6], (DEC_BATCH, D_MODEL), 1.0),
        'w_ada': nrm(ks[7], (L, D_MODEL, 6 * D_MODEL), 0.5 * D_MODEL ** -0.5),
        'b_ada': nrm(ks[8], (L, 6 * D_MODEL), 0.05),
        'norm1_g': gain(ks[9], (L, D_MODEL)),
        'norm2_g': gain(ks[10], (L, D_MODEL)),
        'w_in': nrm(ks[11], (L, D_MODEL, IN_W), D_MODEL ** -0.5),
        'nsa_q_norm': gain(ks[12], (L, HEAD_DIM)),
        'nsa_k_norm': gain(ks[13], (L, 3, HEAD_DIM)),
        'nsa_cmp_wk': (1.0 + 0.1 * jax.random.normal(ks[14], (L, CMP_BLOCK), f32)) / CMP_BLOCK,
        'nsa_cmp_wv': (1.0 + 0.1 * jax.random.normal(ks[15], (L, CMP_BLOCK), f32)) / CMP_BLOCK,
        'nsa_cmp_pe': nrm(ks[16], (L, CMP_BLOCK, HEAD_DIM), 0.1),
        'diff_q_norm': gain(ks[17], (L, HEAD_DIM)),
        'diff_k_norm': gain(ks[18], (L, HEAD_DIM)),
        'diff_lambda': nrm(ks[19], (L, 4, HEAD_DIM), 0.1),
        'diff_subln': gain(ks[20], (L, DIFF_VDIM)),
        'w_br_nsa': nrm(ks[21], (L, NSA_WIDTH, D_MODEL), NSA_WIDTH ** -0.5),
        'w_br_diff': nrm(ks[22], (L, DIFF_WIDTH, D_MODEL), DIFF_WIDTH ** -0.5),
        'w_out': nrm(ks[23], (L, D_MODEL, D_MODEL), D_MODEL ** -0.5),
        'w_ffn_in': nrm(ks[24], (L, D_MODEL, 2 * D_FF), D_MODEL ** -0.5),
        'w_ffn_out': nrm(ks[25], (L, D_FF, D_MODEL), D_FF ** -0.5),
    }

def reference(x_prompt, x_sample, cache_kv, state_win_kv, page_table, c_prompt, c_sample,
              w_ada, b_ada, norm1_g, norm2_g, w_in, nsa_q_norm, nsa_k_norm, nsa_cmp_wk, nsa_cmp_wv,
              nsa_cmp_pe, diff_q_norm, diff_k_norm, diff_lambda, diff_subln, w_br_nsa, w_br_diff,
              w_out, w_ffn_in, w_ffn_out):
    n_pages = page_table.shape[1]
    past_len = n_pages * PAGE_SIZE
    dec_b = x_sample.shape[0]
    bounds = [0] + _offsets(CACHE_SIZES) + [CACHE_W]
    xp, xs = x_prompt, x_sample
    kv_p, kv_s, win_p, win_s = [], [], [], []
    for l in range(DEPTH):
        w = {
            'w_ada': w_ada[l], 'b_ada': b_ada[l], 'norm1_g': norm1_g[l], 'norm2_g': norm2_g[l],
            'w_in': w_in[l], 'nsa_q_norm': nsa_q_norm[l], 'nsa_k_norm': nsa_k_norm[l],
            'nsa_cmp_wk': nsa_cmp_wk[l], 'nsa_cmp_wv': nsa_cmp_wv[l], 'nsa_cmp_pe': nsa_cmp_pe[l],
            'diff_q_norm': diff_q_norm[l], 'diff_k_norm': diff_k_norm[l], 'diff_lambda': diff_lambda[l],
            'diff_subln': diff_subln[l], 'w_br_nsa': w_br_nsa[l], 'w_br_diff': w_br_diff[l],
            'w_out': w_out[l], 'w_ffn_in': w_ffn_in[l], 'w_ffn_out': w_ffn_out[l],
        }
        lam_init = 0.8 - 0.6 * math.exp(-0.3 * l)
        past_parts = [cache_kv[l, page_table, :, a:b].reshape(dec_b, past_len, b - a)
                      for a, b in zip(bounds[:-1], bounds[1:])]
        xp, kvp, wp = _layer(xp, c_prompt, None, None, 0, lam_init, w)
        xs, kvs, ws = _layer(xs, c_sample, past_parts, state_win_kv[l], past_len, lam_init, w)
        kv_p.append(kvp)
        kv_s.append(kvs)
        win_p.append(wp)
        win_s.append(ws)
    return (xp, xs, jnp.stack(kv_p), jnp.stack(kv_s), jnp.stack(win_p), jnp.stack(win_s))


_drawn_inputs = setup_inputs


def setup_inputs(seed=0):
    import zlib

    import numpy as np

    out = dict(_drawn_inputs(seed))
    spreads = {}
    factors = {'norm2_g': 3.795,
     'nsa_q_norm': 8.0,
     'nsa_k_norm': 8.0,
     'nsa_cmp_wk': 8.0,
     'nsa_cmp_wv': 52.611,
     'nsa_cmp_pe': 8.0,
     'diff_q_norm': 8.0,
     'diff_k_norm': 8.0,
     'diff_lambda': 4.974,
     'diff_subln': 7.887}
    for name, (base, spread) in spreads.items():
        noise = np.random.default_rng([zlib.crc32(name.encode()), seed]).standard_normal(out[name].shape)
        drawn = base * np.exp(spread * noise) if base else spread * noise
        out[name] = jnp.asarray(drawn.astype(out[name].dtype))
    for name, factor in factors.items():
        out[name] = (out[name] * factor).astype(out[name].dtype)
    return out
```

```python
from contextlib import ExitStack

import numpy as np
import concourse.bass as bass
from concourse import mybir

F32 = mybir.dt.float32
F32R = mybir.dt.float32r
I32 = mybir.dt.int32
ALU = mybir.AluOpType
ACT = mybir.ActivationFunctionType
AX = mybir.AxisListType
ds = bass.ds

P = 128
D = 1024
KD = D // P
SEQ = 1024
TT = SEQ // P
NDEC = 8
NTOK = SEQ + NDEC
NC9 = NDEC + 1
HD = 64
NH = 8
NDH = 4
WINDOW = 512
PAST = 1024
PAGE = 128
NPAGE = PAST // PAGE
D_FF = 2816
EPS = 1e-6
NEG = -1e30
LAM_INIT = 0.8 - 0.6 * 1.0

C_QN, C_CK, C_CV, C_SK, C_SV, C_DK, C_DV, C_WK, C_WV, C_G, C_QD, C_M = np.cumsum(
    [0, 512, 64, 64, 64, 64, 256, 256, 64, 64, 24, 512]).tolist()
ZW = C_M
CACHE_W = 768
ZCH = 324
NZCH = ZW // ZCH
MC = 2 * D
TCH = NTOK // 3
assert ZCH * NZCH == ZW and TCH * 3 == NTOK
MODC = 512
NMOD = 6 * D // MODC


class Scope:

    cleared = []

    def __init__(self, nc, tag):
        self.nc, self.tag, self.stack, self.sems = nc, tag, ExitStack(), []

    def __enter__(self):
        return self

    def __exit__(self, *a):
        if self.sems and a[0] is None:
            for x in Scope.cleared:
                self.nc.release_semaphore(x)
            for x in self.sems:
                self.nc.gpsimd.sem_clear(x)
            Scope.cleared = self.sems
        return self.stack.__exit__(*a)

    def sb(self, name, shape, dt=F32, side="left"):
        return self.stack.enter_context(self.nc.sbuf_tensor(f"{self.tag}_{name}", shape, dt, side=side))

    def ps(self, name, shape, dt=F32):
        return self.stack.enter_context(self.nc.psum_tensor(f"{self.tag}_{name}", shape, dt))

    def sem(self, name):
        self.sems.append(self.nc.alloc_semaphore(f"{self.tag}_{name}"))
        return self.sems[-1]

    def pool_sem(self, name):
        return self.nc.alloc_semaphore(f"{self.tag}_{name}")


def f32(ap):
    return ap.bitcast(F32)


def modulation_and_h(nc, io, g):
    with Scope(nc, "mod") as s:
        spare = g.z[:].rearrange("p t c -> p (t c)")
        wr = [spare[:, i * KD * MODC:(i + 1) * KD * MODC].rearrange("p (k n) -> p k n", k=KD) for i in range(3)]
        c9 = s.sb("c9", [NC9, D])
        cT = s.sb("cT", [P, KD, NC9])
        mod = s.sb("mod", [NC9, 6 * D])
        at = 3 * KD * MODC + D
        modc = [spare[0:NC9, at + i * MODC:at + (i + 1) * MODC] for i in range(3)]
        x = s.sb("x", [P, TT, D])
        xs = s.sb("xs", [NDEC, D])
        junk = spare[:, 3 * KD * MODC:3 * KD * MODC + D]
        ssq = s.sb("ssq", [P, TT + 1])
        rstd = s.sb("rstd", [P, TT + 1])
        gains = s.sb("gains", [16, P])
        hf = [s.sb(f"hf{i}", [P, 512]) for i in range(2)]
        aT = s.sb("aT", [P, KD, NC9])
        hs = s.sb("hs", [P, KD, NDEC])
        pc = s.ps("pc", [P, KD, NC9])
        pm = [s.ps(f"pm{i}", [NC9, MODC]) for i in range(3)]
        pt = [s.ps(f"pt{i}", [P, 512]) for i in range(3)]
        c_in, w_in, x_in, xs_in = s.sem("c_in"), [s.sem(f"w_in{i}") for i in range(3)], [s.pool_sem(f"x_in{t}") for t in range(TT)], s.pool_sem("xs_in")
        w_free, silu_done, cT_ps, cT_done = s.sem("w_free"), s.sem("silu"), s.sem("cT_ps"), s.sem("cT_done")
        mod_ps, mod_sb, modT_ps, modT_sb, mod_all = (s.sem(n) for n in ("mod_ps", "mod_sb", "modT_ps", "modT_sb", "mod_all"))
        mod_out = s.pool_sem("mod_out")
        sq_done, std_done, rstd_done, xn_done = (s.sem(n) for n in ("sq", "std", "rstd", "xn"))
        coef, h_ps, h_sb, h_split, hs_ps, hs_st, g_ps = (s.sem(n) for n in ("coef", "h_ps", "h_sb", "h_split", "hs_ps", "hs_st", "g_ps"))
        ss0 = s.sem("ssq0")
        w_ada = io["w_ada"][0].rearrange("(k p) n -> p k n", p=P)
        x_v = io["x_prompt"][0].rearrange("(t p) d -> p t d", p=P)
        with nc.Block() as block:

            @block.sync
            def _(sp):
                sp.dma_start(c9[0:NDEC, :], io["c_sample"]).then_inc(c_in, 16)
                sp.dma_start(c9[NDEC:NC9, :], io["c_prompt"]).then_inc(c_in, 16)
                sp.dma_start(mod[:], io["b_ada"].broadcast_to([NC9, 6 * D])).then_inc(c_in, 16)
                sp.dma_start(gains[0:8, :], io["norm1_g"][0].rearrange("(k p) -> k p", p=P)).then_inc(c_in, 16)
                sp.dma_start(gains[8:16, :], io["norm2_g"][0].rearrange("(k p) -> k p", p=P)).then_inc(c_in, 16)
                with sp.Fori(0, NMOD // 3) as i:
                    for j in range(3):
                        sp.wait_ge(w_free, i * 3 + j + 1)
                        sp.dma_start(wr[j], w_ada[:, :, ds((i * 3 + j) * MODC, MODC)]).then_inc(w_in[j], 16)

            @block.gpsimd
            def _(pool):
                pool.dma_start(xs[:], io["x_sample"].rearrange("b t d -> (b t) d")).then_inc(xs_in, 16)
                for t in range(TT):
                    pool.dma_start(x[:, t, :], x_v[:, t, :]).then_inc(x_in[t], 16)
                pool.wait_ge(mod_all, NMOD)
                pool.dma_start(io["mod_d"][:], mod[:]).then_inc(mod_out, 16)
                pool.wait_ge(mod_out, 16)

            @block.scalar
            def _(act):
                act.wait_ge(c_in, 80)
                act.activation(c9[:], c9[:], ACT.Silu).then_inc(silu_done, 1)
                act.wait_ge(ss0, 1)
                act.wait_ge(xs_in, 16)
                act.activation(junk[0:NDEC, :], xs[:], ACT.Square, accum_out=ssq[0:NDEC, TT:TT + 1]).then_inc(sq_done, 1)
                for t in range(TT):
                    act.wait_ge(x_in[t], 16)
                    act.wait_ge(sq_done, t + 1)
                    act.activation(junk, x[:, t, :], ACT.Square, accum_out=ssq[:, t:t + 1]).then_inc(sq_done, 1)
                act.wait_ge(rstd_done, 1)
                act.activation(rstd[:], rstd[:], ACT.Sqrt).then_inc(std_done, 1)
                for n in range(2 * KD):
                    k = n // 2
                    act.wait_ge(h_ps, n + 1)
                    act.wait_ge(coef, 1)
                    if n >= 2:
                        act.wait_ge(h_split, n - 1)
                    act.activation(hf[n % 2][:], pt[n % 3][:], ACT.Identity, bias=g.modT[:, k, NDEC:NC9],
                                   scale=aT[:, k, NDEC:NC9]).then_inc(h_sb, 1)

            @block.tensor
            def _(pe):
                pe.wait_ge(g.const_ready, 2)
                pe.wait_ge(silu_done, 1)
                for k in range(KD):
                    mm = pe.transpose(pc[:, k, :], c9[:, k * P:(k + 1) * P], g.ident[0:NC9, 0:NC9])
                mm.then_inc(cT_ps, 1)
                pe.transpose(pt[0][:, 0:16], gains[:], g.ident[0:16, 0:16]).then_inc(g_ps, 1)
                pe.wait_ge(cT_done, 2)
                pe.sem_inc(w_free, 3)
                with pe.Fori(0, NMOD // 3) as i:
                    for j in range(3):
                        pe.wait_ge(w_in[j], i * 16 + 16)
                        for k in range(KD):
                            mm = pe.matmul(pm[j][:], cT[:, k, :], wr[j][:, k, :], start=(k == 0), stop=(k == KD - 1))
                        mm.then_inc(mod_ps, 1)
                        pe.wait_ge(mod_sb, i * 3 + j + 1)
                        pe.sem_inc(w_free, 1)
                        for q in range(4):
                            mm = pe.transpose(pt[j][:, q * NC9:(q + 1) * NC9], modc[j][:, q * P:(q + 1) * P],
                                              g.ident[0:NC9, 0:NC9])
                        mm.then_inc(modT_ps, 1)
                pe.wait_ge(xn_done, TT + 1)
                pe.wait_ge(modT_sb, NMOD)
                for n in range(2 * KD):
                    k, half = n // 2, n % 2
                    if n >= 3:
                        pe.wait_ge(h_sb, n - 2)
                    for q in range(4):
                        mm = pe.transpose(pt[n % 3][:, q * P:(q + 1) * P], x[:, half * 4 + q, k * P:(k + 1) * P], g.ident[:])
                    mm.then_inc(h_ps, 1)
                for k in range(KD):
                    mm = pe.transpose(pc[:, k, 0:NDEC], xs[:, k * P:(k + 1) * P], g.ident[0:NDEC, 0:NDEC])
                mm.then_inc(hs_ps, 1)

            @block.vector
            def _(dve):
                dve.memset(ssq[:], 0.0).then_inc(ss0, 1)
                dve.wait_ge(cT_ps, 1)
                dve.tensor_copy(cT[:], pc[:]).then_inc(cT_done, 1)
                dve.wait_ge(g_ps, 1)
                dve.tensor_copy(g.gT[:], pt[0][:, 0:16]).then_inc(cT_done, 1)
                dve.wait_ge(c_in, 80)
                with dve.Fori(0, NMOD // 3) as i:
                    for j in range(3):
                        dve.wait_ge(mod_ps, i * 3 + j + 1)
                        part = mod[:, ds((i * 3 + j) * MODC, MODC)]
                        dve.tensor_tensor(modc[j], pm[j][:], part, ALU.add).then_inc(mod_sb, 1)
                        dve.wait_ge(mod_sb, i * 3 + j + 1)
                        dve.tensor_scalar(part, modc[j], 1.0, None, ALU.mult).then_inc(mod_all, 1)
                        dve.wait_ge(modT_ps, i * 3 + j + 1)
                        dve.tensor_scalar(g.modT[:, ds((i * 3 + j) * 4, 4), :], pt[j][:, 0:4 * NC9].rearrange("p (a b) -> p a b", a=4),
                                          1.0, None, ALU.mult).then_inc(modT_sb, 1)
                dve.wait_ge(sq_done, TT + 1)
                dve.tensor_scalar(rstd[:], ssq[:], 1.0 / D, EPS, ALU.mult, ALU.add).then_inc(rstd_done, 1)
                dve.wait_ge(std_done, 1)
                dve.reciprocal(rstd[:], rstd[:]).then_inc(rstd_done, 1)
                dve.wait_ge(rstd_done, 2)
                dve.tensor_scalar(xs[:], xs[:], rstd[0:NDEC, TT:TT + 1], None, ALU.mult).then_inc(xn_done, 1)
                for t in range(TT):
                    dve.tensor_scalar(x[:, t, :], x[:, t, :], rstd[:, t:t + 1], None, ALU.mult).then_inc(xn_done, 1)
                dve.wait_ge(modT_sb, NMOD)
                dve.scalar_tensor_tensor(out=aT[:], in0=g.modT[:, KD:2 * KD, :], scalar=1.0,
                                         in1=g.gT[:, 0:KD].unsqueeze(2).broadcast_to([P, KD, NC9]), op0=ALU.add, op1=ALU.mult).then_inc(coef, 1)
                for n in range(2 * KD):
                    k, half = n // 2, n % 2
                    dve.wait_ge(h_sb, n + 1)
                    hi = g.hT_hi[:, k, half * 512:(half + 1) * 512]
                    lo = g.hT_lo[:, k, half * 512:(half + 1) * 512]
                    dve.tensor_copy(hi, hf[n % 2][:]).then_inc(hs_st, 1)
                    dve.wait_ge(hs_st, n + 1)
                    dve.tensor_tensor(lo, hf[n % 2][:], f32(hi), ALU.subtract).then_inc(h_split, 1)
                dve.wait_ge(hs_ps, 1)
                dve.wait_ge(coef, 1)
                dve.tensor_tensor(hs[:], pc[:, :, 0:NDEC], aT[:, :, 0:NDEC], ALU.mult).then_inc(coef, 1)
                dve.wait_ge(coef, 2)
                dve.tensor_tensor(hs[:], hs[:], g.modT[:, 0:KD, 0:NDEC], ALU.add).then_inc(coef, 1)
                dve.wait_ge(coef, 3)
                dve.tensor_copy(g.hT_hi[:, :, SEQ:NTOK], hs[:]).then_inc(coef, 1)
                dve.wait_ge(coef, 4)
                dve.tensor_tensor(g.hT_lo[:, :, SEQ:NTOK], hs[:], f32(g.hT_hi[:, :, SEQ:NTOK]), ALU.subtract).then_inc(coef, 1)


def project_token_major(nc, io, g):
    with Scope(nc, "z") as s:
        raw = [s.sb(f"raw{i}", [P, KD, ZCH]) for i in range(2)]
        whi = [s.sb(f"whi{i}", [P, KD, ZCH], F32R) for i in range(2)]
        wlo = [s.sb(f"wlo{i}", [P, KD, ZCH], F32R) for i in range(2)]
        acc = [s.ps(f"acc{i}", [P, 512]) for i in range(6)]
        w_in = [s.sem(f"w_in{i}") for i in range(2)]
        raw_free, w_hi, w_lo, w_free = s.sem("raw_free"), s.sem("w_hi"), s.sem("w_lo"), s.sem("w_free")
        acc_full, acc_free = s.sem("acc_full"), s.sem("acc_free")
        w = io["w_in"][0].rearrange("(k p) n -> p k n", p=P)
        NU = TT + 1
        with nc.Block() as block:

            @block.sync
            def _(sp):
                with sp.Fori(0, NZCH // 2) as i:
                    for j in range(2):
                        sp.wait_ge(raw_free, i * 2 + j + 1)
                        sp.dma_start(raw[j][:], w[:, :, ds((i * 2 + j) * ZCH, ZCH)]).then_inc(w_in[j], 16)

            @block.scalar
            def _(act):
                act.sem_inc(acc_free, 6)
                with act.Fori(0, NZCH // 2) as i:
                    for j in range(2):
                        for t in range(NU):
                            u = j * NU + t
                            rows = P if t < TT else NDEC
                            act.wait_ge(acc_full, i * 2 * NU + u + 1)
                            act.activation(g.z[0:rows, t, ds((i * 2 + j) * ZCH, ZCH)], acc[u % 6][0:rows, 0:ZCH],
                                           ACT.Copy).then_inc(acc_free, 1)

            @block.vector
            def _(dve):
                dve.sem_inc(raw_free, 2)
                with dve.Fori(0, NZCH // 2) as i:
                    for j in range(2):
                        dve.wait_ge(w_in[j], i * 16 + 16)
                        dve.wait_ge(w_free, i * 2 + j + 1)
                        dve.tensor_copy(whi[j][:], raw[j][:]).then_inc(w_hi, 1)
                        dve.wait_ge(w_hi, i * 2 + j + 1)
                        dve.tensor_tensor(wlo[j][:], raw[j][:], f32(whi[j][:]), ALU.subtract).then_inc(w_lo, 1)
                        dve.wait_ge(w_lo, i * 2 + j + 1)
                        dve.sem_inc(raw_free, 1)

            @block.tensor
            def _(pe):
                pe.sem_inc(w_free, 2)
                with pe.Fori(0, NZCH // 2) as i:
                    for j in range(2):
                        pe.wait_ge(w_lo, i * 2 + j + 1)
                        for t in range(NU):
                            u = j * NU + t
                            pe.wait_ge(acc_free, i * 2 * NU + u + 1)
                            rows = P if t < TT else NDEC
                            tok = slice(t * P, t * P + rows)
                            for k in range(KD):
                                for n, (a, b) in enumerate(((g.hT_hi, whi), (g.hT_lo, whi), (g.hT_hi, wlo))):
                                    mm = pe.matmul(acc[u % 6][0:rows, 0:ZCH], a[:, k, tok], b[j][:, k, :],
                                                   start=(k == 0 and n == 0), stop=(k == KD - 1 and n == 2))
                            mm.then_inc(acc_full, 1)
                        pe.wait_ge(acc_full, i * 2 * NU + (j + 1) * NU)
                        pe.sem_inc(w_free, 1)


def merge_gates(nc, io, g):
    MCH = 2 * P
    NMCH = MC // MCH
    with Scope(nc, "mg") as s:
        raw = [s.sb(f"raw{i}", [P, KD, MCH]) for i in range(2)]
        whi = [s.sb(f"whi{i}", [P, KD, MCH], F32R) for i in range(2)]
        wlo = [s.sb(f"wlo{i}", [P, KD, MCH], F32R) for i in range(2)]
        gate = [s.sb(f"gate{i}", [P, NTOK]) for i in range(2)]
        acc = [s.ps(f"acc{i}", [P, 512]) for i in range(6)]
        w_in = [s.sem(f"w_in{i}") for i in range(2)]
        raw_free, w_hi, w_lo, w_free = s.sem("raw_free"), s.sem("w_hi"), s.sem("w_lo"), s.sem("w_free")
        acc_full, acc_free, gate_ready = s.sem("acc_full"), s.sem("acc_free"), s.sem("gate_ready")
        gate_free = s.sem("gate_free")
        gate_out = [s.pool_sem(f"gate_out{i}") for i in range(2)]
        w = io["w_in"][0].rearrange("(k p) n -> p k n", p=P)
        with nc.Block() as block:

            @block.sync
            def _(sp):
                with sp.Fori(0, NMCH // 2) as i:
                    for j in range(2):
                        sp.wait_ge(raw_free, i * 2 + j + 1)
                        sp.dma_start(raw[j][:], w[:, :, ds((i * 2 + j) * MCH + C_M, MCH)]).then_inc(w_in[j], 16)

            @block.gpsimd
            def _(pool):
                with pool.Fori(0, NMCH) as i:
                    for f in range(2):
                        pool.wait_ge(gate_ready, i * 6 + f * 3 + 3)
                        pool.dma_start(io["gate_d"][ds((i * 2 + f) * P, P), :], gate[f][:]).then_inc(gate_out[f], 16)
                        pool.wait_ge(gate_out[f], i * 16 + 16)
                        pool.sem_inc(gate_free, 1)

            @block.scalar
            def _(act):
                act.sem_inc(gate_free, 2)
                act.sem_inc(acc_free, 6)
                with act.Fori(0, NMCH // 2) as i:
                    for j in range(2):
                        for f in range(2):
                            act.wait_ge(gate_free, i * 4 + j * 2 + f + 1)
                            for c in range(3):
                                act.wait_ge(acc_full, i * 12 + j * 6 + f * 3 + c + 1)
                                act.activation(gate[f][:, c * TCH:(c + 1) * TCH], acc[f * 3 + c][:, 0:TCH],
                                               ACT.Sigmoid).then_inc(gate_ready, 1)
                            act.wait_ge(gate_ready, i * 12 + j * 6 + f * 3 + 3)
                            act.sem_inc(acc_free, 3)

            @block.vector
            def _(dve):
                dve.sem_inc(raw_free, 2)
                with dve.Fori(0, NMCH // 2) as i:
                    for j in range(2):
                        dve.wait_ge(w_in[j], i * 16 + 16)
                        dve.wait_ge(w_free, i * 2 + j + 1)
                        dve.tensor_copy(whi[j][:], raw[j][:]).then_inc(w_hi, 1)
                        dve.wait_ge(w_hi, i * 2 + j + 1)
                        dve.tensor_tensor(wlo[j][:], raw[j][:], f32(whi[j][:]), ALU.subtract).then_inc(w_lo, 1)
                        dve.wait_ge(w_lo, i * 2 + j + 1)
                        dve.sem_inc(raw_free, 1)

            @block.tensor
            def _(pe):
                pe.sem_inc(w_free, 2)
                with pe.Fori(0, NMCH // 2) as i:
                    for j in range(2):
                        pe.wait_ge(w_lo, i * 2 + j + 1)
                        for f in range(2):
                            cols = slice(f * P, (f + 1) * P)
                            for c in range(3):
                                tok = slice(c * TCH, (c + 1) * TCH)
                                pe.wait_ge(acc_free, i * 12 + j * 6 + f * 3 + c + 1)
                                for k in range(KD):
                                    for n, (a, b) in enumerate(((whi, g.hT_hi), (wlo, g.hT_hi), (whi, g.hT_lo))):
                                        mm = pe.matmul(acc[f * 3 + c][:, 0:TCH], a[j][:, k, cols], b[:, k, tok],
                                                       start=(k == 0 and n == 0), stop=(k == KD - 1 and n == 2))
                                mm.then_inc(acc_full, 1)
                        pe.wait_ge(acc_full, i * 12 + j * 6 + 6)
                        pe.sem_inc(w_free, 1)


def store_new_rows(nc, io, g):
    with Scope(nc, "rows") as s:
        out = s.sem("out")
        kv = io["kv_p"][0, 0].rearrange("(t p) c -> p t c", p=P)
        win = io["win_p"][0, 0].rearrange("(t p) c -> p t c", p=P)
        with nc.Block() as block:

            @block.sync
            def _(sp):
                sp.dma_start(kv, g.z[:, 0:TT, C_CK:C_WK]).then_inc(out, 16)
                sp.dma_start(win, g.z[:, TT - WINDOW // P:TT, C_WK:C_G]).then_inc(out, 16)
                sp.dma_start(io["kv_s"][0, :, 0, :], g.z[0:NDEC, TT, C_CK:C_WK]).then_inc(out, 16)
                sp.dma_start(io["win_s"][0, :, WINDOW - 1, :], g.z[0:NDEC, TT, C_WK:C_G]).then_inc(out, 16)
                sp.dma_start(io["win_s"][0, :, 0:WINDOW - 1, :], io["state_win_kv"][0, :, 1:WINDOW, :]).then_inc(out, 16)
                sp.wait_ge(out, 80)


NORMS = [(C_QN, NH, 0), (C_SK, 1, 8), (C_DK, 4, 9), (C_WK, 1, 13), (C_QD, 8, 14)]
NG = 22
KEYS = [(C_SK, 8, 1), (C_WK, 13, 2)] + [(C_DK + HD * i, 9 + i, 3) for i in range(4)]


def attention_tiles(g, s):
    g.gain = s.sb("gain", [P, 6, HD])
    g.subln = s.sb("subln", [P, 2 * HD])
    g.neglam = s.sb("neglam", [P, 1])
    g.wcmp = s.sb("wcmp", [P, 2, 60])
    g.pe4 = s.sb("pe4", [P, HD])
    g.G = s.sb("G", [P, TT + 1, 24])


def constants(nc, io, g, a):
    g.tsel = a.sb("tsel", [P, SEQ])
    g.twin = a.sb("twin", [P, WINDOW + P])
    g.tcmp = a.sb("tcmp", [P, TT * 32])
    g.seen = a.sb("seen", [P, TT * 32])
    lamb = a.sb("lamb", [P, 4, HD])
    lprod = a.sb("lprod", [P, 2, HD])
    lsum = a.sb("lsum", [P, 2])
    wcol = a.sb("wcol", [P, 2])
    iot = a.sb("iot", [P, SEQ], I32)
    loads, iota, tabs, lam, done = a.sem("k_loads"), a.sem("k_iota"), a.sem("k_tabs"), a.sem("k_lam"), a.sem("k_done")
    lexp = a.sem("k_lexp")
    with nc.Block() as block:

        @block.sync
        def _(sp):
            gains = [io["nsa_q_norm"][0:1, :]] + [io["nsa_k_norm"][0, i:i + 1, :] for i in range(3)] + \
                [io["diff_k_norm"][0:1, :], io["diff_q_norm"][0:1, :]]
            for i, a in enumerate(gains):
                sp.dma_start(g.gain[:, i, :], a.broadcast_to([P, HD])).then_inc(loads, 16)
            sp.dma_start(g.subln[:], io["diff_subln"][0:1, :].broadcast_to([P, 2 * HD])).then_inc(loads, 16)
            sp.dma_start(lamb[:].rearrange("p a b -> p (a b)"),
                         io["diff_lambda"].rearrange("l a b -> l (a b)").broadcast_to([P, 4 * HD])).then_inc(loads, 16)
            for q in range(4):
                rows = slice(32 * q, 32 * q + 32)
                sp.dma_start(g.pe4[rows, :], io["nsa_cmp_pe"][0]).then_inc(loads, 16)
                sp.dma_start(wcol[rows, 0:1], io["nsa_cmp_wk"].rearrange("l c -> c l")).then_inc(loads, 16)
                sp.dma_start(wcol[rows, 1:2], io["nsa_cmp_wv"].rearrange("l c -> c l")).then_inc(loads, 16)

        @block.gpsimd
        def _(pool):
            n = 0

            def table(out, width, pattern, base):
                nonlocal n
                pool.iota(iot[:, 0:width], pattern=pattern, base=base, channel_multiplier=-1).then_inc(iota, 1)
                pool.wait_ge(iota, n + 1)
                pool.tensor_copy(out, iot[:, 0:width]).then_inc(tabs, 1)
                n += 1
                pool.wait_ge(tabs, n)

            def keep(t, fill, pattern, base, mult, count):
                pool.affine_select(out=t, in_=t, compare_op=ALU.is_ge, fill=fill, base=base, pattern=pattern,
                                   channel_multiplier=mult).then_inc(done, 1)
                pool.wait_ge(done, count)

            table(g.tsel[:], SEQ, [[1, SEQ]], P - SEQ)
            keep(g.tsel[:], NEG, [[-1, SEQ]], SEQ - P, 1, 1)
            table(g.twin[:], WINDOW + P, [[1, WINDOW + P]], -WINDOW)
            keep(g.twin[:], NEG, [[-1, WINDOW + P]], WINDOW, 1, 2)
            keep(g.twin[:], NEG, [[1, WINDOW + P]], -1, -1, 3)
            table(g.tcmp[:], TT * 32, [[-P, TT], [32, 32]], 31)
            keep(g.tcmp[:].rearrange("p (t n) -> p t n", t=TT), NEG, [[P, TT], [-32, 32]], -31, 1, 4)
            pool.memset(g.seen[:], 1.0).then_inc(done, 1)
            pool.wait_ge(done, 5)
            keep(g.seen[:].rearrange("p (t n) -> p t n", t=TT), 0.0, [[P, TT], [-32, 32]], -31, 1, 6)
            pool.memset(g.wcmp[:], 0.0).then_inc(done, 1)
            pool.wait_ge(done, 7)
            pool.wait_ge(loads, 20 * 16)
            for v in range(2):
                w4 = g.wcmp[:, v, 28:32]
                pool.tensor_copy(w4, wcol[:, v:v + 1].broadcast_to([P, 4])).then_inc(done, 1)
                pool.wait_ge(done, 8 + 3 * v)
                keep(w4, 0.0, [[-32, 4]], 0, 1, 9 + 3 * v)
                keep(w4, 0.0, [[32, 4]], 31, -1, 10 + 3 * v)

        @block.vector
        def _(dve):
            dve.wait_ge(loads, 20 * 16)
            for n, i in enumerate((0, 5)):
                dve.tensor_scalar(g.gain[:, i, :], g.gain[:, i, :], HD ** -0.5, None, ALU.mult).then_inc(lam, 1)
            lv = lamb[:].rearrange("p (a b) d -> p a b d", b=2)
            dve.tensor_tensor(lprod[:], lv[:, :, 0, :], lv[:, :, 1, :], ALU.mult).then_inc(lam, 1)
            dve.wait_ge(lam, 3)
            dve.tensor_reduce(lsum[:], lprod[:], AX.X, ALU.add).then_inc(lam, 1)
            dve.tensor_scalar(g.subln[:], g.subln[:], 1.0 - LAM_INIT, None, ALU.mult).then_inc(lam, 1)
            dve.wait_ge(lexp, 1)
            dve.tensor_tensor(g.neglam[:], lsum[:, 1:2], lsum[:, 0:1], ALU.subtract).then_inc(lam, 1)
            dve.wait_ge(lam, 6)
            dve.tensor_scalar(g.neglam[:], g.neglam[:], -LAM_INIT, None, ALU.add).then_inc(lam, 1)

        @block.scalar
        def _(act):
            act.wait_ge(lam, 4)
            act.activation(lsum[:], lsum[:], ACT.Exp).then_inc(lexp, 1)


def prepare_keys(nc, io, g, a):
    g.kkd = a.sb("kkd", [P, 4 * SEQ], F32R)
    g.kk = [a.sb(f"kk{i}", [P, SEQ], F32R) for i in range(2)]
    g.kk += [g.kkd[:, i * SEQ:(i + 1) * SEQ] for i in range(4)]
    g.kkc = a.sb("kkc", [P, 32], F32R)
    g.vcb = a.sb("vcb", [P, 4, HD])
    with Scope(nc, "keys") as s:
        sq = [s.sb(f"sq{i}", [P, NG, HD]) for i in range(2)]
        rs = s.sb("rs", [P, TT + 1, NG])
        knorm = s.sb("knorm", [P, TT, HD])
        kdup = [s.sb(f"kdup{i}", [P, TT, 2, HD]) for i in range(2)]
        ckp = s.sb("ckp", [P, TT, HD])
        kc = s.sb("kc", [32, HD])
        kcsq = s.sb("kcsq", [32, HD])
        kcs = s.sb("kcs", [32, 1])
        kcd = s.sb("kcd", [32, 2, HD])
        pk = [s.ps(f"pk{i}", [P, SEQ]) for i in range(2)]
        pcmp = s.ps("pcmp", [32, 2, HD])
        pkc = s.ps("pkc", [P, 32])
        sqd, ssd, rsd, qs, qp = s.sem("sqd"), s.sem("ssd"), s.sem("rsd"), s.sem("qs"), s.sem("qp")
        rstd, kn, kd, kt, khi, klo, cp, cs, gat = (s.sem(n) for n in ("rstd", "kn", "kd", "kt", "khi", "klo", "cp", "cs", "gat"))
        rows = lambda t: P if t < TT else NDEC
        with nc.Block() as block:

            @block.scalar
            def _(act):
                for t in range(TT + 1):
                    r = rows(t)
                    if t >= 2:
                        act.wait_ge(ssd, t - 1)
                    for c, n, o in NORMS:
                        act.activation(sq[t % 2][0:r, o:o + n, :].rearrange("p a b -> p (a b)"),
                                       g.z[0:r, t, c:c + n * HD], ACT.Square).then_inc(sqd, 1)
                act.wait_ge(rsd, 1)
                act.activation(rs[:], rs[:], ACT.Sqrt).then_inc(rstd, 1)
                act.wait_ge(cs, 3)
                act.activation(kcsq[:], kc[:], ACT.Square, accum_out=kcs[:]).then_inc(gat, 1)
                act.wait_ge(cs, 4)
                act.activation(kcs[:], kcs[:], ACT.Sqrt).then_inc(gat, 1)
                for i in range(6):
                    act.wait_ge(kt, i + 1)
                    act.activation(g.kk[i][:], pk[i % 2][:], ACT.Copy).then_inc(khi, 1)
                act.activation(g.G[:, 0:TT, :], g.z[:, 0:TT, C_G:C_QD], ACT.Sigmoid).then_inc(gat, 1)
                act.activation(g.G[0:NDEC, TT, :], g.z[0:NDEC, TT, C_G:C_QD], ACT.Sigmoid).then_inc(gat, 1)

            @block.tensor
            def _(pe):
                pe.wait_ge(cp, 1)
                for v in range(2):
                    for t in range(TT):
                        rhs = ckp[:, t, :] if v == 0 else g.z[:, t, C_CV:C_SK]
                        mm = pe.matmul(pcmp[:, v, :], g.wcmp[:, v, 28 - 4 * t:60 - 4 * t], rhs,
                                       start=(t == 0), stop=(t == TT - 1))
                    mm.then_inc(cs, 1)
                for i in range(6):
                    pe.wait_ge(kd, i + 1)
                    if i >= 2:
                        pe.wait_ge(klo, i - 1)
                    for t in range(TT):
                        mm = pe.transpose(pk[i % 2][:, t * P:(t + 1) * P], kdup[i % 2][:, t].rearrange("p a b -> p (a b)"), g.ident[:])
                    mm.then_inc(kt, 1)
                pe.wait_ge(kd, 7)
                pe.transpose(pkc[:], kcd[:].rearrange("p a b -> p (a b)"), g.ident[0:32, 0:32]).then_inc(kt, 1)

            @block.gpsimd
            def _(pool):
                pool.wait_ge(rstd, 2)
                for t in range(TT + 1):
                    r = rows(t)
                    q = g.z[0:r, t, C_QD:C_M].rearrange("p (a b) -> p a b", b=HD)
                    pool.tensor_tensor(q, q, rs[0:r, t, 14:22].unsqueeze(2).broadcast_to([r, 8, HD]), ALU.mult).then_inc(qp, 1)
                    pool.wait_ge(qp, 2 * t + 1)
                    pool.tensor_tensor(q, q, g.gain[0:r, 5:6, :].broadcast_to([r, 8, HD]), ALU.mult).then_inc(qp, 1)

            def low(dve, i):
                dve.wait_ge(khi, i + 1)
                dve.tensor_tensor(g.kk[i][HD:P, :], pk[i % 2][HD:P, :], f32(g.kk[i][HD:P, :]), ALU.subtract).then_inc(klo, 1)

            @block.vector
            def _(dve):
                dve.tensor_tensor(ckp[:], g.z[:, 0:TT, C_CK:C_CV], g.pe4[:].unsqueeze(1).broadcast_to([P, TT, HD]), ALU.add).then_inc(cp, 1)
                dve.memset(rs[:], 1.0).then_inc(qs, 1)
                dve.memset(g.vcb[:], 0.0).then_inc(qs, 1)
                dve.wait_ge(qs, 2)
                for t in range(TT + 1):
                    r = rows(t)
                    dve.wait_ge(sqd, 5 * (t + 1))
                    dve.tensor_reduce(rs[0:r, t, :], sq[t % 2][0:r], AX.X, ALU.add).then_inc(ssd, 1)
                dve.wait_ge(ssd, TT + 1)
                dve.tensor_scalar(rs[:], rs[:], 1.0 / HD, EPS, ALU.mult, ALU.add).then_inc(rsd, 1)
                dve.wait_ge(rstd, 1)
                dve.reciprocal(rs[:], rs[:]).then_inc(rstd, 1)
                dve.wait_ge(rstd, 2)
                dve.wait_ge(cs, 2)
                for h in range(4):
                    dve.tensor_copy(g.vcb[32 * h:32 * h + 32, h, :], pcmp[:, 1, :]).then_inc(qs, 1)
                dve.tensor_copy(kc[:], pcmp[:, 0, :]).then_inc(cs, 1)
                dve.wait_ge(gat, 1)
                dve.tensor_scalar(kcs[:], kcs[:], 1.0 / HD, EPS, ALU.mult, ALU.add).then_inc(cs, 1)
                for i, (c, slot, gain) in enumerate(KEYS):
                    if i >= 1:
                        dve.wait_ge(kd, i)
                    dve.tensor_tensor(knorm[:], g.z[:, 0:TT, c:c + HD],
                                      rs[:, 0:TT, slot:slot + 1].broadcast_to([P, TT, HD]), ALU.mult).then_inc(kn, 1)
                    dve.wait_ge(kn, i + 1)
                    if i >= 2:
                        dve.wait_ge(kt, i - 1)
                    gk = g.gain[:, gain + 1, :]
                    dve.tensor_tensor(kdup[i % 2][:], knorm[:].unsqueeze(2).broadcast_to([P, TT, 2, HD]),
                                      gk.unsqueeze(1).unsqueeze(1).broadcast_to([P, TT, 2, HD]), ALU.mult).then_inc(kd, 1)
                    if i >= 1:
                        low(dve, i - 1)
                low(dve, 5)
                for t in range(TT + 1):
                    r = rows(t)
                    q = g.z[0:r, t, C_QN:C_CK].rearrange("p (a b) -> p a b", b=HD)
                    dve.tensor_tensor(q, q, rs[0:r, t, 0:8].unsqueeze(2).broadcast_to([r, 8, HD]), ALU.mult).then_inc(qs, 1)
                    dve.wait_ge(qs, 7 + 2 * t)
                    dve.tensor_tensor(q, q, g.gain[0:r, 0:1, :].broadcast_to([r, 8, HD]), ALU.mult).then_inc(qs, 1)
                dve.wait_ge(gat, 2)
                dve.reciprocal(kcs[:], kcs[:]).then_inc(cs, 1)
                dve.wait_ge(cs, 5)
                dve.tensor_scalar(kc[:], kc[:], kcs[:, 0:1], None, ALU.mult).then_inc(cs, 1)
                dve.wait_ge(cs, 6)
                dve.tensor_tensor(kcd[:], kc[:].unsqueeze(1).broadcast_to([32, 2, HD]),
                                  g.gain[0:32, 1:2, :].broadcast_to([32, 2, HD]), ALU.mult).then_inc(kd, 1)
                dve.wait_ge(kt, 7)
                dve.tensor_copy(g.kkc[:], pkc[:]).then_inc(cs, 1)
                dve.wait_ge(cs, 7)
                dve.tensor_tensor(g.kkc[HD:P, :], pkc[HD:P, :], f32(g.kkc[HD:P, :]), ALU.subtract).then_inc(cs, 1)


def key_chunks(n):
    return [(c, min(n, c + 512)) for c in range(0, n, 512)]


def nsa_attention(nc, io, g):
    NU = 2 * TT
    units = [(i, 0, 0, (i + 1) * P) if b == 0 else (i, 1, max(0, i - 4) * P, (i + 1) * P)
             for i in range(TT) for b in range(2)]
    groups = [(k1 - k0 + 511) // 512 for _, _, k0, k1 in units]
    second = np.cumsum([0] + [n - 1 for n in groups]).tolist()
    VCOL = (C_SV, C_WV)
    with Scope(nc, "nsa") as s:
        qd = s.sb("qd", [P, TT, 2, HD])
        qhi = s.sb("qhi", [P, SEQ], F32R)
        qlo = s.sb("qlo", [P, SEQ], F32R)
        prob = [s.sb(f"prob{i}", [P, SEQ]) for i in range(4)]
        probT = [s.sb(f"probT{i}", [P, TT, P]) for i in range(2)]
        nmax = s.sb("nmax", [P, NU])
        total = s.sb("total", [P, NU])
        share = s.sb("share", [P, 2, 2])
        scmp = s.sb("scmp", [P, TT, NH, 32])
        cm = s.sb("cm", [P, NH * TT])
        cs = s.sb("cs", [P, NH * TT])
        pcT = [s.sb(f"pcT{i}", [P, P]) for i in range(2)]
        sc = [s.ps(f"sc{i}", [P, SEQ]) for i in range(2)]
        tp = [s.ps(f"tp{i}", [P, 512]) for i in range(2)]
        out = [s.ps(f"out{i}", [P, 2, P]) for i in range(2)]
        q_dup, q_ps, q_hi = s.sem("q_dup"), s.sem("q_ps"), s.sem("q_hi")
        sc_full, sc_free = s.sem("sc_full"), s.sem("sc_free")
        tab, biased, p_full = s.sem("tab"), s.sem("biased"), s.sem("p_full")
        tp_full, tp_act, tp_dve = s.sem("tp_full"), s.sem("tp_act"), s.sem("tp_dve")
        turn = s.sem("turn")
        pv_done, o_free, shares, o_sel = s.sem("pv_done"), s.sem("o_free"), s.sem("shares"), s.sem("o_sel")
        c_step, c_exp, c_tp, c_ev, c_pv, c_add = (s.sem(n) for n in ("c_step", "c_exp", "c_tp", "c_ev", "c_pv", "c_add"))
        LAG = 2
        NG2 = second[NU]
        NT = NU + NG2
        with nc.Block() as block:

            @block.gpsimd
            def _(pool):
                with pool.Fori(0, NH + 1) as h:
                    pool.wait_ge(q_ps, h + 1)
                    for d in range(2):
                        pool.tensor_copy(qd[:, :, d, :], g.z[:, 0:TT, ds(h * HD + C_QN, HD)]).then_inc(q_dup, 1)

            @block.tensor
            def _(pe):
                def score(slot, c0, i, k0, k1, keys):
                    for a, b in key_chunks(k1 - k0):
                        for n, q in enumerate((qhi, qlo)):
                            mm = pe.matmul(sc[slot][:, c0 + a:c0 + b], q[:, i * P:(i + 1) * P], keys[:, k0 + a:k0 + b],
                                           start=(n == 0), stop=(n == 1))
                    return mm

                pe.sem_inc(pv_done, 2)
                pe.sem_inc(q_ps, 1)

                def transpose_queries(h):
                    pe.wait_ge(q_dup, h * 2 + 2)
                    pe.wait_ge(sc_free, h * (NU + 2) + 1)
                    for t in range(TT):
                        mm = pe.transpose(sc[0][:, t * P:(t + 1) * P], qd[:, t].rearrange("p a b -> p (a b)"), g.ident[:])
                    mm.then_inc(q_ps, 1)

                transpose_queries(0)
                with pe.Fori(0, NH) as h:
                    pe.wait_ge(sc_free, h * (NU + 2) + 3)
                    for i in range(TT):
                        mm = score(1, 32 * i, i, 0, 32, g.kkc)
                    mm.then_inc(sc_full, 1)
                    for u in range(NU + LAG + 1):
                        if u < NU:
                            i, b, k0, k1 = units[u]
                            pe.wait_ge(sc_free, h * (NU + 2) + 3 + u)
                            score(u % 2, 0, i, k0, k1, g.kk[b]).then_inc(sc_full, 1)
                        if u == NU:
                            transpose_queries(h + 1)
                        if LAG <= u < NU + LAG:
                            v = u - LAG
                            i, b, k0, k1 = units[v]
                            nt = (k1 - k0) // P
                            pe.wait_ge(p_full, h * NU + v + 1)
                            for gr in range(groups[v]):
                                if gr == 0:
                                    pe.wait_ge(tp_act, h * NU + v + 1)
                                else:
                                    pe.wait_ge(tp_dve, h * NG2 + second[v] + 1)
                                for q in range(4 * gr, min(nt, 4 * gr + 4)):
                                    mm = pe.transpose(tp[gr][:, (q - 4 * gr) * P:(q - 4 * gr + 1) * P],
                                                      prob[v % 4][:, q * P:(q + 1) * P], g.ident[:])
                                mm.then_inc(tp_full, 1)
                        if u > LAG:
                            v = u - LAG - 1
                            i, b, k0, k1 = units[v]
                            nt = (k1 - k0) // P
                            if b == 0:
                                pe.wait_ge(o_free, h * TT + i + 1)
                            for gr in range(groups[v]):
                                if gr == 0:
                                    pe.wait_ge(tp_act, h * NU + v + 2)
                                else:
                                    pe.wait_ge(tp_dve, h * NG2 + second[v] + 2)
                                for q in range(4 * gr, min(nt, 4 * gr + 4)):
                                    mm = pe.matmul(out[i % 2][:, b, :], probT[v % 2][:, q, :],
                                                   g.z[:, k0 // P + q, VCOL[b]:VCOL[b] + P], start=(q == 0), stop=(q == nt - 1))
                            mm.then_inc(pv_done, 1)
                pe.wait_ge(c_step, 6)
                for n in range(2 * TT):
                    i, hh = n // 2, n % 2
                    if n >= 2:
                        pe.wait_ge(c_ev, n - 1)
                    src = scmp[:, i, 4 * hh:4 * hh + 4, :].rearrange("p h n -> p (h n)")
                    pe.transpose(tp[n % 2][:, 0:P], src, g.ident[:]).then_inc(c_tp, 1)
                    pe.wait_ge(c_ev, n + 1)
                    if n >= 2:
                        pe.wait_ge(c_add, n - 1)
                    pe.matmul(sc[n % 2][:, 0:4 * HD], pcT[n % 2][:], g.vcb[:].rearrange("p a b -> p (a b)"),
                              start=True, stop=True).then_inc(c_pv, 1)

            @block.scalar
            def _(act):
                act.sem_inc(tp_act, 1)

                def queries_hi(h):
                    act.wait_ge(q_ps, h + 2)
                    act.activation(qhi[:], sc[0][:], ACT.Copy).then_inc(q_hi, 1)

                queries_hi(0)
                with act.Fori(0, NH) as h:
                    for u in range(NU + LAG):
                        if u >= LAG:
                            v = u - LAG
                            i, b, k0, k1 = units[v]
                            n = min(4, (k1 - k0) // P)
                            act.wait_ge(tp_full, h * NT + v + second[v] + 1)
                            act.wait_ge(pv_done, h * NU + v + 1)
                            act.activation(probT[v % 2][:, 0:n, :].rearrange("p a b -> p (a b)"), tp[0][:, 0:n * P],
                                           ACT.Copy).then_inc(tp_act, 1)
                        if u < NU:
                            i, b, k0, k1 = units[u]
                            act.wait_ge(biased, h * NU + u + 1)
                            act.activation(prob[u % 4][:, 0:k1 - k0], prob[u % 4][:, 0:k1 - k0], ACT.Exp,
                                           bias=nmax[:, u:u + 1], scale=-1.0, accum_out=total[:, u:u + 1]).then_inc(p_full, 1)
                        if u == NU:
                            queries_hi(h + 1)
                act.wait_ge(c_step, 2)
                act.activation(scmp[:], scmp[:], ACT.Exp).then_inc(c_exp, 1)

            @block.vector
            def _(dve):
                dve.sem_inc(sc_free, 2)
                dve.sem_inc(o_free, 2)
                dve.sem_inc(tp_dve, 1)

                def finish(h, i):
                    dve.wait_ge(pv_done, h * NU + 2 * i + 2 + 2)
                    r = share[:, i % 2, :]
                    dve.reciprocal(r, total[:, 2 * i:2 * i + 2]).then_inc(shares, 1)
                    dve.wait_ge(shares, h * 2 * TT + 2 * i + 1)
                    dve.tensor_tensor(r, r, g.G[:, i, ds(h * 3 + 1, 2)], ALU.mult).then_inc(shares, 1)
                    dve.wait_ge(shares, h * 2 * TT + 2 * i + 2)
                    o = g.z[:, i, ds(h * HD + C_QN, HD)]
                    dve.tensor_scalar(o, out[i % 2][:, 0, 0:HD], share[:, i % 2, 0:1], None, ALU.mult).then_inc(o_sel, 1)
                    dve.wait_ge(o_sel, h * TT + i + 1)
                    dve.scalar_tensor_tensor(out=o, in0=out[i % 2][:, 1, 0:HD], scalar=share[:, i % 2, 1:2], in1=o,
                                             op0=ALU.mult, op1=ALU.add).then_inc(o_free, 1)


                def halve_slopes():
                    for t in (g.tsel, g.twin, g.tcmp):
                        dve.tensor_scalar(t[:], t[:], 0.5, None, ALU.mult).then_inc(tab, 1)

                def queries_lo(h):
                    dve.wait_ge(q_hi, h + 1)
                    dve.tensor_tensor(qlo[:], sc[0][:], f32(qhi[:]), ALU.subtract).then_inc(sc_free, 1)

                halve_slopes()
                queries_lo(0)
                with dve.Fori(0, NH) as h:
                    dve.wait_ge(tab, h * 3 + 3)
                    dve.wait_ge(sc_full, h * (NU + 1) + 1)
                    tn = lambda a: a.rearrange("p (t n) -> p t n", t=TT)
                    dve.tensor_tensor(scmp[:, :, ds(h, 1), :].rearrange("p t a n -> p t (a n)"), tn(sc[1][:, 0:TT * 32]),
                                      tn(g.tcmp[:]), ALU.add).then_inc(sc_free, 1)
                    for u in range(NU + LAG):
                        if u < NU:
                            i, b, k0, k1 = units[u]
                            n = k1 - k0
                            table = g.tsel if b == 0 else g.twin
                            w = SEQ if b == 0 else WINDOW + P
                            dve.wait_ge(sc_full, h * (NU + 1) + u + 2)
                            if u < 4:
                                dve.wait_ge(pv_done, h * NU + 2)
                            else:
                                v = u - 4
                                dve.wait_ge(tp_full, h * NT + v + second[v] + groups[v])
                            dve.sem_inc(turn, 1)
                            dve.tensor_tensor_reduce(prob[u % 4][:, 0:n], sc[u % 2][:, 0:n], table[:, w - n:w], -1.0, 3e38,
                                                     ALU.add, ALU.min, nmax[:, u:u + 1]).then_inc(biased, 1)
                            dve.wait_ge(biased, h * NU + u + 1)
                            dve.sem_inc(sc_free, 1)
                        if u >= LAG and groups[u - LAG] == 2:
                            v = u - LAG
                            i, b, k0, k1 = units[v]
                            nt = (k1 - k0) // P
                            dve.wait_ge(tp_full, h * NT + v + second[v] + 2)
                            dve.wait_ge(pv_done, h * NU + v + 1)
                            dve.tensor_copy(probT[v % 2][:, 4:nt, :].rearrange("p a b -> p (a b)"),
                                            tp[1][:, 0:(nt - 4) * P]).then_inc(tp_dve, 1)
                        if u >= LAG + 3 and (u - LAG) % 2 == 1:
                            finish(h, (u - LAG - 3) // 2)
                    queries_lo(h + 1)
                    halve_slopes()
                    finish(h, TT - 1)
                sv = scmp[:].rearrange("p t h n -> p (t h) n")
                m3 = lambda a: a[:].unsqueeze(2).broadcast_to([P, NH * TT, 32])
                dve.wait_ge(sc_free, NH * (NU + 2) + 3)
                dve.tensor_reduce(cm[:], sv, AX.X, ALU.max).then_inc(c_step, 1)
                dve.wait_ge(c_step, 1)
                dve.tensor_tensor(sv, sv, m3(cm), ALU.subtract).then_inc(c_step, 1)
                dve.wait_ge(c_exp, 1)
                seen = g.seen[:].rearrange("p (t n) -> p t n", t=TT).unsqueeze(2).broadcast_to([P, TT, NH, 32])
                dve.tensor_tensor(scmp[:], scmp[:], seen, ALU.mult).then_inc(c_step, 1)
                dve.wait_ge(c_step, 3)
                dve.tensor_reduce(cs[:], sv, AX.X, ALU.add).then_inc(c_step, 1)
                dve.wait_ge(c_step, 4)
                dve.tensor_scalar(cm[:], cs[:], 1e-30, None, ALU.max).then_inc(c_step, 1)
                dve.wait_ge(c_step, 5)
                dve.reciprocal(cs[:], cm[:]).then_inc(shares, 1)
                dve.wait_ge(shares, NH * 2 * TT + 1)
                csv = cs[:].rearrange("p (t h) -> p t h", t=TT)
                dve.tensor_tensor(csv, csv, g.G[:, 0:TT, 0:24:3], ALU.mult).then_inc(shares, 1)
                dve.wait_ge(shares, NH * 2 * TT + 2)
                dve.tensor_tensor(sv, sv, m3(cs), ALU.mult).then_inc(c_step, 1)
                for n in range(2 * TT):
                    i, hh = n // 2, n % 2
                    dve.wait_ge(c_tp, n + 1)
                    if n >= 2:
                        dve.wait_ge(c_pv, n - 1)
                    dve.tensor_copy(pcT[n % 2][:], tp[n % 2][:, 0:P]).then_inc(c_ev, 1)
                    dve.wait_ge(c_pv, n + 1)
                    o = g.z[:, i, C_QN + 4 * HD * hh:C_QN + 4 * HD * (hh + 1)]
                    dve.tensor_tensor(o, sc[n % 2][:, 0:4 * HD], o, ALU.add).then_inc(c_add, 1)


def diff_attention(nc, io, g):
    NU = 2 * TT
    groups = [(i + 4) // 4 for i in range(TT)]
    second = np.cumsum([0] + [n - 1 for n in groups]).tolist()
    NG2 = second[TT]
    NT = TT + NG2
    with Scope(nc, "dif") as s:
        qd = s.sb("qd", [P, TT, 2, 2, HD])
        qhi = [s.sb(f"qhi{m}", [P, SEQ], F32R) for m in range(2)]
        qlo = [s.sb(f"qlo{m}", [P, SEQ], F32R) for m in range(2)]
        prob = [s.sb(f"prob{i}", [P, SEQ]) for i in range(6)]
        probT = [s.sb(f"probT{i}", [P, TT, P]) for i in range(2)]
        nmax = s.sb("nmax", [P, NU])
        total = s.sb("total", [P, NU])
        share = s.sb("share", [P, TT, 2])
        factor = s.sb("factor", [P, 2])
        osq = s.sb("osq", [P, TT, NDH, 2 * HD])
        oss = s.sb("oss", [P, TT * NDH])
        sc = [s.ps(f"sc{i}", [P, SEQ]) for i in range(2)]
        tp = [s.ps(f"tp{i}", [P, 512]) for i in range(2)]
        out = [s.ps(f"out{i}", [P, P]) for i in range(2)]
        q_dup, q_ps, q_hi, q_lo = s.sem("q_dup"), s.sem("q_ps"), s.sem("q_hi"), s.sem("q_lo")
        sc_full, sc_free = s.sem("sc_full"), s.sem("sc_free")
        tab, biased, p_full = s.sem("tab"), s.sem("biased"), s.sem("p_full")
        joined, shares = s.sem("joined"), s.sem("shares")
        tp_full, tp_act, tp_dve = s.sem("tp_full"), s.sem("tp_act"), s.sem("tp_dve")
        turn = s.sem("turn")
        pv_done, o_free, o_step, o_act = s.sem("pv_done"), s.sem("o_free"), s.sem("o_step"), s.sem("o_act")
        with nc.Block() as block:

            @block.gpsimd
            def _(pool):
                with pool.Fori(0, NDH) as j:
                    pool.wait_ge(q_ps, j * 2 + 1)
                    for m in range(2):
                        for d in range(2):
                            pool.tensor_copy(qd[:, :, m, d, :], g.z[:, 0:TT, ds(j * 2 * HD + C_QD + m * HD, HD)]).then_inc(q_dup, 1)
                pool.wait_ge(q_ps, NDH * 2 + 1)
                pool.sem_inc(q_dup, 4)

            @block.tensor
            def _(pe):
                pe.sem_inc(pv_done, 2)
                pe.sem_inc(q_ps, 1)

                def transpose_queries(j):
                    pe.wait_ge(q_dup, j * 4 + 4)
                    for m in range(2):
                        pe.wait_ge(sc_free, j * (NU + 2) + m + 1)
                        for t in range(TT):
                            mm = pe.transpose(sc[m][:, t * P:(t + 1) * P], qd[:, t, m].rearrange("p a b -> p (a b)"), g.ident[:])
                        mm.then_inc(q_ps, 1)

                def transpose_probs(j, v):
                    nt = v + 1
                    pe.wait_ge(joined, j * TT + v + 1)
                    for gr in range(groups[v]):
                        if gr == 0:
                            pe.wait_ge(tp_act, j * TT + v + 1)
                        else:
                            pe.wait_ge(tp_dve, j * NG2 + second[v] + 1)
                        for q in range(4 * gr, min(nt, 4 * gr + 4)):
                            mm = pe.transpose(tp[gr][:, (q - 4 * gr) * P:(q - 4 * gr + 1) * P],
                                              prob[2 * (v % 3)][:, q * P:(q + 1) * P], g.ident[:])
                        mm.then_inc(tp_full, 1)

                def values(n, j, v):
                    nt = v + 1
                    pe.wait_ge(o_free, j * TT + v + 1)
                    for gr in range(groups[v]):
                        if gr == 0:
                            pe.wait_ge(tp_act, j * TT + v + 2)
                        else:
                            pe.wait_ge(tp_dve, j * NG2 + second[v] + 2)
                        for q in range(4 * gr, min(nt, 4 * gr + 4)):
                            mm = pe.matmul(out[v % 2][:], probT[v % 2][:, q, :],
                                           g.z[:, q, ds(n * 2 * HD + C_DV, 2 * HD)], start=(q == 0), stop=(q == nt - 1))
                    mm.then_inc(pv_done, 1)

                def scores(n, j, i):
                    for m in range(2):
                        pe.wait_ge(sc_free, j * (NU + 2) + 2 * i + m + 3)
                        for a, b in key_chunks((i + 1) * P):
                            for x, q in enumerate((qhi[m], qlo[m])):
                                mm = pe.matmul(sc[m][:, a:b], q[:, i * P:(i + 1) * P], g.kkd[:, ds(n * 2 * SEQ + m * SEQ + a, b - a)],
                                               start=(x == 0), stop=(x == 1))
                        mm.then_inc(sc_full, 1)

                transpose_queries(0)
                with pe.Fori(0, NDH // 2) as n:
                    for gg in range(2):
                        j = n * 2 + gg
                        for i in range(TT + 3):
                            if i < TT:
                                scores(n, j, i)
                            if i == TT:
                                transpose_queries(j + 1)
                            if 2 <= i < TT + 2:
                                transpose_probs(j, i - 2)
                            if i > 2:
                                values(n, j, i - 3)

            @block.scalar
            def _(act):
                act.sem_inc(tp_act, 1)

                def queries_hi(j):
                    for m in range(2):
                        act.wait_ge(q_ps, j * 2 + m + 2)
                        act.activation(qhi[m][:], sc[m][:], ACT.Copy).then_inc(q_hi, 1)

                queries_hi(0)
                with act.Fori(0, NDH) as j:
                    for i in range(TT + 2):
                        if i > 1:
                            v = i - 2
                            n = min(4, v + 1)
                            act.wait_ge(tp_full, j * NT + v + second[v] + 1)
                            act.wait_ge(pv_done, j * TT + v + 1)
                            act.activation(probT[v % 2][:, 0:n, :].rearrange("p a b -> p (a b)"), tp[0][:, 0:n * P],
                                           ACT.Copy).then_inc(tp_act, 1)
                        if i < TT:
                            for m in range(2):
                                u = 2 * i + m
                                act.wait_ge(biased, j * NU + u + 1)
                                pr = prob[u % 6][:, 0:(i + 1) * P]
                                act.activation(pr, pr, ACT.Exp, bias=nmax[:, u:u + 1], scale=-1.0,
                                               accum_out=total[:, u:u + 1]).then_inc(p_full, 1)
                        if i == TT:
                            queries_hi(j + 1)
                act.wait_ge(o_step, 1)
                act.activation(oss[:], oss[:], ACT.Sqrt).then_inc(o_act, 1)

            @block.vector
            def _(dve):
                dve.sem_inc(sc_free, 2)
                dve.sem_inc(o_free, 2)
                dve.sem_inc(tp_dve, 1)
                dve.tensor_scalar(g.tsel[:], g.tsel[:], 512.0, None, ALU.mult).then_inc(tab, 1)
                dve.wait_ge(tab, 1)

                def finish(j, i):
                    dve.wait_ge(pv_done, j * TT + i + 3)
                    dve.tensor_scalar(g.z[:, i, ds(j * 2 * HD + C_QD, 2 * HD)], out[i % 2][:], share[:, i, 0:1], None,
                                      ALU.mult).then_inc(o_free, 1)

                def quarter_slopes():
                    dve.tensor_scalar(g.tsel[:], g.tsel[:], 0.25, None, ALU.mult).then_inc(tab, 1)

                def queries_lo(j):
                    for m in range(2):
                        dve.wait_ge(q_hi, j * 2 + m + 1)
                        dve.tensor_tensor(qlo[m][:], sc[m][:], f32(qhi[m][:]), ALU.subtract).then_inc(q_lo, 1)
                        dve.wait_ge(q_lo, j * 2 + m + 1)
                        dve.sem_inc(sc_free, 1)

                quarter_slopes()
                queries_lo(0)
                with dve.Fori(0, NDH) as j:
                    dve.wait_ge(tab, j + 2)
                    for i in range(TT + 2):
                        if i < TT:
                            n = (i + 1) * P
                            for m in range(2):
                                u = 2 * i + m
                                dve.wait_ge(sc_full, j * NU + u + 1)
                                if i >= 3:
                                    v = i - 3
                                    dve.wait_ge(tp_full, j * NT + v + second[v] + groups[v])
                                else:
                                    dve.wait_ge(pv_done, j * TT + 2)
                                dve.sem_inc(turn, 1)
                                dve.tensor_tensor_reduce(prob[u % 6][:, 0:n], sc[m][:, 0:n], g.tsel[:, SEQ - n:SEQ], -1.0, 3e38,
                                                         ALU.add, ALU.min, nmax[:, u:u + 1]).then_inc(biased, 1)
                                dve.wait_ge(biased, j * NU + u + 1)
                                dve.sem_inc(sc_free, 1)
                        if 0 < i <= TT:
                            v = i - 1
                            dve.wait_ge(p_full, j * NU + 2 * v + 2)
                            dve.reciprocal(share[:, v, :], total[:, 2 * v:2 * v + 2]).then_inc(shares, 1)
                            dve.wait_ge(shares, j * 2 * TT + 2 * v + 1)
                            dve.tensor_scalar(factor[:, v % 2:v % 2 + 1], share[:, v, 1:2], total[:, 2 * v:2 * v + 1], g.neglam[:, 0:1],
                                              ALU.mult, ALU.mult).then_inc(shares, 1)
                            dve.wait_ge(shares, j * 2 * TT + 2 * v + 2)
                            p0, p1 = (prob[2 * (v % 3) + m][:, 0:(v + 1) * P] for m in range(2))
                            dve.scalar_tensor_tensor(out=p0, in0=p1, scalar=factor[:, v % 2:v % 2 + 1], in1=p0,
                                                     op0=ALU.mult, op1=ALU.add).then_inc(joined, 1)
                        if i > 1 and groups[i - 2] == 2:
                            v = i - 2
                            dve.wait_ge(tp_full, j * NT + v + second[v] + 2)
                            dve.wait_ge(pv_done, j * TT + v + 1)
                            dve.tensor_copy(probT[v % 2][:, 4:v + 1, :].rearrange("p a b -> p (a b)"),
                                            tp[1][:, 0:(v - 3) * P]).then_inc(tp_dve, 1)
                        if i >= 4:
                            finish(j, i - 4)
                    queries_lo(j + 1)
                    quarter_slopes()
                    finish(j, TT - 2)
                    finish(j, TT - 1)
                o = g.z[:, 0:TT, C_QD:C_M].rearrange("p t (j v) -> p t j v", j=NDH)
                dve.wait_ge(o_free, NDH * TT + 2)
                dve.tensor_tensor(osq[:], o, o, ALU.mult).then_inc(shares, 1)
                dve.wait_ge(shares, NDH * 2 * TT + 1)
                dve.tensor_reduce(oss[:].rearrange("p (t j) -> p t j", t=TT), osq[:], AX.X, ALU.add).then_inc(shares, 1)
                dve.wait_ge(shares, NDH * 2 * TT + 2)
                dve.tensor_scalar(oss[:], oss[:], 1.0 / (2 * HD), EPS, ALU.mult, ALU.add).then_inc(o_step, 1)
                dve.wait_ge(o_act, 1)
                dve.reciprocal(oss[:], oss[:]).then_inc(o_step, 1)
                dve.wait_ge(o_step, 2)
                r4 = oss[:].rearrange("p (t j) -> p t j", t=TT).unsqueeze(3).broadcast_to([P, TT, NDH, 2 * HD])
                dve.tensor_tensor(o, o, r4, ALU.mult).then_inc(o_step, 1)
                dve.wait_ge(o_step, 3)
                for j in range(NDH):
                    oj = g.z[:, 0:TT, C_QD + j * 2 * HD:C_QD + (j + 1) * 2 * HD]
                    dve.tensor_tensor(oj, oj, g.subln[:].unsqueeze(1).broadcast_to([P, TT, 2 * HD]), ALU.mult).then_inc(o_step, 1)


T_SEL, T_DIF, T_WIN, T_CMP, T_SN, T_S, T_N, T_MAP, T_IDX, T_SUM, T_END = np.cumsum(
    [0, PAST + 1, PAST + 1, WINDOW + 1, 32, 4, 2, 2, 2, 15, 16]).tolist()


def decode_table():
    r = np.arange(16)
    t = np.zeros((16, T_END), np.float32)
    slope_a = 2.0 ** -(r % 8 + 1.0)
    slope_b = 2.0 ** (-2.0 * (r % 8 // 2 + 1))
    pos = np.arange(PAST + 1) - PAST
    t[:, T_SEL:T_DIF] = slope_a[:, None] * pos
    t[:, T_DIF:T_WIN] = slope_b[:, None] * pos
    t[:, T_WIN:T_CMP] = slope_a[:, None] * (np.arange(WINDOW + 1) - WINDOW)
    t[:, T_WIN] = NEG
    t[:, T_CMP:T_SN] = slope_a[:, None] * (32 * np.arange(32) + 31 - PAST)
    t[:, T_SN:T_S] = r[:, None] // 4 == np.arange(4)
    t[:, T_S:T_N] = r[:, None] // 8 == np.arange(2)
    t[:, T_N:T_MAP] = r[:, None] % 8 // 4 == np.arange(2)
    t[:, T_MAP:T_IDX] = r[:, None] % 2 == np.arange(2)
    t[:, T_IDX:T_SUM] = np.arange(1, 16)
    t[:, T_SUM:T_END] = r[:, None] // 8 == r[None, :] // 8
    return t


def decode_attention(nc, io, g):
    NP = NDEC // 2
    R = 16
    NW = WINDOW // P
    NY = 11
    with Scope(nc, "dec") as s:
        tab = s.sb("tab", [R, T_END])
        coef = s.sb("coef", [R, 1])
        ptab = s.sb("ptab", [1, NDEC * NPAGE], I32)
        kin = [s.sb(f"kin{i}", [P, 2, NPAGE, CACHE_W]) for i in range(2)]
        zc = lambda c, n: g.z[:, 0:TT, c:c + n]
        win = [s.sb("win0", [P, 2 * NW, 2 * HD])[:], zc(C_CK + CACHE_W, 2 * HD)]
        win = [w.rearrange("p (x t) c -> p x t c", x=2) for w in win]
        vnew = [s.sb(f"vnew{i}", [R, 6 * HD]) for i in range(2)]
        early = kin[1][0:NDEC].rearrange("p x t c -> p (x t c)")
        qs = early[:, 0:2 * NH * HD].rearrange("p (h x d) -> p h x d", h=NH, x=2)
        qdt = early[:, 1024:1024 + NH * HD].rearrange("p (h d) -> p h d", h=NH)
        kns = early[:, 2048:2048 + 6 * HD].rearrange("p (h d) -> p h d", h=6)
        knd = early[:, 3072:3072 + 4 * HD].rearrange("p (b x d) -> p b x d", b=2, x=2)
        nrs = s.sb("nrs", [NDEC, 6])
        qb = s.sb("qb", [P, 3, NP * R])
        qdb = s.sb("qdb", [P, NP, 4 * R])
        knT = s.sb("knT", [P, 2, NP])
        kndT = s.sb("kndT", [P, 2, NDEC])
        qc = s.sb("qc", [P, 3, R])
        qdc = s.sb("qdc", [P, 4 * R])
        sq = zc(C_CK, 6 * HD)
        sqw = zc(C_CK + 8 * HD, HD)
        rs = s.sb("rs", [P, 2, NPAGE, 6])
        rw = s.sb("rw", [P, 2, NW])
        nS = zc(C_CK + 6 * HD, 2 * HD).rearrange("p t (x d) -> p t x d", x=2)
        nW = g.z[:, 0:NW, C_CK + 9 * HD:C_CK + 11 * HD].rearrange("p t (x d) -> p t x d", x=2)
        nD = zc(C_CK, 4 * HD)
        kT = s.sb("kT", [P, 2, 512])
        kc = s.sb("kc", [32, 2, HD])
        kcq = s.sb("kcq", [32, 2, HD])
        kcr = s.sb("kcr", [32, 2])
        vc = [s.sb(f"vc{i}", [32, 2, HD]) for i in range(2)]
        kcT = s.sb("kcT", [P, 32])
        pS = s.sb("pS", [R, PAST + 1])
        pD = s.sb("pD", [R, PAST + 1])
        pW = g.z[0:R, TT, C_CK:C_CK + WINDOW + 1]
        pC = s.sb("pC", [R, 32])
        st = s.sb("st", [R, 16])
        imp = s.sb("imp", [R, 16])
        low = s.sb("low", [R, 16])
        pT = s.sb("pT", [P, 21, R])
        o16 = s.sb("o16", [R, 5 * HD])
        od = kin[0][0:NDEC].rearrange("p x t c -> p (x t c)")[:, 0:NH * 5 * HD].rearrange("p (h c) -> p h c", h=NH)
        kt = s.ps("kt", [P, 2, 512])
        ss = s.ps("ss", [R, PAST])
        sd = s.ps("sd", [R, PAST])
        ma = s.ps("ma", [P, 512])
        mb = s.ps("mb", [P, 512])
        ckp = nS
        kin_in, win_in = [s.sem(f"kin_in{i}") for i in range(2)], [s.sem(f"win_in{i}") for i in range(2)]
        vnew_in = [s.sem(f"vnew_in{i}") for i in range(2)]
        slot_free, row_d, t_in = s.sem("slot_free"), s.sem("row_d"), s.sem("t_in")
        chain, pre, pre_ps = s.sem("chain"), s.sem("pre"), s.sem("pre_ps")
        pt_in = s.sem("pt_in")

        def load_pair(sp, p):
            j = p % 2
            for x in range(2):
                b = 2 * p + x
                for pg in range(NPAGE):
                    n = b * NPAGE + pg
                    page = sp.value_load(ptab[0:1, n:n + 1], min_val=0, max_val=io["cache_kv"].shape[1] - 1)
                    sp.dma_start(kin[j][:, x, pg, :], io["cache_kv"][0, ds(page, 1)].rearrange("a p c -> (a p) c")
                                 ).then_inc(kin_in[j], 16)
                sp.dma_start(win[j][:, x], io["state_win_kv"][0, b].rearrange("(t p) c -> p t c", p=P)).then_inc(win_in[j], 16)
                new = io["new_d"][b:b + 1, :]
                rr = slice(8 * x, 8 * x + 8)
                sp.dma_start(vnew[j][rr, 0:HD], new[:, C_SV - C_CK:C_DK - C_CK].broadcast_to([8, HD])).then_inc(vnew_in[j], 16)
                sp.dma_start(vnew[j][rr, HD:2 * HD], new[:, C_WV - C_CK:C_G - C_CK].broadcast_to([8, HD])).then_inc(vnew_in[j], 16)
                sp.dma_start(vnew[j][rr, 2 * HD:6 * HD], new[:, C_DV - C_CK:C_WK - C_CK].broadcast_to([8, 4 * HD])).then_inc(vnew_in[j], 16)

        with nc.Block() as block:

            @block.sync
            def _(sp):
                sp.dma_start(tab[:], io["dec_tab"]).then_inc(t_in, 16)
                sp.dma_start(ptab[:], io["page_table"].rearrange("b n -> (b n)").unsqueeze(0)).then_inc(pt_in, 16)
                sp.dma_start(io["new_d"], g.z[0:NDEC, TT, C_CK:C_G]).then_inc(row_d, 16)
                sp.wait_ge(row_d, 16)
                sp.wait_ge(pt_in, 16)
                load_pair(sp, 0)
                sp.wait_ge(t_in, 16)

            @block.vector
            def _(dve):
                n = [0]

                def link(ins):
                    n[0] += 1
                    ins.then_inc(chain, 1)
                    dve.wait_ge(chain, n[0])

                dve.wait_ge(t_in, 16)
                link(dve.scalar_tensor_tensor(out=coef[:], in0=tab[:, T_MAP + 1:T_MAP + 2], scalar=g.neglam[0:R, 0:1],
                                              in1=tab[:, T_MAP:T_MAP + 1], op0=ALU.mult, op1=ALU.add))
                link(dve.memset(qb[:], 0.0))
                link(dve.memset(qdb[:], 0.0))
                zrow = lambda c, k: g.z[0:NDEC, TT, c:c + k * HD].rearrange("p (a b) -> p a b", b=HD)
                q = zrow(C_QN, NH)
                both = lambda a, k: a.unsqueeze(2).broadcast_to([NDEC, k, 2, HD])
                for b in range(3):
                    if b < 2:
                        link(dve.tensor_tensor(qs, both(q, NH), g.gain[0:NDEC, 2 + b:3 + b, :].unsqueeze(2).broadcast_to([NDEC, NH, 2, HD]), ALU.mult))
                    else:
                        link(dve.tensor_copy(qs, both(q, NH)))
                    dve.sem_inc(pre, 1)
                    dve.wait_ge(pre_ps, b + 1)
                    src = ma[:, 0:NH * NDEC].rearrange("p (h w x) -> p w x h", h=NH, x=2)
                    dst = qb[:, b, :].rearrange("p (w x h) -> p w x h", x=2, h=NH)
                    for x in range(2):
                        rr = slice(HD * x, HD * x + HD)
                        link(dve.tensor_copy(dst[rr, :, x, :], src[rr, :, x, :]))
                qd = zrow(C_QD, 8)
                link(dve.tensor_tensor(qs[:, :, 0, :], qd, g.gain[0:NDEC, 4:5, :].broadcast_to([NDEC, 8, HD]), ALU.mult))
                link(dve.tensor_copy(qdt, qs[:, :, 0, :]))
                dve.sem_inc(pre, 1)
                dve.wait_ge(pre_ps, 4)
                src = ma[:, 0:4 * NDEC].rearrange("p (n g w x) -> p n w x g", n=2, g=2, x=2)
                dst = qdb[:].rearrange("p w (c k) -> p w c k", c=4)
                for x in range(2):
                    for nn in range(2):
                        for m in range(2):
                            rr = slice(HD * m, HD * m + HD)
                            c0 = x * 8 + nn * 4 + m
                            link(dve.tensor_copy(dst[rr, :, 2 * x + nn, c0:c0 + 3:2], src[rr, nn, :, x, :]))
                groups = [(0, C_SK, 1), (1, C_DK, 4), (5, C_WK, 1)]
                for o, c, k in groups:
                    link(dve.tensor_tensor(kns[:, o:o + k, :], zrow(c, k), zrow(c, k), ALU.mult))
                link(dve.tensor_reduce(nrs[:], kns[:], AX.X, ALU.add))
                link(dve.tensor_scalar(nrs[:], nrs[:], 1.0 / HD, EPS, ALU.mult, ALU.add))
                dve.sem_inc(pre, 1)
                dve.wait_ge(pre_ps, 5)
                link(dve.reciprocal(nrs[:], nrs[:]))
                for o, c, k in groups:
                    link(dve.tensor_tensor(kns[:, o:o + k, :], zrow(c, k), nrs[:, o:o + k].unsqueeze(2).broadcast_to([NDEC, k, HD]), ALU.mult))
                for b, o in enumerate((0, 5)):
                    link(dve.tensor_copy(knd[:, b], kns[:, o:o + 1, :].broadcast_to([NDEC, 2, HD])))
                dve.sem_inc(pre, 1)
                dve.wait_ge(pre_ps, 6)
                for b in range(2):
                    for x in range(2):
                        rr = slice(HD * x, HD * x + HD)
                        src = ma[rr, b * NDEC:(b + 1) * NDEC].rearrange("p (w x) -> p w x", x=2)
                        link(dve.tensor_copy(knT[rr, b, :], src[:, :, x]))
                link(dve.tensor_copy(kndT[:], ma[:, 2 * NDEC:4 * NDEC].rearrange("p (a b) -> p a b", a=2)))

            @block.scalar
            def _(act):
                act.wait_ge(pre, 5)
                act.activation(nrs[:], nrs[:], ACT.Sqrt).then_inc(pre_ps, 1)

            @block.tensor
            def _(pe):
                idn = g.ident[0:NDEC, 0:NDEC]
                for b in range(3):
                    pe.wait_ge(pre, b + 1)
                    for h in range(NH):
                        mm = pe.transpose(ma[:, h * NDEC:(h + 1) * NDEC], qs[:, h].rearrange("p a b -> p (a b)"), idn)
                    mm.then_inc(pre_ps, 1)
                pe.wait_ge(pre, 4)
                for h in range(4):
                    mm = pe.transpose(ma[:, h * NDEC:(h + 1) * NDEC], qdt[:, 2 * h:2 * h + 2, :].rearrange("p a b -> p (a b)"), idn)
                mm.then_inc(pre_ps, 1)
                pe.wait_ge(pre, 6)
                for b in range(2):
                    pe.transpose(ma[:, b * NDEC:(b + 1) * NDEC], knd[:, b].rearrange("p a b -> p (a b)"), idn)
                for nn in range(2):
                    mm = pe.transpose(ma[:, (2 + nn) * NDEC:(3 + nn) * NDEC], kns[:, 1 + 2 * nn:3 + 2 * nn, :].rearrange("p a b -> p (a b)"), idn)
                mm.then_inc(pre_ps, 1)

        with nc.Block() as block:
            (sq_done, sum_done, root_done, nS_done, nD_done, nW_done, ck_done, kc_ps, kc_done, kcT_ps, kcT_sb, kt_full, kt_sb,
             kt_used, s_full, ss_read, masked, exps, pc_done, imp_ps, pT_ps, pT_sb, pv, o_done, q_cur, chain2) = (
                s.sem(x) for x in ("sq_done", "sum_done", "root_done", "nS_done", "nD_done", "nW_done", "ck_done", "kc_ps",
                                   "kc_done", "kcT_ps", "kcT_sb", "kt_full", "kt_sb", "kt_used", "s_full", "ss_read", "masked",
                                   "exps", "pc_done", "imp_ps", "pT_ps", "pT_sb", "pv", "o_done", "q_cur", "chain2"))
            o_out = s.pool_sem("o_out")

            @block.sync
            def _(sp):
                for p in range(1, NP):
                    if p >= 2:
                        sp.wait_ge(slot_free, p - 1)
                    load_pair(sp, p)

            @block.gpsimd
            def _(pool):
                for p in range(NP):
                    pool.wait_ge(o_done, p + 1)
                    pool.dma_start(io["dec_d"][p * R:(p + 1) * R, :], o16[:]).then_inc(o_out, 16)
                    pool.wait_ge(o_out, p * 16 + 16)

            @block.scalar
            def _(act):

                def squares(p, xs):
                    i, j = p // 2, p % 2
                    for x in xs:
                        if x == 0:
                            act.wait_ge(kin_in[j], i * 256 + 256)
                        else:
                            act.wait_ge(sum_done, p * 3 + 1)
                        act.activation(sq, kin[j][:, x, :, C_SK - C_CK:C_DV - C_CK], ACT.Square).then_inc(sq_done, 1)
                    if 1 not in xs:
                        return
                    act.wait_ge(win_in[j], i * 32 + 32)
                    act.activation(sqw, win[j][:, :, :, 0:HD].rearrange("p a b c -> p (a b) c"), ACT.Square).then_inc(sq_done, 1)
                    act.wait_ge(sum_done, p * 3 + 3)
                    act.activation(rs[:], rs[:], ACT.Sqrt).then_inc(root_done, 1)
                    act.activation(rw[:], rw[:], ACT.Sqrt).then_inc(root_done, 1)

                def root_compressed(p):
                    i, j = p // 2, p % 2
                    act.wait_ge(kc_done, p * 3 + 1)
                    act.activation(kcr[:], kcr[:], ACT.Sqrt).then_inc(root_done, 1)

                def middle(p):
                    i, j = p // 2, p % 2
                    for y in range(NY):
                        at = p * NY + y
                        act.wait_ge(kt_full, at + 1)
                        if at >= 2:
                            act.wait_ge(kt_used, at - 1)
                        act.activation(kT[:, at % 2, :], kt[:, at % 2, :], ACT.Copy).then_inc(kt_sb, 1)
                        if y == 0:
                            act.wait_ge(kcT_ps, p + 1)
                            act.activation(kcT[:], ma[:, 4 * HD:4 * HD + 32], ACT.Copy).then_inc(kcT_sb, 1)
                        if y == 5:
                            act.wait_ge(masked, p * 4 + 1)
                            act.activation(pC[:], pC[:], ACT.Exp, bias=st[:, 0:1], scale=1.0, accum_out=st[:, 4:5]).then_inc(exps, 1)
                    for x, t in enumerate((pS[:], pD[:], pW)):
                        act.wait_ge(masked, p * 4 + x + 2)
                        act.activation(t, t, ACT.Exp, bias=st[:, x + 1:x + 2], scale=1.0,
                                       accum_out=st[:, x + 5:x + 6]).then_inc(exps, 1)

                def evacuate(p):
                    i, j = p // 2, p % 2
                    act.wait_ge(pT_ps, p + 1)
                    act.activation(pT[:, 0:20, :].rearrange("p a b -> p (a b)"), mb[:, 0:20 * R], ACT.Copy).then_inc(pT_sb, 1)
                    act.activation(pT[0:32, 20, :], mb[0:32, 20 * R:21 * R], ACT.Copy).then_inc(pT_sb, 1)

                squares(0, (0, 1))
                root_compressed(0)
                for p in range(NP):
                    middle(p)
                    if p + 1 < NP:
                        squares(p + 1, (0,))
                    evacuate(p)
                    if p + 1 < NP:
                        squares(p + 1, (1,))
                        root_compressed(p + 1)

            @block.tensor
            def _(pe):

                def compress(p):
                    i, j = p // 2, p % 2
                    pe.wait_ge(ck_done, p + 1)
                    for t in range(NPAGE):
                        mm = pe.matmul(ma[0:32, 0:2 * HD], g.wcmp[:, 0, 28 - 4 * t:60 - 4 * t],
                                       ckp[:, t].rearrange("p a b -> p (a b)"), start=(t == 0), stop=(t == NPAGE - 1))
                    for t in range(NPAGE):
                        mm = pe.matmul(ma[0:32, 2 * HD:4 * HD], g.wcmp[:, 1, 28 - 4 * t:60 - 4 * t],
                                       kin[j][:, :, t, C_CV - C_CK:C_SK - C_CK], start=(t == 0), stop=(t == NPAGE - 1))
                    mm.then_inc(kc_ps, 1)

                def scores(p):
                    i, j = p // 2, p % 2
                    def transposed(y):
                        at = p * NY + y
                        if at >= 2:
                            pe.wait_ge(kt_sb, at - 1)
                        x, c = (y - 2) // 2, y % 2
                        if y < 2:
                            src = nS.rearrange("p t a b -> p t (a b)")
                            pe.wait_ge(nS_done, p + 1)
                        elif y < 10:
                            src = nD[:, :, x % 2 * P:(x % 2 + 1) * P]
                            pe.wait_ge(nD_done, p * 2 + x // 2 + 1)
                        else:
                            src = nW.rearrange("p t a b -> p t (a b)")
                            pe.wait_ge(nW_done, p + 1)
                        for q in range(4):
                            mm = pe.transpose(kt[:, at % 2, q * P:(q + 1) * P], src[:, c * 4 + q], g.ident[:])
                        mm.then_inc(kt_full, 1)

                    def score(y):
                        at = p * NY + y
                        x, c = (y - 2) // 2, y % 2
                        pe.wait_ge(kt_sb, at + 1)
                        if y < 2:
                            out, q, first, last = ss[:, c * 512:(c + 1) * 512], qc[:, 0, :], True, True
                        elif y < 10:
                            out, q, first, last = sd[:, c * 512:(c + 1) * 512], qdc[:, x * R:(x + 1) * R], x == 0, x == 3
                        else:
                            out, q, first, last = ss[:, 0:WINDOW], qc[:, 1, :], True, True
                        if y == 2 and p:
                            pe.wait_ge(o_done, p)
                        pe.matmul(out, q, kT[:, at % 2, :], start=first, stop=last, skip_group_check=True).then_inc(kt_used, 1)

                    transposed(0)
                    pe.wait_ge(kc_done, p * 3 + 3)
                    pe.matmul(ma[:, 4 * HD:4 * HD + 32], kc[:].rearrange("p a b -> p (a b)"), g.ident[0:32, 0:32], start=True,
                              stop=True).then_inc(kcT_ps, 1)
                    transposed(1)
                    pe.wait_ge(kcT_sb, p + 1)
                    pe.wait_ge(q_cur, p + 1)
                    pe.matmul(ma[0:R, 288:320], qc[:, 2, :], kcT[:], start=True, stop=True).then_inc(s_full, 1)
                    score(0)
                    for y in range(2, NY):
                        transposed(y)
                        score(y - 1)
                        if y == 7:
                            pe.wait_ge(pc_done, p + 1)
                            pe.matmul(ma[0:R, 320:321], qc[:, 0, :], knT[:, 0, p:p + 1], start=True, stop=True).then_inc(s_full, 1)
                            pe.matmul(ma[0:R, 324:356], tab[:, T_SUM:T_END], pC[:], start=True, stop=True).then_inc(imp_ps, 1)
                    pe.wait_ge(ss_read, p + 1)
                    for x in range(4):
                        mm = pe.matmul(ma[0:R, 322:323], qdc[:, x * R:(x + 1) * R], kndT[:, x % 2, p * 2 + x // 2:p * 2 + x // 2 + 1],
                                       start=(x == 0), stop=(x == 3))
                    pe.matmul(ma[0:R, 321:322], qc[:, 1, :], knT[:, 1, p:p + 1], start=True, stop=True).then_inc(s_full, 1)
                    score(NY - 1)
                    pe.wait_ge(kt_used, (p + 1) * NY)
                    pe.sem_inc(s_full, 1)

                def outputs(p):
                    i, j = p // 2, p % 2
                    pe.wait_ge(exps, p * 4 + 4)
                    idr = g.ident[0:R, 0:R]
                    for x, (src, n0, n) in enumerate(((pS, 0, 8), (pD, 8, 8), (pW, 16, 4))):
                        for t in range(n):
                            pe.transpose(mb[:, (n0 + t) * R:(n0 + t + 1) * R], src[:, t * P:(t + 1) * P], idr)
                    pe.transpose(mb[0:32, 20 * R:21 * R], pC[:], idr).then_inc(pT_ps, 1)
                    pe.wait_ge(pT_sb, p * 2 + 2)
                    for t in range(NPAGE):
                        pe.matmul(sd[0:R, 512:640], pT[:, t, :], kin[j][:, :, t, C_SV - C_CK:C_DK - C_CK],
                                  start=(t == 0), stop=(t == NPAGE - 1))
                    for t in range(NPAGE):
                        pe.matmul(sd[0:R, 0:512], pT[:, 8 + t, :], kin[j][:, :, t, C_DV - C_CK:CACHE_W],
                                  start=(t == 0), stop=(t == NPAGE - 1))
                    for t in range(NW):
                        pe.matmul(sd[0:R, 640:768], pT[:, 16 + t, :], win[j][:, :, t, HD:2 * HD],
                                  start=(t == 0), stop=(t == NW - 1))
                    pe.matmul(sd[0:R, 768:896], pT[0:32, 20, :], vc[j][:].rearrange("p a b -> p (a b)"), start=True, stop=True
                              ).then_inc(pv, 1)

                compress(0)
                for p in range(NP):
                    scores(p)
                    if p + 1 < NP:
                        compress(p + 1)
                    outputs(p)

            @block.vector
            def _(dve):
                n = [0]

                def link(ins):
                    n[0] += 1
                    ins.then_inc(chain2, 1)
                    dve.wait_ge(chain2, n[0])

                def norm_diff(p, x):
                    j = p % 2
                    kd = kin[j][:, x, :, C_DK - C_CK:C_DV - C_CK].rearrange("p a (b c) -> p a b c", c=HD)
                    dve.tensor_tensor(nD.rearrange("p a (b c) -> p a b c", c=HD), kd,
                                      rs[:, x, :, 2:6].unsqueeze(3).broadcast_to([P, NPAGE, 4, HD]), ALU.mult).then_inc(nD_done, 1)

                def front(p):
                    i, j = p // 2, p % 2

                    dve.tensor_copy(qc[:], qb[:, :, p * R:(p + 1) * R])
                    dve.tensor_copy(qdc[:], qdb[:, p, :]).then_inc(q_cur, 1)
                    dve.wait_ge(kin_in[j], i * 256 + 256)
                    for x in range(2):
                        ins = dve.tensor_tensor(ckp[:, :, x, :], kin[j][:, x, :, 0:HD],
                                                g.pe4[:].unsqueeze(1).broadcast_to([P, NPAGE, HD]), ALU.add)
                    ins.then_inc(ck_done, 1)
                    for x in range(2):
                        dve.wait_ge(sq_done, p * 3 + x + 1)
                        dve.tensor_reduce(rs[:, x], sq.rearrange("p a (b c) -> p a b c", c=HD), AX.X, ALU.add).then_inc(sum_done if x == 0 else chain2, 1)
                    n[0] += 1
                    dve.wait_ge(sq_done, p * 3 + 3)
                    link(dve.tensor_reduce(rw[:].rearrange("p a b -> p (a b)"), sqw, AX.X, ALU.add))
                    dve.tensor_scalar(rs[:], rs[:], 1.0 / HD, EPS, ALU.mult, ALU.add).then_inc(sum_done, 1)
                    dve.tensor_scalar(rw[:], rw[:], 1.0 / HD, EPS, ALU.mult, ALU.add).then_inc(sum_done, 1)
                    dve.wait_ge(kc_ps, p + 1)
                    link(dve.tensor_copy(kc[:], ma[0:32, 0:2 * HD].rearrange("p (a b) -> p a b", a=2)))
                    link(dve.tensor_copy(vc[j][:], ma[0:32, 2 * HD:4 * HD].rearrange("p (a b) -> p a b", a=2)))
                    link(dve.tensor_tensor(kcq[:], kc[:], kc[:], ALU.mult))
                    link(dve.tensor_reduce(kcr[:], kcq[:], AX.X, ALU.add))
                    dve.tensor_scalar(kcr[:], kcr[:], 1.0 / HD, EPS, ALU.mult, ALU.add).then_inc(kc_done, 1)
                    dve.wait_ge(root_done, p * 3 + 2)
                    link(dve.reciprocal(rs[:], rs[:]))
                    link(dve.reciprocal(rw[:], rw[:]))
                    for x in range(2):
                        ins = dve.tensor_tensor(nS[:, :, x, :], kin[j][:, x, :, C_SK - C_CK:C_SV - C_CK],
                                                rs[:, x, :, 0:1].broadcast_to([P, NPAGE, HD]), ALU.mult)
                    ins.then_inc(nS_done, 1)

                    norm_diff(p, 0)
                    for x in range(2):
                        ins = dve.tensor_tensor(nW[:, :, x, :], win[j][:, x, :, 0:HD],
                                                rw[:, x, :].unsqueeze(2).broadcast_to([P, NW, HD]), ALU.mult)
                    ins.then_inc(nW_done, 1)

                def compressed_keys(p):
                    i, j = p // 2, p % 2
                    dve.wait_ge(root_done, p * 3 + 3)
                    link(dve.reciprocal(kcr[:], kcr[:]))
                    dve.tensor_tensor(kc[:], kc[:], kcr[:].unsqueeze(2).broadcast_to([32, 2, HD]), ALU.mult).then_inc(kc_done, 1)
                    dve.wait_ge(kc_done, p * 3 + 2)
                    dve.tensor_tensor(kc[:], kc[:], g.gain[0:32, 1:2, :].broadcast_to([32, 2, HD]), ALU.mult).then_inc(kc_done, 1)

                def middle(p):
                    i, j = p // 2, p % 2
                    dve.wait_ge(s_full, p * 4 + 1)
                    link(dve.tensor_tensor(pC[:], ma[0:R, 288:320], tab[:, T_CMP:T_SN], ALU.add))
                    dve.tensor_reduce(st[:, 0:1], pC[:], AX.X, ALU.max, negate=True).then_inc(masked, 1)
                    dve.wait_ge(kt_full, p * NY + 6)
                    norm_diff(p, 1)
                    dve.wait_ge(exps, p * 4 + 1)
                    link(dve.reciprocal(st[:, 8:9], st[:, 4:5]))
                    dve.tensor_scalar(pC[:], pC[:], st[:, 8:9], None, ALU.mult).then_inc(pc_done, 1)
                    dve.wait_ge(imp_ps, p + 1)
                    link(dve.tensor_reduce(imp[:], ma[0:R, 324:356].rearrange("p (a b) -> p a b", b=2), AX.X, ALU.add))
                    link(dve.tensor_reduce(st[:, 9:10], imp[:, 1:16], AX.X, ALU.min))
                    link(dve.tensor_scalar(low[:, 1:16], imp[:, 1:16], st[:, 9:10], None, ALU.is_equal))
                    link(dve.tensor_tensor(low[:, 1:16], low[:, 1:16], tab[:, T_IDX:T_SUM], ALU.mult))
                    link(dve.tensor_reduce(st[:, 10:11], low[:, 1:16], AX.X, ALU.max))
                    link(dve.memset(low[:, 0:1], 0.0))
                    link(dve.tensor_scalar(low[:, 1:16], tab[:, T_IDX:T_SUM], st[:, 10:11], NEG, ALU.is_equal, ALU.mult))
                    dve.wait_ge(s_full, p * 4 + 2)
                    link(dve.tensor_tensor(pS[:, PAST:PAST + 1], ma[0:R, 320:321], tab[:, T_DIF - 1:T_DIF], ALU.add))
                    dve.tensor_tensor(pS[:, 0:PAST], ss[:], tab[:, T_SEL:T_DIF - 1], ALU.add).then_inc(ss_read, 1)
                    dve.wait_ge(ss_read, p + 1)
                    blk = pS[:, 0:PAST].rearrange("p (a b) -> p a b", b=HD)
                    link(dve.tensor_tensor(blk, blk, low[:].unsqueeze(2).broadcast_to([R, 16, HD]), ALU.add))
                    dve.tensor_reduce(st[:, 1:2], pS[:], AX.X, ALU.max, negate=True).then_inc(masked, 1)
                    dve.wait_ge(s_full, p * 4 + 3)
                    link(dve.tensor_tensor(pD[:, PAST:PAST + 1], ma[0:R, 322:323], tab[:, T_WIN - 1:T_WIN], ALU.add))
                    link(dve.tensor_tensor(pD[:, 0:PAST], sd[:], tab[:, T_DIF:T_WIN - 1], ALU.add))
                    dve.tensor_reduce(st[:, 2:3], pD[:], AX.X, ALU.max, negate=True).then_inc(masked, 1)
                    dve.wait_ge(s_full, p * 4 + 4)
                    link(dve.tensor_tensor(pW[:, WINDOW:WINDOW + 1], ma[0:R, 321:322], tab[:, T_CMP - 1:T_CMP], ALU.add))
                    link(dve.tensor_tensor(pW[:, 0:WINDOW], ss[:, 0:WINDOW], tab[:, T_WIN:T_CMP - 1], ALU.add))
                    dve.tensor_reduce(st[:, 3:4], pW, AX.X, ALU.max, negate=True).then_inc(masked, 1)

                def outputs(p):
                    i, j = p // 2, p % 2
                    dve.wait_ge(exps, p * 4 + 4)
                    link(dve.reciprocal(st[:, 11:14], st[:, 5:8]))
                    link(dve.tensor_tensor(st[:, 12:13], st[:, 12:13], coef[:], ALU.mult))
                    dve.wait_ge(vnew_in[j], i * 96 + 96)
                    dve.wait_ge(pv, p + 1)
                    if p:
                        dve.wait_ge(o_out, p * 16)

                    def add(o, a, sc, first=False):
                        if first:
                            link(dve.tensor_scalar(o, a, sc, None, ALU.mult))
                        else:
                            link(dve.scalar_tensor_tensor(out=o, in0=a, scalar=sc, in1=o, op0=ALU.mult, op1=ALU.add))

                    for b, c in enumerate((512, 640, 768)):
                        o = o16[:, b * HD:(b + 1) * HD]
                        for x in range(2):
                            add(o, sd[0:R, c + x * HD:c + (x + 1) * HD], tab[:, T_S + x:T_S + x + 1], x == 0)
                        if b < 2:
                            pn = pS[:, PAST:PAST + 1] if b == 0 else pW[:, WINDOW:WINDOW + 1]
                            add(o, vnew[j][:, b * HD:(b + 1) * HD], pn)
                            link(dve.tensor_scalar(o, o, st[:, 11 + 2 * b:12 + 2 * b], None, ALU.mult))
                    o = o16[:, 3 * HD:5 * HD]
                    for x in range(4):
                        add(o, sd[0:R, x * 2 * HD:(x + 1) * 2 * HD], tab[:, T_SN + x:T_SN + x + 1], x == 0)
                    for nn in range(2):
                        link(dve.tensor_tensor(st[:, 14 + nn:15 + nn], pD[:, PAST:PAST + 1], tab[:, T_N + nn:T_N + nn + 1], ALU.mult))
                        add(o, vnew[j][:, 2 * HD * (1 + nn):2 * HD * (2 + nn)], st[:, 14 + nn:15 + nn])
                    dve.tensor_scalar(o, o, st[:, 12:13], None, ALU.mult).then_inc(o_done, 1)
                    dve.sem_inc(slot_free, 1)

                front(0)
                compressed_keys(0)
                for p in range(NP):
                    middle(p)
                    if p + 1 < NP:
                        front(p + 1)
                        compressed_keys(p + 1)
                    outputs(p)

        with nc.Block() as block:
            od_in, chain3, root = s.sem("od_in"), s.sem("chain3"), s.sem("root")
            dsq = g.z[0:NDEC, TT, C_CK:C_CK + NDH * 2 * HD].rearrange("p (j v) -> p j v", j=NDH)

            @block.sync
            def _(sp):
                sp.dma_start(od, io["dec_d"].rearrange("(b r) c -> b r c", r=8)).then_inc(od_in, 16)

            @block.scalar
            def _(act):
                act.wait_ge(root, 1)
                act.activation(nrs[:, 0:NDH], nrs[:, 0:NDH], ACT.Sqrt).then_inc(root, 1)

            @block.vector
            def _(dve):
                n = [0]

                def link(ins):
                    n[0] += 1
                    ins.then_inc(chain3, 1)
                    dve.wait_ge(chain3, n[0])

                dve.wait_ge(od_in, 16)
                qo = g.z[0:NDEC, TT, C_QN:C_CK].rearrange("p (a b) -> p a b", b=HD)
                for b, gate in enumerate((1, 2, 0)):
                    gb = g.G[0:NDEC, TT, gate:24:3].unsqueeze(2).broadcast_to([NDEC, NH, HD])
                    part = od[:, :, b * HD:(b + 1) * HD]
                    if b == 0:
                        link(dve.tensor_tensor(qo, part, gb, ALU.mult))
                    else:
                        link(dve.tensor_tensor(part, part, gb, ALU.mult))
                        link(dve.tensor_tensor(qo, qo, part, ALU.add))
                do = g.z[0:NDEC, TT, C_QD:C_M].rearrange("p (j v) -> p j v", j=NDH)
                ov = od.rearrange("p (j m) c -> p j m c", m=2)
                link(dve.tensor_tensor(do, ov[:, :, 0, 3 * HD:5 * HD], ov[:, :, 1, 3 * HD:5 * HD], ALU.add))
                link(dve.tensor_tensor(dsq, do, do, ALU.mult))
                link(dve.tensor_reduce(nrs[:, 0:NDH], dsq, AX.X, ALU.add))
                dve.tensor_scalar(nrs[:, 0:NDH], nrs[:, 0:NDH], 1.0 / (2 * HD), EPS, ALU.mult, ALU.add).then_inc(root, 1)
                dve.wait_ge(root, 2)
                link(dve.reciprocal(nrs[:, 0:NDH], nrs[:, 0:NDH]))
                link(dve.tensor_tensor(do, do, nrs[:, 0:NDH].unsqueeze(2).broadcast_to([NDEC, NDH, 2 * HD]), ALU.mult))
                link(dve.tensor_tensor(do, do, g.subln[0:NDEC].unsqueeze(1).broadcast_to([NDEC, NDH, 2 * HD]), ALU.mult))


def transpose_branches(nc, io, g):
    KB = NH * HD // P
    with Scope(nc, "ot") as s:
        pt = [s.ps(f"pt{i}", [P, 512]) for i in range(6)]
        oT_ps, hi_done, split = s.sem("oT_ps"), s.sem("hi_done"), s.sem("split")
        cols = [C_QN + k * P for k in range(KB)] + [C_QD + k * P for k in range(KB)]
        NU = 4 * KB + 1
        with nc.Block() as block:

            @block.tensor
            def _(pe):
                for u in range(NU):
                    if u >= 6:
                        pe.wait_ge(split, u - 5)
                    if u < NU - 1:
                        for q in range(4):
                            mm = pe.transpose(pt[u % 6][:, q * P:(q + 1) * P], g.z[:, u % 2 * 4 + q, cols[u // 2]:cols[u // 2] + P], g.ident[:])
                    else:
                        for k in range(2 * KB):
                            mm = pe.transpose(pt[u % 6][:, k * NDEC:(k + 1) * NDEC], g.z[0:NDEC, TT, cols[k]:cols[k] + P],
                                              g.ident[0:NDEC, 0:NDEC])
                    mm.then_inc(oT_ps, 1)

            @block.vector
            def _(dve):
                for u in range(NU):
                    dve.wait_ge(oT_ps, u + 1)
                    if u < NU - 1:
                        half = slice(u % 2 * 512, u % 2 * 512 + 512)
                        src, hi, lo = pt[u % 6][:], g.oT_hi[:, u // 2, half], g.oT_lo[:, u // 2, half]
                    else:
                        src = pt[u % 6][:, 0:2 * KB * NDEC].rearrange("p (k t) -> p k t", k=2 * KB)
                        hi, lo = g.oT_hi[:, :, SEQ:NTOK], g.oT_lo[:, :, SEQ:NTOK]
                    dve.tensor_copy(hi, src).then_inc(hi_done, 1)
                    dve.wait_ge(hi_done, u + 1)
                    dve.tensor_tensor(lo, src, f32(hi), ALU.subtract).then_inc(split, 1)


def merge_branches(nc, io, g):
    KB = NH * HD // P
    with Scope(nc, "br") as s:
        raw = [s.sb(f"raw{i}", [P, 2 * KB, P]) for i in range(2)]
        whi = [s.sb(f"whi{i}", [P, 2 * KB, P], F32R) for i in range(2)]
        wlo = [s.sb(f"wlo{i}", [P, 2 * KB, P], F32R) for i in range(2)]
        late = g.x2[:].rearrange("p t d -> p (t d)")
        gate = [late[:, i * 2 * NTOK:(i + 1) * 2 * NTOK].rearrange("p (b t) -> p b t", b=2) for i in range(2)]
        acc = [s.ps(f"acc{i}", [P, 512]) for i in range(6)]
        m_hi, m_lo = g.words_hi, g.words_lo
        w_in, gate_in = [s.sem(f"w_in{i}") for i in range(2)], [s.sem(f"gate_in{i}") for i in range(2)]
        raw_free, w_hi, w_lo, w_free = s.sem("raw_free"), s.sem("w_hi"), s.sem("w_lo"), s.sem("w_free")
        gate_free = s.sem("gate_free")
        acc_full, prod, merged, m_hi_done, m_split = (s.sem(x) for x in ("acc_full", "prod", "merged", "m_hi_done", "m_split"))
        w_a = io["w_br_nsa"][0].rearrange("(k p) n -> p k n", p=P)
        w_b = io["w_br_diff"][0].rearrange("(k p) n -> p k n", p=P)
        gate_v = io["gate_d"].rearrange("(b r) t -> r b t", b=2)
        with nc.Block() as block:

            @block.sync
            def _(sp):
                with sp.Fori(0, KD // 2) as i:
                    for j in range(2):
                        n = i * 2 + j
                        sp.wait_ge(raw_free, n + 1)
                        sp.dma_start(raw[j][:, 0:KB, :], w_a[:, :, ds(n * P, P)]).then_inc(w_in[j], 16)
                        sp.dma_start(raw[j][:, KB:2 * KB, :], w_b[:, :, ds(n * P, P)]).then_inc(w_in[j], 16)
                        sp.wait_ge(gate_free, n + 1)
                        sp.dma_start(gate[j], gate_v[ds(n * P, P), :, :]).then_inc(gate_in[j], 16)

            @block.tensor
            def _(pe):
                with pe.Fori(0, KD // 2) as i:
                    for j in range(2):
                        n = i * 2 + j
                        pe.wait_ge(w_lo, n + 1)
                        for c in range(3):
                            tok = slice(c * TCH, (c + 1) * TCH)
                            pe.wait_ge(prod, n * 6 + c * 2 + 2)
                            for b in range(2):
                                for k in range(b * KB, (b + 1) * KB):
                                    for q, (w, o) in enumerate(((whi, g.oT_hi), (wlo, g.oT_hi), (whi, g.oT_lo))):
                                        mm = pe.matmul(acc[c * 2 + b][:, 0:TCH], w[j][:, k, :], o[:, k, tok],
                                                       start=(k == b * KB and q == 0), stop=(k == (b + 1) * KB - 1 and q == 2))
                                mm.then_inc(acc_full, 1)
                        pe.wait_ge(acc_full, n * 6 + 6)
                        pe.sem_inc(w_free, 1)

            @block.vector
            def _(dve):
                dve.sem_inc(raw_free, 2)
                dve.sem_inc(gate_free, 2)
                dve.sem_inc(prod, 6)
                dve.sem_inc(w_free, 2)

                def split_weights(n, j, round):
                    dve.wait_ge(w_in[j], round * 32 + 32)
                    dve.wait_ge(w_free, n + 1)
                    dve.tensor_copy(whi[j][:], raw[j][:]).then_inc(w_hi, 1)
                    dve.wait_ge(w_hi, n + 1)
                    dve.tensor_tensor(wlo[j][:], raw[j][:], f32(whi[j][:]), ALU.subtract).then_inc(w_lo, 1)
                    dve.wait_ge(w_lo, n + 1)
                    dve.sem_inc(raw_free, 1)

                def merge(n, j, round, more=True):
                    if more:
                        split_weights(n + 1, 1 - j, round + j)
                    dve.wait_ge(gate_in[j], round * 16 + 16)
                    for c in range(3):
                        tok = slice(c * TCH, (c + 1) * TCH)
                        for b in range(2):
                            dve.wait_ge(acc_full, n * 6 + c * 2 + b + 1)
                            gt = gate[j][:, b, tok]
                            dve.tensor_tensor(gt, acc[c * 2 + b][:, 0:TCH], gt, ALU.mult).then_inc(prod, 1)
                    dve.wait_ge(prod, n * 6 + 12)
                    row = (lambda a: a[:, n, :]) if isinstance(n, int) else (lambda a: a[:, ds(n, 1), :].rearrange("p a t -> p (a t)"))
                    hi, lo = row(m_hi), row(m_lo)
                    dve.tensor_tensor(hi, gate[j][:, 0, :], gate[j][:, 1, :], ALU.add).then_inc(m_hi_done, 1)
                    dve.wait_ge(m_hi_done, n + 1)
                    dve.tensor_tensor(gate[j][:, 0, :], gate[j][:, 0, :], gate[j][:, 1, :], ALU.add).then_inc(merged, 1)
                    dve.wait_ge(merged, n + 1)
                    dve.tensor_tensor(lo, gate[j][:, 0, :], f32(hi), ALU.subtract).then_inc(m_split, 1)
                    dve.wait_ge(m_split, n + 1)
                    dve.sem_inc(gate_free, 1)

                split_weights(0, 0, 0)
                with dve.Fori(0, KD // 2 - 1) as i:
                    merge(i * 2, 0, i)
                    merge(i * 2 + 1, 1, i)
                merge(KD - 2, 0, KD // 2 - 1)
                merge(KD - 1, 1, KD // 2 - 1, more=False)


def output_and_norm(nc, io, g):
    NU = TT + 1
    with Scope(nc, "out") as s:
        raw = [s.sb(f"raw{i}", [P, KD, 256]) for i in range(2)]
        whi = [s.sb(f"whi{i}", [P, KD, 512], F32R) for i in range(2)]
        wlo = [s.sb(f"wlo{i}", [P, KD, 512], F32R) for i in range(2)]
        ga = s.sb("ga", [P, D])
        gs = s.sb("gs", [NDEC, D])
        tmp = [s.sb(f"tmp{i}", [P, 512]) for i in range(2)]
        hf = [s.sb(f"hf{i}", [P, 512]) for i in range(2)]
        junk = raw[0][:, 0:4, :].rearrange("p a b -> p (a b)")
        ssq = s.sb("ssq", [P, NU])
        rstd = s.sb("rstd", [P, NU])
        aT = s.sb("aT", [P, KD, NC9])
        hs = s.sb("hs", [P, KD, NDEC])
        acc = [s.ps(f"acc{i}", [P, 512]) for i in range(4)]
        pt = [s.ps(f"pt{i}", [P, 512]) for i in range(3)]
        pc = s.ps("pc", [P, KD, NDEC])
        h_hi, h_lo = g.words_hi, g.words_lo
        w_in, x_in, ga_in = [s.sem(f"w_in{i}") for i in range(4)], s.pool_sem("x_in"), s.sem("ga_in")
        w_hi, w_lo, acc_full, acc_free, scaled = (s.sem(x) for x in ("w_hi", "w_lo", "acc_full", "acc_free", "scaled"))
        x2_ready, ss0, sq, mean, root, xn = (s.sem(x) for x in ("x2_ready", "ss0", "sq", "mean", "root", "xn"))
        x2_out = [s.sem(f"x2_out{n}") for n in range(NU)]
        rs_done = s.sem("rs_done")
        h_ps, h_sb, h_hi_done, h_split, coef, hs_ps = (s.sem(x) for x in ("h_ps", "h_sb", "h_hi_done", "h_split", "coef", "hs_ps"))
        w = io["w_out"][0].rearrange("(k p) n -> p k n", p=P)
        x_v = io["x_prompt"][0].rearrange("(t p) d -> p t d", p=P)
        x2_v = io["x2_d"].rearrange("(t p) d -> p t d", p=P)
        order = [0, 1, 2, 3, 4, 5, "half 0", 6, 7, TT, "half 1", "decode"]
        tiles = [t for t in order if isinstance(t, int)]
        rows = lambda t: P if t < TT else NDEC
        with nc.Block() as block:

            @block.sync
            def _(sp):
                for i in range(4):
                    if i >= 2:
                        sp.wait_ge(w_lo, i - 1)
                    sp.dma_start(raw[i % 2][:], w[:, :, i * 256:(i + 1) * 256]).then_inc(w_in[i], 16)
                sp.dma_start(ga[:], io["mod_d"][NDEC:NC9, 2 * D:3 * D].broadcast_to([P, D])).then_inc(ga_in, 16)
                sp.dma_start(gs[:], io["mod_d"][0:NDEC, 2 * D:3 * D]).then_inc(ga_in, 16)
                for n, t in enumerate(tiles):
                    sp.wait_ge(x2_ready, n + 1)
                    r = rows(t)
                    sp.dma_start(x2_v[:, t, :] if t < TT else io["x2s_d"], g.x2[0:r, t, :]).then_inc(x2_out[n], 16)
                for n in range(NU):
                    sp.wait_ge(x2_out[n], 16)

            @block.gpsimd
            def _(pool):
                pool.dma_start(g.x2[:, 0:TT, :], x_v).then_inc(x_in, 16)
                pool.dma_start(g.x2[0:NDEC, TT, :], io["x_sample"].rearrange("b t d -> (b t) d")).then_inc(x_in, 16)

            @block.scalar
            def _(act):
                n = 0
                for t in order:
                    if isinstance(t, int):
                        r = rows(t)
                        act.wait_ge(x2_ready, n + 1)
                        if n == 0:
                            act.wait_ge(ss0, 1)
                            act.wait_ge(w_lo, 4)
                        else:
                            act.wait_ge(sq, n)
                        act.activation(junk[0:r], g.x2[0:r, t, :], ACT.Square, accum_out=ssq[0:r, t:t + 1]).then_inc(sq, 1)
                        act.wait_ge(mean, n + 1)
                        act.activation(rstd[0:r, t:t + 1], rstd[0:r, t:t + 1], ACT.Sqrt).then_inc(root, 1)
                        n += 1
                    elif t != "decode":
                        for k in range(KD):
                            u = int(t[-1]) * KD + k
                            act.wait_ge(h_ps, u + 1)
                            act.wait_ge(coef, 1)
                            if u >= 2:
                                act.wait_ge(h_split, u - 1)
                            act.activation(hf[u % 2][:], pt[u % 3][:], ACT.Identity, bias=g.modT[:, 3 * KD + k, NDEC:NC9],
                                           scale=aT[:, k, NDEC:NC9]).then_inc(h_sb, 1)

            @block.tensor
            def _(pe):
                pe.wait_ge(w_lo, 2)
                n = 0
                for t in order:
                    if isinstance(t, int):
                        r = rows(t)
                        tok = slice(t * P, t * P + r)
                        for c in range(2):
                            u = n * 2 + c
                            if u == 1:
                                pe.wait_ge(w_lo, 4)
                            if u >= 4:
                                pe.wait_ge(acc_free, u - 3)
                            for k in range(KD):
                                for q, (a, b) in enumerate(((h_hi, whi), (h_lo, whi), (h_hi, wlo))):
                                    mm = pe.matmul(acc[u % 4][0:r, :], a[:, k, tok], b[c][:, k, :],
                                                   start=(k == 0 and q == 0), stop=(k == KD - 1 and q == 2))
                            mm.then_inc(acc_full, 1)
                        n += 1
                    elif t == "decode":
                        for k in range(KD):
                            mm = pe.transpose(pc[:, k, :], g.x2[0:NDEC, TT, k * P:(k + 1) * P], g.ident[0:NDEC, 0:NDEC])
                        mm.then_inc(hs_ps, 1)
                    else:
                        half = int(t[-1])
                        pe.wait_ge(xn, 4 if half == 0 else NU)
                        for k in range(KD):
                            u = half * KD + k
                            if u >= 3:
                                pe.wait_ge(h_sb, u - 2)
                            for q in range(4):
                                mm = pe.transpose(pt[u % 3][:, q * P:(q + 1) * P], g.x2[:, half * 4 + q, k * P:(k + 1) * P], g.ident[:])
                            mm.then_inc(h_ps, 1)

            @block.vector
            def _(dve):
                dve.memset(ssq[:], 0.0).then_inc(ss0, 1)
                dve.scalar_tensor_tensor(out=aT[:], in0=g.modT[:, 4 * KD:5 * KD, :], scalar=1.0,
                                         in1=g.gT[:, KD:2 * KD].unsqueeze(2).broadcast_to([P, KD, NC9]), op0=ALU.add, op1=ALU.mult).then_inc(coef, 1)
                for i in range(4):
                    hi, lo = (w[i // 2][:, :, i % 2 * 256:i % 2 * 256 + 256] for w in (whi, wlo))
                    dve.wait_ge(w_in[i], 16)
                    dve.tensor_copy(hi, raw[i % 2][:]).then_inc(w_hi, 1)
                    dve.wait_ge(w_hi, i + 1)
                    dve.tensor_tensor(lo, raw[i % 2][:], f32(hi), ALU.subtract).then_inc(w_lo, 1)
                dve.wait_ge(ga_in, 32)
                dve.wait_ge(x_in, 32)

                def normalise(m, t):
                    r = rows(t)
                    one = rstd[0:r, t:t + 1]
                    dve.wait_ge(sq, m + 1)
                    dve.tensor_scalar(one, ssq[0:r, t:t + 1], 1.0 / D, EPS, ALU.mult, ALU.add).then_inc(mean, 1)
                    dve.wait_ge(root, m + 1)
                    dve.reciprocal(one, one).then_inc(rs_done, 1)
                    dve.wait_ge(rs_done, m + 1)
                    dve.wait_ge(x2_out[m], 16)
                    dve.tensor_scalar(g.x2[0:r, t, :], g.x2[0:r, t, :], one, None, ALU.mult).then_inc(xn, 1)

                n = 0
                for t in order:
                    if isinstance(t, int):
                        r = rows(t)
                        for c in range(2):
                            u = n * 2 + c
                            cs = slice(c * 512, (c + 1) * 512)
                            gate = ga if t < TT else gs
                            dve.wait_ge(acc_full, u + 1)
                            dve.tensor_tensor(tmp[c][0:r], acc[u % 4][0:r, :], gate[0:r, cs], ALU.mult).then_inc(acc_free, 1)
                            dve.wait_ge(acc_free, u + 1)
                            dve.tensor_tensor(g.x2[0:r, t, cs], g.x2[0:r, t, cs], tmp[c][0:r], ALU.add).then_inc(scaled, 1)
                        dve.wait_ge(scaled, n * 2 + 2)
                        dve.sem_inc(x2_ready, 1)
                        if n and n != 6:
                            normalise(n - 1, tiles[n - 1])
                        if n in (5, TT):
                            normalise(n, t)
                        n += 1
                    elif t == "decode":
                        dve.wait_ge(hs_ps, 1)
                        dve.tensor_tensor(hs[:], pc[:], aT[:, :, 0:NDEC], ALU.mult).then_inc(coef, 1)
                        dve.wait_ge(coef, 2)
                        dve.tensor_tensor(hs[:], hs[:], g.modT[:, 3 * KD:4 * KD, 0:NDEC], ALU.add).then_inc(coef, 1)
                        dve.wait_ge(coef, 3)
                        dve.tensor_copy(h_hi[:, :, SEQ:NTOK], hs[:]).then_inc(coef, 1)
                        dve.wait_ge(coef, 4)
                        dve.tensor_tensor(h_lo[:, :, SEQ:NTOK], hs[:], f32(h_hi[:, :, SEQ:NTOK]), ALU.subtract).then_inc(coef, 1)
                    else:
                        half = int(t[-1])
                        for k in range(KD):
                            u = half * KD + k
                            dve.wait_ge(h_sb, u + 1)
                            hi = h_hi[:, k, half * 512:(half + 1) * 512]
                            lo = h_lo[:, k, half * 512:(half + 1) * 512]
                            dve.tensor_copy(hi, hf[u % 2][:]).then_inc(h_hi_done, 1)
                            dve.wait_ge(h_hi_done, u + 1)
                            dve.tensor_tensor(lo, hf[u % 2][:], f32(hi), ALU.subtract).then_inc(h_split, 1)


def feed_forward(nc, io, g):
    NF = D_FF // P
    NU = TT + 1
    NO = 2 * NU
    with Scope(nc, "ffn") as s:
        raw_u = [s.sb(f"raw_u{i}", [P, 2 * KD, P]) for i in range(2)]
        uhi = [s.sb(f"uhi{i}", [P, 2 * KD, P], F32R) for i in range(2)]
        ulo = [s.sb(f"ulo{i}", [P, 2 * KD, P], F32R) for i in range(2)]
        raw_o = [s.sb(f"raw_o{i}", [P, D]) for i in range(2)]
        ohi = [s.sb(f"ohi{i}", [P, D], F32R) for i in range(2)]
        olo = [s.sb(f"olo{i}", [P, D], F32R) for i in range(2)]
        sg = [s.sb(f"sg{i}", [P, TCH]) for i in range(2)]
        av = [s.sb(f"av{i}", [P, TCH]) for i in range(2)]
        a_hi = [s.sb(f"a_hi{i}", [P, NTOK], F32R) for i in range(2)]
        a_lo = [s.sb(f"a_lo{i}", [P, NTOK], F32R) for i in range(2)]
        ga, gs = raw_o[0], raw_o[1]
        xr = [raw_u[i // 2][:, i % 2 * KD:(i % 2 + 1) * KD, :].rearrange("p k n -> p (k n)") for i in range(4)]
        total = g.x2
        pg = [s.ps(f"pg{i}", [P, 512]) for i in range(2)]
        pv = [s.ps(f"pv{i}", [P, 512]) for i in range(2)]
        po = [s.ps(f"po{i}", [P, 512]) for i in range(4)]
        h_hi, h_lo = g.words_hi, g.words_lo
        u_in, o_in = [s.sem(f"u_in{i}") for i in range(2)], [s.sem(f"o_in{i}") for i in range(2)]
        raw_u_free, raw_o_free, u_hi_done, u_ready, o_hi_done, o_ready = (
            s.sem(x) for x in ("raw_u_free", "raw_o_free", "u_hi_done", "u_ready", "o_hi_done", "o_ready"))
        gate_full, val_full, silu_done, a_done, a_hi_done, a_ready = (
            s.sem(x) for x in ("gate_full", "val_full", "silu_done", "a_done", "a_hi_done", "a_ready"))
        o_full, o_read, ga_in = s.sem("o_full"), s.sem("o_read"), s.pool_sem("ga_in")
        xr_in = [s.pool_sem(f"xr_in{t}") for t in range(NU)]
        tot0, y1, y_ready, y_out = s.sem("tot0"), s.sem("y1"), s.sem("y_ready"), s.sem("y_out")
        w_u = io["w_ffn_in"][0].rearrange("(k p) n -> p k n", p=P)
        w_o = io["w_ffn_out"][0]
        x2_v = io["x2_d"].rearrange("(t p) d -> p t d", p=P)
        y_v = io["y_p"][0].rearrange("(t p) d -> p t d", p=P)
        rows = lambda t: P if t < TT else NDEC
        with nc.Block() as block:

            @block.sync
            def _(sp):
                with sp.Fori(0, NF // 2) as i:
                    for j in range(2):
                        f = i * 2 + j
                        sp.wait_ge(raw_u_free, f + 1)
                        sp.dma_start(raw_u[j][:, 0:KD, :], w_u[:, :, ds(f * P, P)]).then_inc(u_in[j], 16)
                        sp.dma_start(raw_u[j][:, KD:2 * KD, :], w_u[:, :, ds(f * P + D_FF, P)]).then_inc(u_in[j], 16)
                        sp.wait_ge(raw_o_free, f + 1)
                        sp.dma_start(raw_o[j][:], w_o[ds(f * P, P), :]).then_inc(o_in[j], 16)
                for t in range(NU):
                    r = rows(t)
                    sp.wait_ge(y_ready, t + 1)
                    sp.dma_start(y_v[:, t, :] if t < TT else io["y_s"].rearrange("b t d -> (b t) d"),
                                 total[0:r, t, :]).then_inc(y_out, 16)
                sp.wait_ge(y_out, 16 * NU)

            @block.gpsimd
            def _(pool):
                pool.wait_ge(o_ready, NF)
                pool.dma_start(ga[:], io["mod_d"][NDEC:NC9, 5 * D:6 * D].broadcast_to([P, D])).then_inc(ga_in, 16)
                pool.dma_start(gs[0:NDEC, :], io["mod_d"][0:NDEC, 5 * D:6 * D]).then_inc(ga_in, 16)
                pool.wait_ge(u_ready, NF)
                for t in range(NU):
                    r = rows(t)
                    if t >= 4:
                        pool.wait_ge(y_ready, t - 3)
                    pool.dma_start(xr[t % 4][0:r], x2_v[:, t, :] if t < TT else io["x2s_d"]).then_inc(xr_in[t], 16)

            @block.scalar
            def _(act):
                with act.Fori(0, NF // 2) as i:
                    for j in range(2):
                        for c in range(3):
                            n = (i * 2 + j) * 3 + c
                            act.wait_ge(gate_full, n + 1)
                            act.wait_ge(a_done, n + 1)
                            act.activation(sg[(j + c) % 2][:], pg[(j + c) % 2][:, 0:TCH], ACT.Silu).then_inc(silu_done, 1)

            def hidden(pe, f, j):
                pe.wait_ge(u_ready, f + 1)
                for c in range(3):
                    n = f * 3 + c
                    b = (j + c) % 2
                    tok = slice(c * TCH, (c + 1) * TCH)
                    pe.wait_ge(a_done, n + 1)
                    for v, (bank, full) in enumerate(((pg, gate_full), (pv, val_full))):
                        for k in range(KD):
                            for q, (w, h) in enumerate(((uhi, h_hi), (ulo, h_hi), (uhi, h_lo))):
                                mm = pe.matmul(bank[b][:, 0:TCH], w[j][:, v * KD + k, :], h[:, k, tok],
                                               start=(k == 0 and q == 0), stop=(k == KD - 1 and q == 2))
                        mm.then_inc(full, 1)

            def output(pe, f, j):
                pe.wait_ge(o_ready, f + 1)
                pe.wait_ge(a_ready, f * 3 + 3)
                for t in range(NU):
                    r = rows(t)
                    tok = slice(t * P, t * P + r)
                    for c in range(2):
                        u = t * 2 + c
                        cs = slice(c * 512, (c + 1) * 512)
                        pe.wait_ge(o_read, f * NO + u + 1)
                        for q, (a, w) in enumerate(((a_hi, ohi), (a_lo, ohi), (a_hi, olo))):
                            mm = pe.matmul(po[(j * NO + u) % 4][0:r, :], a[j][:, tok], w[j][:, cs], start=(q == 0), stop=(q == 2))
                        mm.then_inc(o_full, 1)

            @block.tensor
            def _(pe):
                hidden(pe, 0, 0)
                with pe.Fori(0, NF // 2 - 1) as i:
                    hidden(pe, i * 2 + 1, 1)
                    output(pe, i * 2, 0)
                    hidden(pe, i * 2 + 2, 0)
                    output(pe, i * 2 + 1, 1)
                hidden(pe, NF - 1, 1)
                output(pe, NF - 2, 0)
                output(pe, NF - 1, 1)

            def split_hidden(dve, f, j):
                dve.wait_ge(u_in[j], (f - j) * 16 + 32)
                dve.tensor_copy(uhi[j][:], raw_u[j][:]).then_inc(u_hi_done, 1)
                dve.wait_ge(u_hi_done, f + 1)
                dve.tensor_tensor(ulo[j][:], raw_u[j][:], f32(uhi[j][:]), ALU.subtract).then_inc(u_ready, 1)
                dve.wait_ge(u_ready, f + 1)
                dve.sem_inc(raw_u_free, 1)

            def split_output(dve, f, j):
                dve.wait_ge(o_in[j], (f - j) * 8 + 16)
                dve.tensor_copy(ohi[j][:], raw_o[j][:]).then_inc(o_hi_done, 1)
                dve.wait_ge(o_hi_done, f + 1)
                dve.tensor_tensor(olo[j][:], raw_o[j][:], f32(ohi[j][:]), ALU.subtract).then_inc(o_ready, 1)
                dve.wait_ge(o_ready, f + 1)
                dve.sem_inc(raw_o_free, 1)

            def gated(dve, f, j):
                for c in range(3):
                    n = f * 3 + c
                    b = (j + c) % 2
                    tok = slice(c * TCH, (c + 1) * TCH)
                    dve.wait_ge(silu_done, n + 1)
                    dve.wait_ge(val_full, n + 1)
                    dve.tensor_tensor(av[b][:], pv[b][:, 0:TCH], sg[b][:], ALU.mult).then_inc(a_done, 1)
                    dve.wait_ge(a_done, n + 3)
                    dve.tensor_copy(a_hi[j][:, tok], av[b][:]).then_inc(a_hi_done, 1)
                    dve.wait_ge(a_hi_done, n + 1)
                    dve.tensor_tensor(a_lo[j][:, tok], av[b][:], f32(a_hi[j][:, tok]), ALU.subtract).then_inc(a_ready, 1)

            def accumulate(dve, f, j, last=False):
                for t in range(NU):
                    r = rows(t)
                    for c in range(2):
                        u = t * 2 + c
                        part = total[0:r, t, c * 512:(c + 1) * 512]
                        dve.wait_ge(o_full, f * NO + u + 1)
                        dve.tensor_tensor(part, part, po[(j * NO + u) % 4][0:r, :], ALU.add).then_inc(o_read, 1)
                    if last:
                        gate = ga if t < TT else gs
                        dve.wait_ge(o_read, f * NO + t * 2 + 6)
                        dve.tensor_tensor(total[0:r, t, :], total[0:r, t, :], gate[0:r, :], ALU.mult).then_inc(y1, 1)
                        dve.wait_ge(y1, t + 1)
                        dve.wait_ge(xr_in[t], 16)
                        dve.tensor_tensor(total[0:r, t, :], total[0:r, t, :], xr[t % 4][0:r], ALU.add).then_inc(y_ready, 1)

            @block.vector
            def _(dve):
                dve.sem_inc(raw_u_free, 2)
                dve.sem_inc(raw_o_free, 2)
                dve.sem_inc(a_done, 2)
                dve.sem_inc(o_read, 4)
                split_hidden(dve, 0, 0)
                split_hidden(dve, 1, 1)
                dve.memset(total[:], 0.0).then_inc(tot0, 1)
                split_output(dve, 0, 0)
                gated(dve, 0, 0)
                dve.wait_ge(tot0, 1)
                with dve.Fori(0, NF // 2 - 1) as i:
                    for j in range(2):
                        f = i * 2 + j
                        dve.wait_ge(val_full, f * 3 + 3)
                        split_hidden(dve, f + 2, j)
                        split_output(dve, f + 1, 1 - j)
                        gated(dve, f + 1, 1 - j)
                        accumulate(dve, f, j)
                split_output(dve, NF - 1, 1)
                gated(dve, NF - 1, 1)
                accumulate(dve, NF - 2, 0)
                dve.wait_ge(ga_in, 32)
                accumulate(dve, NF - 1, 1, last=True)


class Globals:
    pass


def trunk_step(nc, io):
    g = Globals()
    Scope.cleared = []
    with Scope(nc, "g") as s:
        g.ident = s.sb("ident", [P, P])
        g.modT = s.sb("modT", [P, 6 * KD, NC9])
        g.gT = s.sb("gT", [P, 16])
        g.const_ready = s.sem("const_ready")
        z0 = s.sem("z0")
        zs = Scope(nc, "zs")
        g.z = zs.sb("z", [P, TT + 1, ZW], side="right")
        with nc.Block() as block:

            @block.gpsimd
            def _(pool):
                pool.memset(g.ident[:], 0.0).then_inc(g.const_ready, 1)
                pool.wait_ge(g.const_ready, 1)
                pool.affine_select(out=g.ident[:], in_=g.ident[:], compare_op=ALU.not_equal, fill=1.0, base=0,
                                   pattern=[[-1, P]], channel_multiplier=1).then_inc(g.const_ready, 1)
        with Scope(nc, "h") as h:
            g.hT_hi = h.sb("hT_hi", [P, KD, NTOK], F32R)
            g.hT_lo = h.sb("hT_lo", [P, KD, NTOK], F32R)
            modulation_and_h(nc, io, g)
            project_token_major(nc, io, g)
            merge_gates(nc, io, g)
        store_new_rows(nc, io, g)
        with Scope(nc, "a") as a:
            attention_tiles(g, a)
            with Scope(nc, "at") as at:
                constants(nc, io, g, at)
                prepare_keys(nc, io, g, at)
                nsa_attention(nc, io, g)
                diff_attention(nc, io, g)
            decode_attention(nc, io, g)
        with Scope(nc, "late") as late:
            g.x2 = late.sb("x2", [P, TT + 1, D])
            with Scope(nc, "oT") as o:
                g.oT_hi = o.sb("hi", [P, KD, NTOK], F32R)
                g.oT_lo = o.sb("lo", [P, KD, NTOK], F32R)
                transpose_branches(nc, io, g)
                zs.__exit__(None, None, None)
                g.words_hi = late.sb("words_hi", [P, KD, NTOK], F32R, side="right")
                g.words_lo = late.sb("words_lo", [P, KD, NTOK], F32R, side="right")
                merge_branches(nc, io, g)
            output_and_norm(nc, io, g)
            feed_forward(nc, io, g)


_OUTS = [("y_p", (1, SEQ, D)), ("y_s", (NDEC, 1, D)), ("kv_p", (1, 1, SEQ, CACHE_W)),
         ("kv_s", (1, NDEC, 1, CACHE_W)), ("win_p", (1, 1, WINDOW, 128)), ("win_s", (1, NDEC, WINDOW, 128))]
_SCRATCH = [("mod_d", (NC9, 6 * D)), ("gate_d", (MC, NTOK)), ("x2_d", (SEQ, D)), ("x2s_d", (NDEC, D)), ("new_d", (NDEC, C_G - C_CK)), ("dec_d", (NDEC * 8, 5 * HD))]


def kernel(**inputs):
    import numpy as _np
    import concourse.bacc as _bacc
    from concourse.bass_utils import run_bass_kernel_spmd as _run

    nc = _bacc.Bacc("TRN2", target_bir_lowering=False, num_devices=1)
    arrays, io = {}, {}
    for name, a in inputs.items():
        a = _np.ascontiguousarray(a)
        arrays[f"in_{name}"] = a
        io[name] = nc.dram_tensor(f"in_{name}", a.shape, mybir.dt.from_np(a.dtype), kind="ExternalInput").ap()
    arrays["in_dec_tab"] = decode_table()
    io["dec_tab"] = nc.dram_tensor("in_dec_tab", (16, T_END), F32, kind="ExternalInput").ap()
    for name, shape in _OUTS:
        io[name] = nc.dram_tensor(f"out_{name}", shape, F32, kind="ExternalOutput").ap()
    for name, shape in _SCRATCH:
        io[name] = nc.dram_tensor(name, shape, F32).ap()
    trunk_step(nc, io)
    r = _run(nc, [arrays], core_ids=[0])
    return tuple(r.results[0][f"out_{name}"] for name, _ in _OUTS)
```

```python
from contextlib import ExitStack

import numpy as np
import concourse.bass as bass
from concourse import mybir

F32 = mybir.dt.float32
F32R = mybir.dt.float32r
I32 = mybir.dt.int32
ALU = mybir.AluOpType
ACT = mybir.ActivationFunctionType
AX = mybir.AxisListType
ds = bass.ds

P = 128
D = 1024
KD = D // P
SEQ = 1024
TT = SEQ // P
NDEC = 8
NTOK = SEQ + NDEC
NC9 = NDEC + 1
HD = 64
NH = 8
NDH = 4
WINDOW = 512
PAST = 1024
PAGE = 128
NPAGE = PAST // PAGE
D_FF = 2816
EPS = 1e-6
NEG = -1e30
LAM_INIT = 0.8 - 0.6 * 1.0

C_QN, C_CK, C_CV, C_SK, C_SV, C_DK, C_DV, C_WK, C_WV, C_G, C_QD, C_M = np.cumsum(
    [0, 512, 64, 64, 64, 64, 256, 256, 64, 64, 24, 512]).tolist()
ZW = C_M
CACHE_W = 768
ZCH = 324
NZCH = ZW // ZCH
MC = 2 * D
TCH = NTOK // 3
assert ZCH * NZCH == ZW and TCH * 3 == NTOK
MODC = 512
NMOD = 6 * D // MODC


class Scope:

    cleared = []

    def __init__(self, nc, tag, side="left"):
        self.nc, self.tag, self.stack, self.sems, self.side = nc, tag, ExitStack(), [], side

    def __enter__(self):
        return self

    def __exit__(self, *a):
        if self.sems and a[0] is None:
            for x in Scope.cleared:
                self.nc.release_semaphore(x)
            for x in self.sems:
                self.nc.gpsimd.sem_clear(x)
            Scope.cleared = self.sems
        return self.stack.__exit__(*a)

    def sb(self, name, shape, dt=F32, side=None):
        return self.stack.enter_context(self.nc.sbuf_tensor(f"{self.tag}_{name}", shape, dt, side=side or self.side))

    def ps(self, name, shape, dt=F32):
        return self.stack.enter_context(self.nc.psum_tensor(f"{self.tag}_{name}", shape, dt))

    def sem(self, name):
        self.sems.append(self.nc.alloc_semaphore(f"{self.tag}_{name}"))
        return self.sems[-1]

    def pool_sem(self, name):
        return self.nc.alloc_semaphore(f"{self.tag}_{name}")


def f32(ap):
    return ap.bitcast(F32)


def modulation_and_h(nc, io, g):
    with Scope(nc, "mod") as s:
        spare = g.z[:].rearrange("p t c -> p (t c)")
        wr = [spare[:, i * KD * MODC:(i + 1) * KD * MODC].rearrange("p (k n) -> p k n", k=KD) for i in range(3)]
        c9 = s.sb("c9", [NC9, D])
        cT = s.sb("cT", [P, KD, NC9])
        mod = s.sb("mod", [NC9, 6 * D])
        x = s.sb("x", [P, TT, D])
        xs = s.sb("xs", [NDEC, D])
        junk = spare[:, 3 * KD * MODC:3 * KD * MODC + D]
        ssq = s.sb("ssq", [P, TT + 1])
        rstd = s.sb("rstd", [P, TT + 1])
        gains = s.sb("gains", [16, P])
        hf = [s.sb(f"hf{i}", [P, 512]) for i in range(2)]
        aT = s.sb("aT", [P, KD, NC9])
        hs = s.sb("hs", [P, KD, NDEC])
        pc = s.ps("pc", [P, KD, NC9])
        pm = [s.ps(f"pm{i}", [NC9, MODC]) for i in range(3)]
        pt = [s.ps(f"pt{i}", [P, 512]) for i in range(3)]
        pq = s.ps("pq", [P, 4 * NC9])
        c_in, w_in, x_in, xs_in = s.sem("c_in"), [s.sem(f"w_in{i}") for i in range(3)], [s.pool_sem(f"x_in{t}") for t in range(TT)], s.pool_sem("xs_in")
        silu_done, cT_ps, cT_done = s.sem("silu"), s.sem("cT_ps"), s.sem("cT_done")
        mod_ps, mod_sb, modT_ps, modT_sb = (s.sem(n) for n in ("mod_ps", "mod_sb", "modT_ps", "modT_sb"))
        mod_out = s.pool_sem("mod_out")
        sq_done, std_done, rstd_done, xn_done = (s.sem(n) for n in ("sq", "std", "rstd", "xn"))
        coef, h_ps, h_sb, h_split, hs_ps, hs_st, g_ps = (s.sem(n) for n in ("coef", "h_ps", "h_sb", "h_split", "hs_ps", "hs_st", "g_ps"))
        ss0 = s.sem("ssq0")
        w_ada = io["w_ada"][0].rearrange("(k p) n -> p k n", p=P)
        x_v = io["x_prompt"][0].rearrange("(t p) d -> p t d", p=P)
        FIRST = 6
        units = lambda n: range(max(0, 3 * (n - FIRST)), max(0, min(2 * KD, 3 * (n - FIRST) + 3)))
        with nc.Block() as block:

            @block.sync
            def _(sp):
                sp.dma_start(c9[0:NDEC, :], io["c_sample"]).then_inc(c_in, 16)
                sp.dma_start(c9[NDEC:NC9, :], io["c_prompt"]).then_inc(c_in, 16)
                sp.dma_start(mod[:], io["b_ada"].broadcast_to([NC9, 6 * D])).then_inc(c_in, 16)
                sp.dma_start(gains[0:8, :], io["norm1_g"][0].rearrange("(k p) -> k p", p=P)).then_inc(c_in, 16)
                sp.dma_start(gains[8:16, :], io["norm2_g"][0].rearrange("(k p) -> k p", p=P)).then_inc(c_in, 16)
                for n in range(NMOD):
                    if n >= 3:
                        sp.wait_ge(mod_ps, n - 2)
                    sp.dma_start(wr[n % 3], w_ada[:, :, n * MODC:(n + 1) * MODC]).then_inc(w_in[n % 3], 16)

            @block.gpsimd
            def _(pool):
                pool.dma_start(xs[:], io["x_sample"].rearrange("b t d -> (b t) d")).then_inc(xs_in, 16)
                for t in range(TT):
                    pool.dma_start(x[:, t, :], x_v[:, t, :]).then_inc(x_in[t], 16)
                pool.wait_ge(mod_sb, NMOD)
                pool.dma_start(io["mod_d"][:], mod[:]).then_inc(mod_out, 16)
                pool.wait_ge(mod_out, 16)

            @block.scalar
            def _(act):
                act.wait_ge(c_in, 80)
                act.activation(c9[:], c9[:], ACT.Silu).then_inc(silu_done, 1)
                act.wait_ge(ss0, 1)
                act.wait_ge(xs_in, 16)
                act.activation(junk[0:NDEC, :], xs[:], ACT.Square, accum_out=ssq[0:NDEC, TT:TT + 1]).then_inc(sq_done, 1)
                for t in range(TT):
                    act.wait_ge(x_in[t], 16)
                    act.wait_ge(sq_done, t + 1)
                    act.activation(junk, x[:, t, :], ACT.Square, accum_out=ssq[:, t:t + 1]).then_inc(sq_done, 1)
                act.wait_ge(rstd_done, 1)
                act.activation(rstd[:], rstd[:], ACT.Sqrt).then_inc(std_done, 1)
                for n in range(2 * KD):
                    k = n // 2
                    act.wait_ge(h_ps, n + 1)
                    act.wait_ge(coef, 1)
                    if n >= 2:
                        act.wait_ge(h_split, n - 1)
                    act.activation(hf[n % 2][:], pt[n % 3][:], ACT.Identity, bias=g.modT[:, k, NDEC:NC9],
                                   scale=aT[:, k, NDEC:NC9]).then_inc(h_sb, 1)

            @block.tensor
            def _(pe):
                pe.wait_ge(g.const_ready, 2)
                pe.wait_ge(silu_done, 1)
                for k in range(KD):
                    mm = pe.transpose(pc[:, k, :], c9[:, k * P:(k + 1) * P], g.ident[0:NC9, 0:NC9])
                mm.then_inc(cT_ps, 1)
                pe.transpose(pt[0][:, 0:16], gains[:], g.ident[0:16, 0:16]).then_inc(g_ps, 1)
                pe.wait_ge(cT_done, 2)

                def mod_transposed(n):
                    pe.wait_ge(mod_sb, n + 1)
                    if n:
                        pe.wait_ge(modT_sb, n)
                    for q in range(4):
                        at = n * MODC + q * P
                        mm = pe.transpose(pq[:, q * NC9:(q + 1) * NC9], mod[:, at:at + P], g.ident[0:NC9, 0:NC9])
                    mm.then_inc(modT_ps, 1)

                for n in range(NMOD):
                    pe.wait_ge(w_in[n % 3], n // 3 * 16 + 16)
                    for k in range(KD):
                        mm = pe.matmul(pm[n % 3][:], cT[:, k, :], wr[n % 3][:, k, :], start=(k == 0), stop=(k == KD - 1))
                    mm.then_inc(mod_ps, 1)
                    if n:
                        mod_transposed(n - 1)
                    if n == FIRST:
                        pe.wait_ge(xn_done, TT + 1)
                    for u in units(n):
                        k, half = u // 2, u % 2
                        if u >= 3:
                            pe.wait_ge(h_sb, u - 2)
                        for q in range(4):
                            mm = pe.transpose(pt[u % 3][:, q * P:(q + 1) * P], x[:, half * 4 + q, k * P:(k + 1) * P], g.ident[:])
                        mm.then_inc(h_ps, 1)
                mod_transposed(NMOD - 1)
                for k in range(KD):
                    mm = pe.transpose(pc[:, k, 0:NDEC], xs[:, k * P:(k + 1) * P], g.ident[0:NDEC, 0:NDEC])
                mm.then_inc(hs_ps, 1)

            @block.vector
            def _(dve):
                dve.memset(ssq[:], 0.0).then_inc(ss0, 1)
                dve.wait_ge(cT_ps, 1)
                dve.tensor_copy(cT[:], pc[:]).then_inc(cT_done, 1)
                dve.wait_ge(g_ps, 1)
                dve.tensor_copy(g.gT[:], pt[0][:, 0:16]).then_inc(cT_done, 1)
                dve.wait_ge(c_in, 80)

                def mod_evacuated(n):
                    dve.wait_ge(modT_ps, n + 1)
                    dve.tensor_copy(g.modT[:, n * 4:(n + 1) * 4, :], pq[:].rearrange("p (a b) -> p a b", a=4)).then_inc(modT_sb, 1)

                for n in range(NMOD):
                    part = mod[:, n * MODC:(n + 1) * MODC]
                    dve.wait_ge(mod_ps, n + 1)
                    dve.tensor_tensor(part, pm[n % 3][:], part, ALU.add).then_inc(mod_sb, 1)
                    if n:
                        mod_evacuated(n - 1)
                    if n == 4:
                        dve.wait_ge(modT_sb, 4)
                        dve.scalar_tensor_tensor(out=aT[:], in0=g.modT[:, KD:2 * KD, :], scalar=1.0,
                                                 in1=g.gT[:, 0:KD].unsqueeze(2).broadcast_to([P, KD, NC9]), op0=ALU.add, op1=ALU.mult).then_inc(coef, 1)
                    if n == FIRST - 1:
                        dve.wait_ge(sq_done, TT + 1)
                        dve.tensor_scalar(rstd[:], ssq[:], 1.0 / D, EPS, ALU.mult, ALU.add).then_inc(rstd_done, 1)
                        dve.wait_ge(std_done, 1)
                        dve.reciprocal(rstd[:], rstd[:]).then_inc(rstd_done, 1)
                        dve.wait_ge(rstd_done, 2)
                        dve.tensor_scalar(xs[:], xs[:], rstd[0:NDEC, TT:TT + 1], None, ALU.mult).then_inc(xn_done, 1)
                        for t in range(TT):
                            dve.tensor_scalar(x[:, t, :], x[:, t, :], rstd[:, t:t + 1], None, ALU.mult).then_inc(xn_done, 1)
                    for u in units(n):
                        k, half = u // 2, u % 2
                        dve.wait_ge(h_sb, u + 1)
                        hi = g.hT_hi[:, k, half * 512:(half + 1) * 512]
                        lo = g.hT_lo[:, k, half * 512:(half + 1) * 512]
                        dve.tensor_copy(hi, hf[u % 2][:]).then_inc(hs_st, 1)
                        dve.wait_ge(hs_st, u + 1)
                        dve.tensor_tensor(lo, hf[u % 2][:], f32(hi), ALU.subtract).then_inc(h_split, 1)
                mod_evacuated(NMOD - 1)
                dve.wait_ge(hs_ps, 1)
                dve.wait_ge(coef, 1)
                dve.tensor_tensor(hs[:], pc[:, :, 0:NDEC], aT[:, :, 0:NDEC], ALU.mult).then_inc(coef, 1)
                dve.wait_ge(coef, 2)
                dve.tensor_tensor(hs[:], hs[:], g.modT[:, 0:KD, 0:NDEC], ALU.add).then_inc(coef, 1)
                dve.wait_ge(coef, 3)
                dve.tensor_copy(g.hT_hi[:, :, SEQ:NTOK], hs[:]).then_inc(coef, 1)
                dve.wait_ge(coef, 4)
                dve.tensor_tensor(g.hT_lo[:, :, SEQ:NTOK], hs[:], f32(g.hT_hi[:, :, SEQ:NTOK]), ALU.subtract).then_inc(coef, 1)


def project_token_major(nc, io, g):
    with Scope(nc, "z") as s:
        raw = [s.sb(f"raw{i}", [P, KD, ZCH]) for i in range(2)]
        whi = [s.sb(f"whi{i}", [P, KD, ZCH], F32R) for i in range(2)]
        wlo = [s.sb(f"wlo{i}", [P, KD, ZCH], F32R) for i in range(2)]
        acc = [s.ps(f"acc{i}", [P, 512]) for i in range(6)]
        w_in = [s.sem(f"w_in{i}") for i in range(2)]
        raw_free, w_hi, w_lo, w_free = s.sem("raw_free"), s.sem("w_hi"), s.sem("w_lo"), s.sem("w_free")
        acc_full, acc_free = s.sem("acc_full"), s.sem("acc_free")
        w = io["w_in"][0].rearrange("(k p) n -> p k n", p=P)
        NU = TT + 1
        with nc.Block() as block:

            @block.sync
            def _(sp):
                with sp.Fori(0, NZCH // 2) as i:
                    for j in range(2):
                        sp.wait_ge(raw_free, i * 2 + j + 1)
                        sp.dma_start(raw[j][:], w[:, :, ds((i * 2 + j) * ZCH, ZCH)]).then_inc(w_in[j], 16)

            @block.scalar
            def _(act):
                act.sem_inc(acc_free, 6)
                with act.Fori(0, NZCH // 2) as i:
                    for j in range(2):
                        for t in range(NU):
                            u = j * NU + t
                            rows = P if t < TT else NDEC
                            act.wait_ge(acc_full, i * 2 * NU + u + 1)
                            act.activation(g.z[0:rows, t, ds((i * 2 + j) * ZCH, ZCH)], acc[u % 6][0:rows, 0:ZCH],
                                           ACT.Copy).then_inc(acc_free, 1)

            @block.vector
            def _(dve):
                dve.sem_inc(raw_free, 2)
                with dve.Fori(0, NZCH // 2) as i:
                    for j in range(2):
                        dve.wait_ge(w_in[j], i * 16 + 16)
                        dve.wait_ge(w_free, i * 2 + j + 1)
                        dve.tensor_copy(whi[j][:], raw[j][:]).then_inc(w_hi, 1)
                        dve.wait_ge(w_hi, i * 2 + j + 1)
                        dve.tensor_tensor(wlo[j][:], raw[j][:], f32(whi[j][:]), ALU.subtract).then_inc(w_lo, 1)
                        dve.wait_ge(w_lo, i * 2 + j + 1)
                        dve.sem_inc(raw_free, 1)

            @block.tensor
            def _(pe):
                pe.sem_inc(w_free, 2)
                with pe.Fori(0, NZCH // 2) as i:
                    for j in range(2):
                        pe.wait_ge(w_lo, i * 2 + j + 1)
                        for t in range(NU):
                            u = j * NU + t
                            pe.wait_ge(acc_free, i * 2 * NU + u + 1)
                            rows = P if t < TT else NDEC
                            tok = slice(t * P, t * P + rows)
                            for k in range(KD):
                                for n, (a, b) in enumerate(((g.hT_hi, whi), (g.hT_lo, whi), (g.hT_hi, wlo))):
                                    mm = pe.matmul(acc[u % 6][0:rows, 0:ZCH], a[:, k, tok], b[j][:, k, :],
                                                   start=(k == 0 and n == 0), stop=(k == KD - 1 and n == 2))
                            mm.then_inc(acc_full, 1)
                        pe.wait_ge(acc_full, i * 2 * NU + (j + 1) * NU)
                        pe.sem_inc(w_free, 1)


def store_new_rows(sp, io, g, out):
    kv = io["kv_p"][0, 0].rearrange("(t p) c -> p t c", p=P)
    win = io["win_p"][0, 0].rearrange("(t p) c -> p t c", p=P)
    sp.dma_start(kv, g.z[:, 0:TT, C_CK:C_WK]).then_inc(out, 16)
    sp.dma_start(win, g.z[:, TT - WINDOW // P:TT, C_WK:C_G]).then_inc(out, 16)
    sp.dma_start(io["kv_s"][0, :, 0, :], g.z[0:NDEC, TT, C_CK:C_WK]).then_inc(out, 16)
    sp.dma_start(io["win_s"][0, :, WINDOW - 1, :], g.z[0:NDEC, TT, C_WK:C_G]).then_inc(out, 16)
    sp.dma_start(io["win_s"][0, :, 0:WINDOW - 1, :], io["state_win_kv"][0, :, 1:WINDOW, :]).then_inc(out, 16)


NORMS = [(C_QN, NH, 0), (C_SK, 1, 8), (C_DK, 4, 9), (C_WK, 1, 13), (C_QD, 8, 14)]
NG = 22
KEYS = [(C_SK, 8, 1), (C_WK, 13, 2)] + [(C_DK + HD * i, 9 + i, 3) for i in range(4)]


def attention_tiles(g, s):
    g.gain = s.sb("gain", [P, 6, HD])
    g.subln = s.sb("subln", [P, 2 * HD])
    g.neglam = s.sb("neglam", [P, 1])
    g.oss = s.sb("oss", [P, TT * NDH])
    g.wcmp = s.sb("wcmp", [P, 2, 60])
    g.pe4 = s.sb("pe4", [P, HD])
    g.G = s.sb("G", [P, TT + 1, 24])


def gates_and_constants(nc, io, g, a):
    NM = MC // P
    g.tsel = a.sb("tsel", [P, SEQ])
    g.twin = a.sb("twin", [P, WINDOW + P])
    g.tcmp = a.sb("tcmp", [P, TT * 32])
    g.seen = a.sb("seen", [P, TT * 32])
    lamb = a.sb("lamb", [P, 4, HD])
    lprod = a.sb("lprod", [P, 2, HD])
    lsum = a.sb("lsum", [P, 2])
    wcol = a.sb("wcol", [P, 2])
    iot = a.sb("iot", [P, SEQ], I32)
    loads, iota, tabs, lam, done = a.sem("k_loads"), a.sem("k_iota"), a.sem("k_tabs"), a.sem("k_lam"), a.sem("k_done")
    lexp, rows_out = a.sem("k_lexp"), a.sem("k_rows_out")
    g.rs = a.sb("rs", [P, TT + 1, NG])
    rs = g.rs
    rows = lambda t: P if t < TT else NDEC
    with Scope(nc, "mg") as s:
        raw = [s.sb(f"raw{i}", [P, KD, P]) for i in range(2)]
        whi = [s.sb(f"whi{i}", [P, KD, P], F32R) for i in range(2)]
        wlo = [s.sb(f"wlo{i}", [P, KD, P], F32R) for i in range(2)]
        gate = [s.sb(f"gate{i}", [P, NTOK]) for i in range(2)]
        sq = [s.sb(f"sq{i}", [P, NG, HD]) for i in range(2)]
        acc = [s.ps(f"acc{i}", [P, 512]) for i in range(6)]
        w_in = [s.sem(f"w_in{i}") for i in range(2)]
        raw_free, w_hi, w_lo, w_free = s.sem("raw_free"), s.sem("w_hi"), s.sem("w_lo"), s.sem("w_free")
        acc_full, acc_free, gate_ready = s.sem("acc_full"), s.sem("acc_free"), s.sem("gate_ready")
        gate_out = [s.sem(f"gate_out{i}") for i in range(2)]
        sqd, ssd, rsd, rstd, qs, qp, gat = (s.sem(n) for n in ("sqd", "ssd", "rsd", "rstd", "qs", "qp", "gat"))
        w = io["w_in"][0].rearrange("(k p) n -> p k n", p=P)
        with nc.Block() as block:

            @block.sync
            def _(sp):
                with sp.Fori(0, NM // 2) as i:
                    for j in range(2):
                        sp.wait_ge(raw_free, i * 2 + j + 1)
                        sp.dma_start(raw[j][:], w[:, :, ds((i * 2 + j) * P + C_M, P)]).then_inc(w_in[j], 16)
                store_new_rows(sp, io, g, rows_out)
                sp.wait_ge(rows_out, 80)

            @block.gpsimd
            def _(pool):
                n = 0

                def table(out, width, pattern, base):
                    nonlocal n
                    pool.iota(iot[:, 0:width], pattern=pattern, base=base, channel_multiplier=-1).then_inc(iota, 1)
                    pool.wait_ge(iota, n + 1)
                    pool.tensor_copy(out, iot[:, 0:width]).then_inc(tabs, 1)
                    n += 1
                    pool.wait_ge(tabs, n)

                def keep(t, fill, pattern, base, mult, count):
                    pool.affine_select(out=t, in_=t, compare_op=ALU.is_ge, fill=fill, base=base, pattern=pattern,
                                       channel_multiplier=mult).then_inc(done, 1)
                    pool.wait_ge(done, count)

                table(g.tsel[:], SEQ, [[1, SEQ]], P - SEQ)
                keep(g.tsel[:], NEG, [[-1, SEQ]], SEQ - P, 1, 1)
                table(g.twin[:], WINDOW + P, [[1, WINDOW + P]], -WINDOW)
                keep(g.twin[:], NEG, [[-1, WINDOW + P]], WINDOW, 1, 2)
                keep(g.twin[:], NEG, [[1, WINDOW + P]], -1, -1, 3)
                table(g.tcmp[:], TT * 32, [[-P, TT], [32, 32]], 31)
                keep(g.tcmp[:].rearrange("p (t n) -> p t n", t=TT), NEG, [[P, TT], [-32, 32]], -31, 1, 4)
                pool.memset(g.seen[:], 1.0).then_inc(done, 1)
                pool.wait_ge(done, 5)
                keep(g.seen[:].rearrange("p (t n) -> p t n", t=TT), 0.0, [[P, TT], [-32, 32]], -31, 1, 6)
                pool.memset(g.wcmp[:], 0.0).then_inc(done, 1)
                pool.wait_ge(done, 7)
                pool.wait_ge(loads, 20 * 16)
                for v in range(2):
                    w4 = g.wcmp[:, v, 28:32]
                    pool.tensor_copy(w4, wcol[:, v:v + 1].broadcast_to([P, 4])).then_inc(done, 1)
                    pool.wait_ge(done, 8 + 3 * v)
                    keep(w4, 0.0, [[-32, 4]], 0, 1, 9 + 3 * v)
                    keep(w4, 0.0, [[32, 4]], 31, -1, 10 + 3 * v)
                pool.wait_ge(rstd, 2)
                pool.wait_ge(lam, 2)
                for t in range(TT + 1):
                    r = rows(t)
                    q = g.z[0:r, t, C_QD:C_M].rearrange("p (a b) -> p a b", b=HD)
                    pool.tensor_tensor(q, q, rs[0:r, t, 14:22].unsqueeze(2).broadcast_to([r, 8, HD]), ALU.mult).then_inc(qp, 1)
                    pool.wait_ge(qp, 2 * t + 1)
                    pool.tensor_tensor(q, q, g.gain[0:r, 5:6, :].broadcast_to([r, 8, HD]), ALU.mult).then_inc(qp, 1)

            @block.scalar
            def _(act):
                act.sem_inc(acc_free, 6)
                gains = [io["nsa_q_norm"][0:1, :]] + [io["nsa_k_norm"][0, i:i + 1, :] for i in range(3)] + \
                    [io["diff_k_norm"][0:1, :], io["diff_q_norm"][0:1, :]]
                for i, gn in enumerate(gains):
                    act.dma_start(g.gain[:, i, :], gn.broadcast_to([P, HD])).then_inc(loads, 16)
                act.dma_start(g.subln[:], io["diff_subln"][0:1, :].broadcast_to([P, 2 * HD])).then_inc(loads, 16)
                act.dma_start(lamb[:].rearrange("p a b -> p (a b)"),
                             io["diff_lambda"].rearrange("l a b -> l (a b)").broadcast_to([P, 4 * HD])).then_inc(loads, 16)
                for q in range(4):
                    quarter = slice(32 * q, 32 * q + 32)
                    act.dma_start(g.pe4[quarter, :], io["nsa_cmp_pe"][0]).then_inc(loads, 16)
                    act.dma_start(wcol[quarter, 0:1], io["nsa_cmp_wk"].rearrange("l c -> c l")).then_inc(loads, 16)
                    act.dma_start(wcol[quarter, 1:2], io["nsa_cmp_wv"].rearrange("l c -> c l")).then_inc(loads, 16)
                act.wait_ge(lam, 4)
                act.activation(lsum[:], lsum[:], ACT.Exp).then_inc(lexp, 1)
                for t in range(TT + 1):
                    r = rows(t)
                    if t >= 2:
                        act.wait_ge(ssd, t - 1)
                    for c, n, o in NORMS:
                        act.activation(sq[t % 2][0:r, o:o + n, :].rearrange("p a b -> p (a b)"),
                                       g.z[0:r, t, c:c + n * HD], ACT.Square).then_inc(sqd, 1)
                act.wait_ge(rsd, 1)
                act.activation(rs[:], rs[:], ACT.Sqrt).then_inc(rstd, 1)
                act.activation(g.G[:, 0:TT, :], g.z[:, 0:TT, C_G:C_QD], ACT.Sigmoid).then_inc(gat, 1)
                act.activation(g.G[0:NDEC, TT, :], g.z[0:NDEC, TT, C_G:C_QD], ACT.Sigmoid).then_inc(gat, 1)

                def gates(j, n):
                    for c in range(3):
                        act.wait_ge(acc_full, n * 3 + c + 1)
                        act.activation(gate[j][:, c * TCH:(c + 1) * TCH], acc[j * 3 + c][:, 0:TCH],
                                       ACT.Sigmoid).then_inc(gate_ready, 1)
                    act.wait_ge(gate_ready, n * 3 + 3)
                    act.sem_inc(acc_free, 3)
                    act.dma_start(io["gate_d"][ds(n * P, P), :], gate[j][:]).then_inc(gate_out[j], 16)

                gates(0, 0)
                gates(1, 1)
                with act.Fori(1, NM // 2) as i:
                    for j in range(2):
                        act.wait_ge(gate_out[j], i * 16)
                        gates(j, i * 2 + j)
                for j in range(2):
                    act.wait_ge(gate_out[j], NM // 2 * 16)

            @block.vector
            def _(dve):
                dve.sem_inc(raw_free, 2)

                def split(j, n, turn):
                    dve.wait_ge(w_in[j], turn * 16 + 16)
                    dve.wait_ge(w_free, n + 1)
                    dve.tensor_copy(whi[j][:], raw[j][:]).then_inc(w_hi, 1)
                    dve.wait_ge(w_hi, n + 1)
                    dve.tensor_tensor(wlo[j][:], raw[j][:], f32(whi[j][:]), ALU.subtract).then_inc(w_lo, 1)
                    dve.wait_ge(w_lo, n + 1)
                    dve.sem_inc(raw_free, 1)

                def normalise_queries(tiles):
                    for t in tiles:
                        r = rows(t)
                        q = g.z[0:r, t, C_QN:C_CK].rearrange("p (a b) -> p a b", b=HD)
                        dve.tensor_tensor(q, q, rs[0:r, t, 0:8].unsqueeze(2).broadcast_to([r, 8, HD]), ALU.mult).then_inc(qs, 1)
                        dve.wait_ge(qs, 2 + 2 * t)
                        dve.tensor_tensor(q, q, g.gain[0:r, 0:1, :].broadcast_to([r, 8, HD]), ALU.mult).then_inc(qs, 1)

                split(0, 0, 0)
                split(1, 1, 0)
                dve.wait_ge(loads, 20 * 16)
                for n, i in enumerate((0, 5)):
                    dve.tensor_scalar(g.gain[:, i, :], g.gain[:, i, :], HD ** -0.5, None, ALU.mult).then_inc(lam, 1)
                lv = lamb[:].rearrange("p (a b) d -> p a b d", b=2)
                dve.tensor_tensor(lprod[:], lv[:, :, 0, :], lv[:, :, 1, :], ALU.mult).then_inc(lam, 1)
                dve.wait_ge(lam, 3)
                dve.tensor_reduce(lsum[:], lprod[:], AX.X, ALU.add).then_inc(lam, 1)
                dve.tensor_scalar(g.subln[:], g.subln[:], 1.0 - LAM_INIT, None, ALU.mult).then_inc(lam, 1)
                dve.wait_ge(lexp, 1)
                dve.tensor_tensor(g.neglam[:], lsum[:, 1:2], lsum[:, 0:1], ALU.subtract).then_inc(lam, 1)
                dve.wait_ge(lam, 6)
                dve.tensor_scalar(g.neglam[:], g.neglam[:], -LAM_INIT, None, ALU.add).then_inc(lam, 1)
                dve.memset(rs[:], 1.0).then_inc(qs, 1)
                dve.wait_ge(qs, 1)
                for t in range(TT + 1):
                    r = rows(t)
                    dve.wait_ge(sqd, 5 * (t + 1))
                    dve.tensor_reduce(rs[0:r, t, :], sq[t % 2][0:r], AX.X, ALU.add).then_inc(ssd, 1)
                dve.wait_ge(ssd, TT + 1)
                dve.tensor_scalar(rs[:], rs[:], 1.0 / HD, EPS, ALU.mult, ALU.add).then_inc(rsd, 1)
                dve.wait_ge(rstd, 1)
                dve.reciprocal(rs[:], rs[:]).then_inc(rstd, 1)
                dve.wait_ge(rstd, 2)
                split(0, 2, 1)
                split(1, 3, 1)
                normalise_queries(range(0, 5))
                split(0, 4, 2)
                split(1, 5, 2)
                normalise_queries(range(5, TT + 1))
                with dve.Fori(3, NM // 2) as i:
                    for j in range(2):
                        split(j, i * 2 + j, i)

            @block.tensor
            def _(pe):
                pe.sem_inc(w_free, 2)
                with pe.Fori(0, NM // 2) as i:
                    for j in range(2):
                        n = i * 2 + j
                        pe.wait_ge(w_lo, n + 1)
                        for c in range(3):
                            tok = slice(c * TCH, (c + 1) * TCH)
                            pe.wait_ge(acc_free, n * 3 + c + 1)
                            for k in range(KD):
                                for q, (x, b) in enumerate(((whi, g.hT_hi), (wlo, g.hT_hi), (whi, g.hT_lo))):
                                    mm = pe.matmul(acc[j * 3 + c][:, 0:TCH], x[j][:, k, :], b[:, k, tok],
                                                   start=(k == 0 and q == 0), stop=(k == KD - 1 and q == 2))
                            mm.then_inc(acc_full, 1)
                        pe.wait_ge(acc_full, n * 3 + 3)
                        pe.sem_inc(w_free, 1)


def prepare_keys(nc, io, g, a):
    g.kkd = a.sb("kkd", [P, 4 * SEQ], F32R)
    g.kk = [a.sb(f"kk{i}", [P, SEQ], F32R) for i in range(2)]
    g.kk += [g.kkd[:, i * SEQ:(i + 1) * SEQ] for i in range(4)]
    g.kkc = a.sb("kkc", [P, 32], F32R)
    g.vcb = a.sb("vcb", [P, 4, HD])
    with Scope(nc, "keys") as s:
        rs = g.rs
        knorm = s.sb("knorm", [P, TT, HD])
        kdup = [s.sb(f"kdup{i}", [P, TT, 2, HD]) for i in range(2)]
        ckp = s.sb("ckp", [P, TT, HD])
        kc = s.sb("kc", [32, HD])
        kcsq = s.sb("kcsq", [32, HD])
        kcs = s.sb("kcs", [32, 1])
        kcd = s.sb("kcd", [32, 2, HD])
        pk = [s.ps(f"pk{i}", [P, SEQ]) for i in range(2)]
        pcmp = s.ps("pcmp", [32, 2, HD])
        pkc = s.ps("pkc", [P, 32])
        qs, kn, kd, kt, khi, klo, cp, cs, gat = (s.sem(n) for n in ("qs", "kn", "kd", "kt", "khi", "klo", "cp", "cs", "gat"))
        with nc.Block() as block:

            @block.scalar
            def _(act):
                act.wait_ge(cs, 3)
                act.activation(kcsq[:], kc[:], ACT.Square, accum_out=kcs[:]).then_inc(gat, 1)
                act.wait_ge(cs, 4)
                act.activation(kcs[:], kcs[:], ACT.Sqrt).then_inc(gat, 1)
                for i in range(6):
                    act.wait_ge(kt, i + 1)
                    act.activation(g.kk[i][:], pk[i % 2][:], ACT.Copy).then_inc(khi, 1)

            @block.tensor
            def _(pe):
                pe.wait_ge(cp, 1)
                for v in range(2):
                    for t in range(TT):
                        rhs = ckp[:, t, :] if v == 0 else g.z[:, t, C_CV:C_SK]
                        mm = pe.matmul(pcmp[:, v, :], g.wcmp[:, v, 28 - 4 * t:60 - 4 * t], rhs,
                                       start=(t == 0), stop=(t == TT - 1))
                    mm.then_inc(cs, 1)
                for i in range(6):
                    pe.wait_ge(kd, i + 1)
                    if i >= 2:
                        pe.wait_ge(klo, i - 1)
                    for t in range(TT):
                        mm = pe.transpose(pk[i % 2][:, t * P:(t + 1) * P], kdup[i % 2][:, t].rearrange("p a b -> p (a b)"), g.ident[:])
                    mm.then_inc(kt, 1)
                pe.wait_ge(kd, 7)
                pe.transpose(pkc[:], kcd[:].rearrange("p a b -> p (a b)"), g.ident[0:32, 0:32]).then_inc(kt, 1)

            def low(dve, i):
                dve.wait_ge(khi, i + 1)
                dve.tensor_tensor(g.kk[i][HD:P, :], pk[i % 2][HD:P, :], f32(g.kk[i][HD:P, :]), ALU.subtract).then_inc(klo, 1)

            @block.vector
            def _(dve):
                dve.tensor_tensor(ckp[:], g.z[:, 0:TT, C_CK:C_CV], g.pe4[:].unsqueeze(1).broadcast_to([P, TT, HD]), ALU.add).then_inc(cp, 1)
                dve.memset(g.vcb[:], 0.0).then_inc(qs, 1)
                dve.wait_ge(qs, 1)
                dve.wait_ge(cs, 2)
                for h in range(4):
                    dve.tensor_copy(g.vcb[32 * h:32 * h + 32, h, :], pcmp[:, 1, :]).then_inc(qs, 1)
                dve.tensor_copy(kc[:], pcmp[:, 0, :]).then_inc(cs, 1)
                dve.wait_ge(gat, 1)
                dve.tensor_scalar(kcs[:], kcs[:], 1.0 / HD, EPS, ALU.mult, ALU.add).then_inc(cs, 1)
                for i, (c, slot, gain) in enumerate(KEYS):
                    if i >= 1:
                        dve.wait_ge(kd, i)
                    dve.tensor_tensor(knorm[:], g.z[:, 0:TT, c:c + HD],
                                      rs[:, 0:TT, slot:slot + 1].broadcast_to([P, TT, HD]), ALU.mult).then_inc(kn, 1)
                    dve.wait_ge(kn, i + 1)
                    if i >= 2:
                        dve.wait_ge(kt, i - 1)
                    gk = g.gain[:, gain + 1, :]
                    dve.tensor_tensor(kdup[i % 2][:], knorm[:].unsqueeze(2).broadcast_to([P, TT, 2, HD]),
                                      gk.unsqueeze(1).unsqueeze(1).broadcast_to([P, TT, 2, HD]), ALU.mult).then_inc(kd, 1)
                    if i >= 1:
                        low(dve, i - 1)
                low(dve, 5)
                dve.wait_ge(gat, 2)
                dve.reciprocal(kcs[:], kcs[:]).then_inc(cs, 1)
                dve.wait_ge(cs, 5)
                dve.tensor_scalar(kc[:], kc[:], kcs[:, 0:1], None, ALU.mult).then_inc(cs, 1)
                dve.wait_ge(cs, 6)
                dve.tensor_tensor(kcd[:], kc[:].unsqueeze(1).broadcast_to([32, 2, HD]),
                                  g.gain[0:32, 1:2, :].broadcast_to([32, 2, HD]), ALU.mult).then_inc(kd, 1)
                dve.wait_ge(kt, 7)
                dve.tensor_copy(g.kkc[:], pkc[:]).then_inc(cs, 1)
                dve.wait_ge(cs, 7)
                dve.tensor_tensor(g.kkc[HD:P, :], pkc[HD:P, :], f32(g.kkc[HD:P, :]), ALU.subtract).then_inc(cs, 1)


def key_chunks(n):
    return [(c, min(n, c + 512)) for c in range(0, n, 512)]


def nsa_attention(nc, io, g):
    NU = 2 * TT
    units = [(i, 0, 0, (i + 1) * P) if b == 0 else (i, 1, max(0, i - 4) * P, (i + 1) * P)
             for i in range(TT) for b in range(2)]
    groups = [(k1 - k0 + 511) // 512 for _, _, k0, k1 in units]
    second = np.cumsum([0] + [n - 1 for n in groups]).tolist()
    VCOL = (C_SV, C_WV)
    with Scope(nc, "nsa") as s:
        qd = s.sb("qd", [P, TT, 2, HD])
        qhi = s.sb("qhi", [P, SEQ], F32R)
        qlo = s.sb("qlo", [P, SEQ], F32R)
        prob = [s.sb(f"prob{i}", [P, SEQ]) for i in range(4)]
        probT = [s.sb(f"probT{i}", [P, TT, P]) for i in range(2)]
        nmax = s.sb("nmax", [P, NU])
        total = s.sb("total", [P, NU])
        share = s.sb("share", [P, 2, 2])
        scmp = s.sb("scmp", [P, TT, NH, 32])
        cm = s.sb("cm", [P, NH * TT])
        cs = s.sb("cs", [P, NH * TT])
        pcT = [s.sb(f"pcT{i}", [P, P]) for i in range(2)]
        sc = [s.ps(f"sc{i}", [P, SEQ]) for i in range(2)]
        tp = [s.ps(f"tp{i}", [P, 512]) for i in range(2)]
        out = [s.ps(f"out{i}", [P, 2, P]) for i in range(2)]
        q_dup, q_ps, q_hi = s.sem("q_dup"), s.sem("q_ps"), s.sem("q_hi")
        sc_full, sc_free = s.sem("sc_full"), s.sem("sc_free")
        tab, biased, p_full = s.sem("tab"), s.sem("biased"), s.sem("p_full")
        tp_full, tp_act, tp_dve = s.sem("tp_full"), s.sem("tp_act"), s.sem("tp_dve")
        turn = s.sem("turn")
        pv_done, o_free, shares, o_sel = s.sem("pv_done"), s.sem("o_free"), s.sem("shares"), s.sem("o_sel")
        c_step, c_exp, c_tp, c_ev, c_pv, c_add = (s.sem(n) for n in ("c_step", "c_exp", "c_tp", "c_ev", "c_pv", "c_add"))
        LAG = 2
        NG2 = second[NU]
        NT = NU + NG2
        with nc.Block() as block:

            @block.gpsimd
            def _(pool):
                with pool.Fori(0, NH + 1) as h:
                    pool.wait_ge(q_ps, h + 1)
                    for d in range(2):
                        pool.tensor_copy(qd[:, :, d, :], g.z[:, 0:TT, ds(h * HD + C_QN, HD)]).then_inc(q_dup, 1)

            @block.tensor
            def _(pe):
                def score(slot, c0, i, k0, k1, keys):
                    for a, b in key_chunks(k1 - k0):
                        for n, q in enumerate((qhi, qlo)):
                            mm = pe.matmul(sc[slot][:, c0 + a:c0 + b], q[:, i * P:(i + 1) * P], keys[:, k0 + a:k0 + b],
                                           start=(n == 0), stop=(n == 1))
                    return mm

                pe.sem_inc(pv_done, 2)
                pe.sem_inc(q_ps, 1)

                def transpose_queries(h):
                    pe.wait_ge(q_dup, h * 2 + 2)
                    pe.wait_ge(sc_free, h * (NU + 2) + 1)
                    for t in range(TT):
                        mm = pe.transpose(sc[0][:, t * P:(t + 1) * P], qd[:, t].rearrange("p a b -> p (a b)"), g.ident[:])
                    mm.then_inc(q_ps, 1)

                transpose_queries(0)
                with pe.Fori(0, NH) as h:
                    pe.wait_ge(sc_free, h * (NU + 2) + 3)
                    for i in range(TT):
                        mm = score(1, 32 * i, i, 0, 32, g.kkc)
                    mm.then_inc(sc_full, 1)
                    for u in range(NU + LAG + 1):
                        if u < NU:
                            i, b, k0, k1 = units[u]
                            pe.wait_ge(sc_free, h * (NU + 2) + 3 + u)
                            score(u % 2, 0, i, k0, k1, g.kk[b]).then_inc(sc_full, 1)
                        if u == NU:
                            transpose_queries(h + 1)
                        if LAG <= u < NU + LAG:
                            v = u - LAG
                            i, b, k0, k1 = units[v]
                            nt = (k1 - k0) // P
                            pe.wait_ge(p_full, h * NU + v + 1)
                            for gr in range(groups[v]):
                                if gr == 0:
                                    pe.wait_ge(tp_act, h * NU + v + 1)
                                else:
                                    pe.wait_ge(tp_dve, h * NG2 + second[v] + 1)
                                for q in range(4 * gr, min(nt, 4 * gr + 4)):
                                    mm = pe.transpose(tp[gr][:, (q - 4 * gr) * P:(q - 4 * gr + 1) * P],
                                                      prob[v % 4][:, q * P:(q + 1) * P], g.ident[:])
                                mm.then_inc(tp_full, 1)
                        if u > LAG:
                            v = u - LAG - 1
                            i, b, k0, k1 = units[v]
                            nt = (k1 - k0) // P
                            if b == 0:
                                pe.wait_ge(o_free, h * TT + i + 1)
                            for gr in range(groups[v]):
                                if gr == 0:
                                    if v == NU - 1:
                                        pe.wait_ge(tp_act, h * NU + v + 2)
                                elif v == NU - 1 or groups[v + 1] == 1:
                                    pe.wait_ge(tp_dve, h * NG2 + second[v] + 2)
                                for q in range(4 * gr, min(nt, 4 * gr + 4)):
                                    mm = pe.matmul(out[i % 2][:, b, :], probT[v % 2][:, q, :],
                                                   g.z[:, k0 // P + q, VCOL[b]:VCOL[b] + P], start=(q == 0), stop=(q == nt - 1))
                            mm.then_inc(pv_done, 1)
                pe.wait_ge(c_step, 6)
                for n in range(2 * TT):
                    i, hh = n // 2, n % 2
                    if n >= 2:
                        pe.wait_ge(c_ev, n - 1)
                    src = scmp[:, i, 4 * hh:4 * hh + 4, :].rearrange("p h n -> p (h n)")
                    pe.transpose(tp[n % 2][:, 0:P], src, g.ident[:]).then_inc(c_tp, 1)
                    pe.wait_ge(c_ev, n + 1)
                    if n >= 2:
                        pe.wait_ge(c_add, n - 1)
                    pe.matmul(sc[n % 2][:, 0:4 * HD], pcT[n % 2][:], g.vcb[:].rearrange("p a b -> p (a b)"),
                              start=True, stop=True).then_inc(c_pv, 1)

            @block.scalar
            def _(act):
                act.sem_inc(tp_act, 1)

                def queries_hi(h):
                    act.wait_ge(q_ps, h + 2)
                    act.activation(qhi[:], sc[0][:], ACT.Copy).then_inc(q_hi, 1)

                queries_hi(0)
                with act.Fori(0, NH) as h:
                    for u in range(NU + LAG):
                        if u >= LAG:
                            v = u - LAG
                            i, b, k0, k1 = units[v]
                            n = min(4, (k1 - k0) // P)
                            act.wait_ge(tp_full, h * NT + v + second[v] + 1)
                            act.wait_ge(pv_done, h * NU + v + 1)
                            act.activation(probT[v % 2][:, 0:n, :].rearrange("p a b -> p (a b)"), tp[0][:, 0:n * P],
                                           ACT.Copy).then_inc(tp_act, 1)
                        if u < NU:
                            i, b, k0, k1 = units[u]
                            act.wait_ge(biased, h * NU + u + 1)
                            act.activation(prob[u % 4][:, 0:k1 - k0], prob[u % 4][:, 0:k1 - k0], ACT.Exp,
                                           bias=nmax[:, u:u + 1], scale=-1.0, accum_out=total[:, u:u + 1]).then_inc(p_full, 1)
                        if u == NU:
                            queries_hi(h + 1)
                act.wait_ge(c_step, 2)
                act.activation(scmp[:], scmp[:], ACT.Exp).then_inc(c_exp, 1)

            @block.vector
            def _(dve):
                dve.sem_inc(sc_free, 2)
                dve.sem_inc(o_free, 2)
                dve.sem_inc(tp_dve, 1)

                def finish(h, i):
                    dve.wait_ge(pv_done, h * NU + 2 * i + 2 + 2)
                    r = share[:, i % 2, :]
                    dve.reciprocal(r, total[:, 2 * i:2 * i + 2]).then_inc(shares, 1)
                    dve.wait_ge(shares, h * 2 * TT + 2 * i + 1)
                    dve.tensor_tensor(r, r, g.G[:, i, ds(h * 3 + 1, 2)], ALU.mult).then_inc(shares, 1)
                    dve.wait_ge(shares, h * 2 * TT + 2 * i + 2)
                    o = g.z[:, i, ds(h * HD + C_QN, HD)]
                    dve.tensor_scalar(o, out[i % 2][:, 0, 0:HD], share[:, i % 2, 0:1], None, ALU.mult).then_inc(o_sel, 1)
                    dve.wait_ge(o_sel, h * TT + i + 1)
                    dve.scalar_tensor_tensor(out=o, in0=out[i % 2][:, 1, 0:HD], scalar=share[:, i % 2, 1:2], in1=o,
                                             op0=ALU.mult, op1=ALU.add).then_inc(o_free, 1)


                def halve_slopes():
                    for t in (g.tsel, g.twin, g.tcmp):
                        dve.tensor_scalar(t[:], t[:], 0.5, None, ALU.mult).then_inc(tab, 1)

                def queries_lo(h):
                    dve.wait_ge(q_hi, h + 1)
                    dve.tensor_tensor(qlo[:], sc[0][:], f32(qhi[:]), ALU.subtract).then_inc(sc_free, 1)

                halve_slopes()
                queries_lo(0)
                with dve.Fori(0, NH) as h:
                    dve.wait_ge(tab, h * 3 + 3)
                    dve.wait_ge(sc_full, h * (NU + 1) + 1)
                    tn = lambda a: a.rearrange("p (t n) -> p t n", t=TT)
                    dve.tensor_tensor(scmp[:, :, ds(h, 1), :].rearrange("p t a n -> p t (a n)"), tn(sc[1][:, 0:TT * 32]),
                                      tn(g.tcmp[:]), ALU.add).then_inc(sc_free, 1)
                    for u in range(NU + LAG):
                        if u < NU:
                            i, b, k0, k1 = units[u]
                            n = k1 - k0
                            table = g.tsel if b == 0 else g.twin
                            w = SEQ if b == 0 else WINDOW + P
                            dve.wait_ge(sc_full, h * (NU + 1) + u + 2)
                            if u < 4:
                                dve.wait_ge(pv_done, h * NU + 2)
                            else:
                                v = u - 4
                                dve.wait_ge(tp_full, h * NT + v + second[v] + groups[v])
                            dve.sem_inc(turn, 1)
                            dve.tensor_tensor_reduce(prob[u % 4][:, 0:n], sc[u % 2][:, 0:n], table[:, w - n:w], -1.0, 3e38,
                                                     ALU.add, ALU.min, nmax[:, u:u + 1]).then_inc(biased, 1)
                            dve.wait_ge(biased, h * NU + u + 1)
                            dve.sem_inc(sc_free, 1)
                        if u >= LAG and groups[u - LAG] == 2:
                            v = u - LAG
                            i, b, k0, k1 = units[v]
                            nt = (k1 - k0) // P
                            dve.wait_ge(tp_full, h * NT + v + second[v] + 2)
                            dve.wait_ge(pv_done, h * NU + v + 1)
                            dve.tensor_copy(probT[v % 2][:, 4:nt, :].rearrange("p a b -> p (a b)"),
                                            tp[1][:, 0:(nt - 4) * P]).then_inc(tp_dve, 1)
                        if u >= LAG + 3 and (u - LAG) % 2 == 1:
                            finish(h, (u - LAG - 3) // 2)
                    queries_lo(h + 1)
                    halve_slopes()
                    finish(h, TT - 1)
                sv = scmp[:].rearrange("p t h n -> p (t h) n")
                m3 = lambda a: a[:].unsqueeze(2).broadcast_to([P, NH * TT, 32])
                dve.wait_ge(sc_free, NH * (NU + 2) + 3)
                dve.tensor_reduce(cm[:], sv, AX.X, ALU.max).then_inc(c_step, 1)
                dve.wait_ge(c_step, 1)
                dve.tensor_tensor(sv, sv, m3(cm), ALU.subtract).then_inc(c_step, 1)
                dve.wait_ge(c_exp, 1)
                seen = g.seen[:].rearrange("p (t n) -> p t n", t=TT).unsqueeze(2).broadcast_to([P, TT, NH, 32])
                dve.tensor_tensor(scmp[:], scmp[:], seen, ALU.mult).then_inc(c_step, 1)
                dve.wait_ge(c_step, 3)
                dve.tensor_reduce(cs[:], sv, AX.X, ALU.add).then_inc(c_step, 1)
                dve.wait_ge(c_step, 4)
                dve.tensor_scalar(cm[:], cs[:], 1e-30, None, ALU.max).then_inc(c_step, 1)
                dve.wait_ge(c_step, 5)
                dve.reciprocal(cs[:], cm[:]).then_inc(shares, 1)
                dve.wait_ge(shares, NH * 2 * TT + 1)
                csv = cs[:].rearrange("p (t h) -> p t h", t=TT)
                dve.tensor_tensor(csv, csv, g.G[:, 0:TT, 0:24:3], ALU.mult).then_inc(shares, 1)
                dve.wait_ge(shares, NH * 2 * TT + 2)
                dve.tensor_tensor(sv, sv, m3(cs), ALU.mult).then_inc(c_step, 1)
                for n in range(2 * TT):
                    i, hh = n // 2, n % 2
                    dve.wait_ge(c_tp, n + 1)
                    if n >= 2:
                        dve.wait_ge(c_pv, n - 1)
                    dve.tensor_copy(pcT[n % 2][:], tp[n % 2][:, 0:P]).then_inc(c_ev, 1)
                    dve.wait_ge(c_pv, n + 1)
                    o = g.z[:, i, C_QN + 4 * HD * hh:C_QN + 4 * HD * (hh + 1)]
                    dve.tensor_tensor(o, sc[n % 2][:, 0:4 * HD], o, ALU.add).then_inc(c_add, 1)


def diff_attention(nc, io, g):
    NU = 2 * TT
    groups = [(i + 4) // 4 for i in range(TT)]
    second = np.cumsum([0] + [n - 1 for n in groups]).tolist()
    NG2 = second[TT]
    NT = TT + NG2
    with Scope(nc, "dif") as s:
        qd = s.sb("qd", [P, TT, 2, 2, HD])
        qhi = [s.sb(f"qhi{m}", [P, SEQ], F32R) for m in range(2)]
        qlo = [s.sb(f"qlo{m}", [P, SEQ], F32R) for m in range(2)]
        prob = [s.sb(f"prob{i}", [P, SEQ]) for i in range(6)]
        probT = [s.sb(f"probT{i}", [P, TT, P]) for i in range(2)]
        nmax = s.sb("nmax", [P, NU])
        total = s.sb("total", [P, NU])
        share = s.sb("share", [P, TT, 2])
        factor = s.sb("factor", [P, 2])
        oss = g.oss
        junk = [s.sb(f"junk{i}", [P, P]) for i in range(2)]
        sc = [s.ps(f"sc{i}", [P, SEQ]) for i in range(2)]
        tp = [s.ps(f"tp{i}", [P, 512]) for i in range(2)]
        out = [s.ps(f"out{i}", [P, P]) for i in range(2)]
        q_dup, q_ps, q_hi, q_lo = s.sem("q_dup"), s.sem("q_ps"), s.sem("q_hi"), s.sem("q_lo")
        sc_full, sc_free = s.sem("sc_full"), s.sem("sc_free")
        tab, biased, p_full = s.sem("tab"), s.sem("biased"), s.sem("p_full")
        joined, shares = s.sem("joined"), s.sem("shares")
        tp_full, tp_act, tp_dve = s.sem("tp_full"), s.sem("tp_act"), s.sem("tp_dve")
        turn = s.sem("turn")
        pv_done, o_free, o_step, o_act = s.sem("pv_done"), s.sem("o_free"), s.sem("o_step"), s.sem("o_act")
        with nc.Block() as block:

            @block.gpsimd
            def _(pool):
                with pool.Fori(0, NDH) as j:
                    pool.wait_ge(q_ps, j * 2 + 1)
                    for m in range(2):
                        for d in range(2):
                            pool.tensor_copy(qd[:, :, m, d, :], g.z[:, 0:TT, ds(j * 2 * HD + C_QD + m * HD, HD)]).then_inc(q_dup, 1)
                pool.wait_ge(q_ps, NDH * 2 + 1)
                pool.sem_inc(q_dup, 4)

            @block.tensor
            def _(pe):
                pe.sem_inc(pv_done, 2)
                pe.sem_inc(q_ps, 1)

                def transpose_queries(j):
                    pe.wait_ge(q_dup, j * 4 + 4)
                    for m in range(2):
                        pe.wait_ge(sc_free, j * (NU + 2) + m + 1)
                        for t in range(TT):
                            mm = pe.transpose(sc[m][:, t * P:(t + 1) * P], qd[:, t, m].rearrange("p a b -> p (a b)"), g.ident[:])
                        mm.then_inc(q_ps, 1)

                def transpose_probs(j, v):
                    nt = v + 1
                    pe.wait_ge(joined, j * TT + v + 1)
                    for gr in range(groups[v]):
                        if gr == 0:
                            pe.wait_ge(tp_act, j * TT + v + 1)
                        else:
                            pe.wait_ge(tp_dve, j * NG2 + second[v] + 1)
                        for q in range(4 * gr, min(nt, 4 * gr + 4)):
                            mm = pe.transpose(tp[gr][:, (q - 4 * gr) * P:(q - 4 * gr + 1) * P],
                                              prob[2 * (v % 3)][:, q * P:(q + 1) * P], g.ident[:])
                        mm.then_inc(tp_full, 1)

                def values(n, j, v):
                    nt = v + 1
                    pe.wait_ge(o_free, j * TT + v + 1)
                    for gr in range(groups[v]):
                        if gr == 0:
                            pe.wait_ge(tp_act, j * TT + v + 2)
                        else:
                            pe.wait_ge(tp_dve, j * NG2 + second[v] + 2)
                        for q in range(4 * gr, min(nt, 4 * gr + 4)):
                            mm = pe.matmul(out[v % 2][:], probT[v % 2][:, q, :],
                                           g.z[:, q, ds(n * 2 * HD + C_DV, 2 * HD)], start=(q == 0), stop=(q == nt - 1))
                    mm.then_inc(pv_done, 1)

                def scores(n, j, i):
                    for m in range(2):
                        pe.wait_ge(sc_free, j * (NU + 2) + 2 * i + m + 3)
                        for a, b in key_chunks((i + 1) * P):
                            for x, q in enumerate((qhi[m], qlo[m])):
                                mm = pe.matmul(sc[m][:, a:b], q[:, i * P:(i + 1) * P], g.kkd[:, ds(n * 2 * SEQ + m * SEQ + a, b - a)],
                                               start=(x == 0), stop=(x == 1))
                        mm.then_inc(sc_full, 1)

                transpose_queries(0)
                with pe.Fori(0, NDH // 2) as n:
                    for gg in range(2):
                        j = n * 2 + gg
                        for i in range(TT + 3):
                            if i < TT:
                                scores(n, j, i)
                            if i == TT:
                                transpose_queries(j + 1)
                            if 2 <= i < TT + 2:
                                transpose_probs(j, i - 2)
                            if i > 2:
                                values(n, j, i - 3)

            @block.scalar
            def _(act):
                act.sem_inc(tp_act, 1)
                act.sem_inc(o_free, 2)

                def finish(j, i):
                    act.wait_ge(pv_done, j * TT + i + 3)
                    act.activation(g.z[:, i, ds(j * 2 * HD + C_QD, 2 * HD)], out[i % 2][:], ACT.Copy, scale=share[:, i, 0:1]).then_inc(o_step, 1)
                    act.activation(junk[i % 2][:], out[i % 2][:], ACT.Square, scale=share[:, i, 0:1],
                                   accum_out=oss[:, ds(j + i * NDH, 1)]).then_inc(o_free, 1)

                def queries_hi(j):
                    for m in range(2):
                        act.wait_ge(q_ps, j * 2 + m + 2)
                        act.activation(qhi[m][:], sc[m][:], ACT.Copy).then_inc(q_hi, 1)

                queries_hi(0)
                with act.Fori(0, NDH) as j:
                    for i in range(TT + 2):
                        if i > 1:
                            v = i - 2
                            n = min(4, v + 1)
                            act.wait_ge(tp_full, j * NT + v + second[v] + 1)
                            act.wait_ge(pv_done, j * TT + v + 1)
                            act.activation(probT[v % 2][:, 0:n, :].rearrange("p a b -> p (a b)"), tp[0][:, 0:n * P],
                                           ACT.Copy).then_inc(tp_act, 1)
                        if i < TT:
                            for m in range(2):
                                u = 2 * i + m
                                act.wait_ge(biased, j * NU + u + 1)
                                pr = prob[u % 6][:, 0:(i + 1) * P]
                                act.activation(pr, pr, ACT.Exp, bias=nmax[:, u:u + 1], scale=-1.0,
                                               accum_out=total[:, u:u + 1]).then_inc(p_full, 1)
                        if i == TT:
                            queries_hi(j + 1)
                        if i >= 4:
                            finish(j, i - 4)
                    finish(j, TT - 2)
                    finish(j, TT - 1)
                act.wait_ge(shares, NDH * 2 * TT + 1)
                act.activation(oss[:], oss[:], ACT.Sqrt).then_inc(o_act, 1)

            @block.vector
            def _(dve):
                dve.sem_inc(sc_free, 2)
                dve.sem_inc(tp_dve, 1)
                dve.tensor_scalar(g.tsel[:], g.tsel[:], 512.0, None, ALU.mult).then_inc(tab, 1)
                dve.wait_ge(tab, 1)

                def quarter_slopes():
                    dve.tensor_scalar(g.tsel[:], g.tsel[:], 0.25, None, ALU.mult).then_inc(tab, 1)

                def queries_lo(j):
                    for m in range(2):
                        dve.wait_ge(q_hi, j * 2 + m + 1)
                        dve.tensor_tensor(qlo[m][:], sc[m][:], f32(qhi[m][:]), ALU.subtract).then_inc(q_lo, 1)
                        dve.wait_ge(q_lo, j * 2 + m + 1)
                        dve.sem_inc(sc_free, 1)

                quarter_slopes()
                queries_lo(0)
                with dve.Fori(0, NDH) as j:
                    dve.wait_ge(tab, j + 2)
                    for i in range(TT + 2):
                        if i < TT:
                            n = (i + 1) * P
                            for m in range(2):
                                u = 2 * i + m
                                dve.wait_ge(sc_full, j * NU + u + 1)
                                if i >= 3:
                                    v = i - 3
                                    dve.wait_ge(tp_full, j * NT + v + second[v] + groups[v])
                                else:
                                    dve.wait_ge(pv_done, j * TT + 2)
                                dve.sem_inc(turn, 1)
                                dve.tensor_tensor_reduce(prob[u % 6][:, 0:n], sc[m][:, 0:n], g.tsel[:, SEQ - n:SEQ], -1.0, 3e38,
                                                         ALU.add, ALU.min, nmax[:, u:u + 1]).then_inc(biased, 1)
                                dve.wait_ge(biased, j * NU + u + 1)
                                dve.sem_inc(sc_free, 1)
                        if 0 < i <= TT:
                            v = i - 1
                            dve.wait_ge(p_full, j * NU + 2 * v + 2)
                            dve.reciprocal(share[:, v, :], total[:, 2 * v:2 * v + 2]).then_inc(shares, 1)
                            dve.wait_ge(shares, j * 2 * TT + 2 * v + 1)
                            dve.tensor_scalar(factor[:, v % 2:v % 2 + 1], share[:, v, 1:2], total[:, 2 * v:2 * v + 1], g.neglam[:, 0:1],
                                              ALU.mult, ALU.mult).then_inc(shares, 1)
                            dve.wait_ge(shares, j * 2 * TT + 2 * v + 2)
                            p0, p1 = (prob[2 * (v % 3) + m][:, 0:(v + 1) * P] for m in range(2))
                            dve.scalar_tensor_tensor(out=p0, in0=p1, scalar=factor[:, v % 2:v % 2 + 1], in1=p0,
                                                     op0=ALU.mult, op1=ALU.add).then_inc(joined, 1)
                        if i > 1 and groups[i - 2] == 2:
                            v = i - 2
                            dve.wait_ge(tp_full, j * NT + v + second[v] + 2)
                            dve.wait_ge(pv_done, j * TT + v + 1)
                            dve.tensor_copy(probT[v % 2][:, 4:v + 1, :].rearrange("p a b -> p (a b)"),
                                            tp[1][:, 0:(v - 3) * P]).then_inc(tp_dve, 1)
                    queries_lo(j + 1)
                    quarter_slopes()
                dve.wait_ge(o_free, NDH * TT + 2)
                dve.tensor_scalar(oss[:], oss[:], 1.0 / (2 * HD), EPS, ALU.mult, ALU.add).then_inc(shares, 1)
                dve.wait_ge(o_act, 1)
                dve.reciprocal(oss[:], oss[:]).then_inc(shares, 1)


T_SEL, T_DIF, T_WIN, T_CMP, T_SN, T_S, T_N, T_MAP, T_IDX, T_SUM, T_END = np.cumsum(
    [0, PAST + 1, PAST + 1, WINDOW + 1, 32, 4, 2, 2, 2, 15, 16]).tolist()


def decode_table():
    r = np.arange(16)
    t = np.zeros((16, T_END), np.float32)
    slope_a = 2.0 ** -(r % 8 + 1.0)
    slope_b = 2.0 ** (-2.0 * (r % 8 // 2 + 1))
    pos = np.arange(PAST + 1) - PAST
    t[:, T_SEL:T_DIF] = slope_a[:, None] * pos
    t[:, T_DIF:T_WIN] = slope_b[:, None] * pos
    t[:, T_WIN:T_CMP] = slope_a[:, None] * (np.arange(WINDOW + 1) - WINDOW)
    t[:, T_WIN] = NEG
    t[:, T_CMP:T_SN] = slope_a[:, None] * (32 * np.arange(32) + 31 - PAST)
    t[:, T_SN:T_S] = r[:, None] // 4 == np.arange(4)
    t[:, T_S:T_N] = r[:, None] // 8 == np.arange(2)
    t[:, T_N:T_MAP] = r[:, None] % 8 // 4 == np.arange(2)
    t[:, T_MAP:T_IDX] = r[:, None] % 2 == np.arange(2)
    t[:, T_IDX:T_SUM] = np.arange(1, 16)
    t[:, T_SUM:T_END] = r[:, None] // 8 == r[None, :] // 8
    return t


def decode_attention(nc, io, g):
    NP = NDEC // 2
    R = 16
    NW = WINDOW // P
    NY = 11
    with Scope(nc, "dec") as s:
        tab = s.sb("tab", [R, T_END])
        coef = s.sb("coef", [R, 1])
        ptab = s.sb("ptab", [1, NDEC * NPAGE], I32)
        kin = [s.sb(f"kin{i}", [P, 2, NPAGE, CACHE_W]) for i in range(2)]
        zc = lambda c, n: g.z[:, 0:TT, c:c + n]
        win = [s.sb("win0", [P, 2 * NW, 2 * HD])[:], zc(C_CK + CACHE_W, 2 * HD)]
        win = [w.rearrange("p (x t) c -> p x t c", x=2) for w in win]
        vnew = [s.sb(f"vnew{i}", [R, 6 * HD]) for i in range(2)]
        early = kin[1][0:NDEC].rearrange("p x t c -> p (x t c)")
        qs = [early[:, c:c + 2 * NH * HD].rearrange("p (h x d) -> p h x d", h=NH, x=2) for c in (0, 4096, 5120)]
        qdt = early[:, 1024:1024 + NH * HD].rearrange("p (h d) -> p h d", h=NH)
        kns = early[:, 2048:2048 + 6 * HD].rearrange("p (h d) -> p h d", h=6)
        knd = early[:, 3072:3072 + 4 * HD].rearrange("p (b x d) -> p b x d", b=2, x=2)
        nrs = s.sb("nrs", [NDEC, 6])
        qb = s.sb("qb", [P, 3, NP * R])
        qdb = s.sb("qdb", [P, NP, 4 * R])
        knT = s.sb("knT", [P, 2, NP])
        kndT = s.sb("kndT", [P, 2, NDEC])
        qc = s.sb("qc", [P, 3, R])
        qdc = s.sb("qdc", [P, 4 * R])
        sq = zc(C_CK, 6 * HD)
        sqw = zc(C_CK + 8 * HD, HD)
        rs = s.sb("rs", [P, 2, NPAGE, 6])
        rw = s.sb("rw", [P, 2, NW])
        nS = zc(C_CK + 6 * HD, 2 * HD).rearrange("p t (x d) -> p t x d", x=2)
        nW = g.z[:, 0:NW, C_CK + 9 * HD:C_CK + 11 * HD].rearrange("p t (x d) -> p t x d", x=2)
        nD = zc(C_CK, 4 * HD)
        kT = s.sb("kT", [P, 2, 512])
        kc = s.sb("kc", [32, 2, HD])
        kcq = s.sb("kcq", [32, 2, HD])
        kcr = s.sb("kcr", [32, 2])
        vc = [s.sb(f"vc{i}", [32, 2, HD]) for i in range(2)]
        kcT = s.sb("kcT", [P, 32])
        pS = s.sb("pS", [R, PAST + 1])
        pD = s.sb("pD", [R, PAST + 1])
        pW = g.z[0:R, TT, C_CK:C_CK + WINDOW + 1]
        pC = s.sb("pC", [R, 32])
        st = s.sb("st", [R, 16])
        imp = s.sb("imp", [R, 16])
        low = s.sb("low", [R, 16])
        pT = s.sb("pT", [P, 21, R])
        o16 = s.sb("o16", [R, 5 * HD])
        od = kin[0][0:NDEC].rearrange("p x t c -> p (x t c)")[:, 0:NH * 5 * HD].rearrange("p (h c) -> p h c", h=NH)
        kt = s.ps("kt", [P, 2, 512])
        ss = s.ps("ss", [R, PAST])
        sd = s.ps("sd", [R, PAST])
        ma = s.ps("ma", [P, 512])
        mb = s.ps("mb", [P, 512])
        ckp = nS
        kin_in, win_in = [s.sem(f"kin_in{i}") for i in range(2)], [s.sem(f"win_in{i}") for i in range(2)]
        vnew_in = [s.sem(f"vnew_in{i}") for i in range(2)]
        row_d, t_in = s.sem("row_d"), s.sem("t_in")
        chain, pre, pre_ps, roots = s.sem("chain"), s.sem("pre"), s.sem("pre_ps"), s.sem("roots")
        pt_in = s.sem("pt_in")

        pv, slot_free = s.sem("pv"), s.sem("slot_free")

        def load_pair(sp, p):
            j = p % 2
            if p >= 2:
                sp.wait_ge(pv, p - 1)
            for x in range(2):
                b = 2 * p + x
                for pg in range(NPAGE):
                    n = b * NPAGE + pg
                    page = sp.value_load(ptab[0:1, n:n + 1], min_val=0, max_val=io["cache_kv"].shape[1] - 1)
                    sp.dma_start(kin[j][:, x, pg, :], io["cache_kv"][0, ds(page, 1)].rearrange("a p c -> (a p) c")
                                 ).then_inc(kin_in[j], 16)
                sp.dma_start(win[j][:, x], io["state_win_kv"][0, b].rearrange("(t p) c -> p t c", p=P)).then_inc(win_in[j], 16)
            if p >= 2:
                sp.wait_ge(slot_free, p - 1)
            for x in range(2):
                new = io["new_d"][2 * p + x:2 * p + x + 1, :]
                rr = slice(8 * x, 8 * x + 8)
                sp.dma_start(vnew[j][rr, 0:HD], new[:, C_SV - C_CK:C_DK - C_CK].broadcast_to([8, HD])).then_inc(vnew_in[j], 16)
                sp.dma_start(vnew[j][rr, HD:2 * HD], new[:, C_WV - C_CK:C_G - C_CK].broadcast_to([8, HD])).then_inc(vnew_in[j], 16)
                sp.dma_start(vnew[j][rr, 2 * HD:6 * HD], new[:, C_DV - C_CK:C_WK - C_CK].broadcast_to([8, 4 * HD])).then_inc(vnew_in[j], 16)

        with nc.Block() as block:

            @block.sync
            def _(sp):
                sp.dma_start(tab[:], io["dec_tab"]).then_inc(t_in, 16)
                sp.dma_start(ptab[:], io["page_table"].rearrange("b n -> (b n)").unsqueeze(0)).then_inc(pt_in, 16)
                sp.dma_start(io["new_d"], g.z[0:NDEC, TT, C_CK:C_G]).then_inc(row_d, 16)
                sp.wait_ge(row_d, 16)
                sp.wait_ge(pt_in, 16)
                load_pair(sp, 0)
                sp.wait_ge(t_in, 16)

            @block.vector
            def _(dve):
                n = [0]

                def link(ins):
                    n[0] += 1
                    ins.then_inc(chain, 1)
                    dve.wait_ge(chain, n[0])

                dve.wait_ge(t_in, 16)
                zrow = lambda c, k: g.z[0:NDEC, TT, c:c + k * HD].rearrange("p (a b) -> p a b", b=HD)
                groups = [(0, C_SK, 1), (1, C_DK, 4), (5, C_WK, 1)]
                for o, c, k in groups:
                    ins = dve.tensor_tensor(kns[:, o:o + k, :], zrow(c, k), zrow(c, k), ALU.mult)
                link(ins)
                link(dve.tensor_reduce(nrs[:], kns[:], AX.X, ALU.add))
                link(dve.tensor_scalar(nrs[:], nrs[:], 1.0 / HD, EPS, ALU.mult, ALU.add))
                dve.sem_inc(pre, 1)
                q = zrow(C_QN, NH)
                both = lambda a, k: a.unsqueeze(2).broadcast_to([NDEC, k, 2, HD])
                for b in range(3):
                    if b < 2:
                        dve.tensor_tensor(qs[b], both(q, NH), g.gain[0:NDEC, 2 + b:3 + b, :].unsqueeze(2).broadcast_to([NDEC, NH, 2, HD]), ALU.mult)
                    else:
                        dve.tensor_copy(qs[b], both(q, NH))
                link(dve.tensor_tensor(qdt, zrow(C_QD, 8), g.gain[0:NDEC, 4:5, :].broadcast_to([NDEC, 8, HD]), ALU.mult))
                dve.sem_inc(pre, 1)
                dve.wait_ge(roots, 1)
                link(dve.reciprocal(nrs[:], nrs[:]))
                for o, c, k in groups:
                    ins = dve.tensor_tensor(kns[:, o:o + k, :], zrow(c, k), nrs[:, o:o + k].unsqueeze(2).broadcast_to([NDEC, k, HD]), ALU.mult)
                link(ins)
                for b, o in enumerate((0, 5)):
                    ins = dve.tensor_copy(knd[:, b], kns[:, o:o + 1, :].broadcast_to([NDEC, 2, HD]))
                link(ins)
                dve.sem_inc(pre, 1)
                dve.memset(qb[:], 0.0)
                link(dve.memset(qdb[:], 0.0))
                dve.scalar_tensor_tensor(out=coef[:], in0=tab[:, T_MAP + 1:T_MAP + 2], scalar=g.neglam[0:R, 0:1],
                                         in1=tab[:, T_MAP:T_MAP + 1], op0=ALU.mult, op1=ALU.add)
                dve.wait_ge(pre_ps, 1)
                for b in range(3):
                    src = ma[:, b * NH * NDEC:(b + 1) * NH * NDEC].rearrange("p (h w x) -> p w x h", h=NH, x=2)
                    dst = qb[:, b, :].rearrange("p (w x h) -> p w x h", x=2, h=NH)
                    for x in range(2):
                        rr = slice(HD * x, HD * x + HD)
                        dve.tensor_copy(dst[rr, :, x, :], src[rr, :, x, :])
                src = ma[:, 3 * NH * NDEC:(3 * NH + 4) * NDEC].rearrange("p (n g w x) -> p n w x g", n=2, g=2, x=2)
                dst = qdb[:].rearrange("p w (c k) -> p w c k", c=4)
                for x in range(2):
                    for nn in range(2):
                        for m in range(2):
                            rr = slice(HD * m, HD * m + HD)
                            c0 = x * 8 + nn * 4 + m
                            dve.tensor_copy(dst[rr, :, 2 * x + nn, c0:c0 + 3:2], src[rr, nn, :, x, :])
                dve.wait_ge(pre_ps, 2)
                for b in range(2):
                    for x in range(2):
                        rr = slice(HD * x, HD * x + HD)
                        src = mb[rr, b * NDEC:(b + 1) * NDEC].rearrange("p (w x) -> p w x", x=2)
                        dve.tensor_copy(knT[rr, b, :], src[:, :, x])
                link(dve.tensor_copy(kndT[:], mb[:, 2 * NDEC:4 * NDEC].rearrange("p (a b) -> p a b", a=2)))

            @block.scalar
            def _(act):
                act.wait_ge(pre, 1)
                act.activation(nrs[:], nrs[:], ACT.Sqrt).then_inc(roots, 1)

            @block.tensor
            def _(pe):
                idn = g.ident[0:NDEC, 0:NDEC]
                pe.wait_ge(pre, 2)
                for b in range(3):
                    for h in range(NH):
                        at = (b * NH + h) * NDEC
                        pe.transpose(ma[:, at:at + NDEC], qs[b][:, h].rearrange("p a b -> p (a b)"), idn)
                for h in range(4):
                    at = (3 * NH + h) * NDEC
                    mm = pe.transpose(ma[:, at:at + NDEC], qdt[:, 2 * h:2 * h + 2, :].rearrange("p a b -> p (a b)"), idn)
                mm.then_inc(pre_ps, 1)
                pe.wait_ge(pre, 3)
                for b in range(2):
                    pe.transpose(mb[:, b * NDEC:(b + 1) * NDEC], knd[:, b].rearrange("p a b -> p (a b)"), idn)
                for nn in range(2):
                    mm = pe.transpose(mb[:, (2 + nn) * NDEC:(3 + nn) * NDEC], kns[:, 1 + 2 * nn:3 + 2 * nn, :].rearrange("p a b -> p (a b)"), idn)
                mm.then_inc(pre_ps, 1)

        with nc.Block() as block:
            (sq_done, sum_done, root_done, nS_done, nD_done, nW_done, ck_done, kc_ps, kc_done, kcT_ps, kcT_sb, kt_full, kt_sb,
             kt_used, s_full, ss_read, masked, exps, pc_done, imp_ps, pT_ps, pT_sb, o_done, q_cur, chain2) = (
                s.sem(x) for x in ("sq_done", "sum_done", "root_done", "nS_done", "nD_done", "nW_done", "ck_done", "kc_ps",
                                   "kc_done", "kcT_ps", "kcT_sb", "kt_full", "kt_sb", "kt_used", "s_full", "ss_read", "masked",
                                   "exps", "pc_done", "imp_ps", "pT_ps", "pT_sb", "o_done", "q_cur", "chain2"))
            o_out, o_norm = s.pool_sem("o_out"), s.sem("o_norm")

            @block.sync
            def _(sp):
                for p in range(1, NP):
                    load_pair(sp, p)

            @block.gpsimd
            def _(pool):
                o = g.z[:, 0:TT, C_QD:C_M].rearrange("p t (j v) -> p t j v", j=NDH)
                r4 = g.oss[:].rearrange("p (t j) -> p t j", t=TT).unsqueeze(3).broadcast_to([P, TT, NDH, 2 * HD])
                pool.tensor_tensor(o, o, r4, ALU.mult).then_inc(o_norm, 1)
                pool.wait_ge(o_norm, 1)
                for j in range(NDH):
                    oj = g.z[:, 0:TT, C_QD + j * 2 * HD:C_QD + (j + 1) * 2 * HD]
                    pool.tensor_tensor(oj, oj, g.subln[:].unsqueeze(1).broadcast_to([P, TT, 2 * HD]), ALU.mult).then_inc(o_norm, 1)
                for p in range(NP):
                    pool.wait_ge(o_done, p + 1)
                    pool.dma_start(io["dec_d"][p * R:(p + 1) * R, :], o16[:]).then_inc(o_out, 16)
                    pool.wait_ge(o_out, p * 16 + 16)

            @block.scalar
            def _(act):

                def squares(p, xs):
                    i, j = p // 2, p % 2
                    for x in xs:
                        if x == 0:
                            act.wait_ge(kin_in[j], i * 256 + 256)
                        else:
                            act.wait_ge(sum_done, p * 3 + 1)
                        act.activation(sq, kin[j][:, x, :, C_SK - C_CK:C_DV - C_CK], ACT.Square).then_inc(sq_done, 1)
                    if 1 not in xs:
                        return
                    act.wait_ge(win_in[j], i * 32 + 32)
                    act.activation(sqw, win[j][:, :, :, 0:HD].rearrange("p a b c -> p (a b) c"), ACT.Square).then_inc(sq_done, 1)
                    act.wait_ge(sum_done, p * 3 + 3)
                    act.activation(rs[:], rs[:], ACT.Sqrt).then_inc(root_done, 1)
                    act.activation(rw[:], rw[:], ACT.Sqrt).then_inc(root_done, 1)

                def root_compressed(p):
                    i, j = p // 2, p % 2
                    act.wait_ge(kc_done, p * 3 + 1)
                    act.activation(kcr[:], kcr[:], ACT.Sqrt).then_inc(root_done, 1)

                def middle(p):
                    i, j = p // 2, p % 2
                    for y in range(NY):
                        at = p * NY + y
                        act.wait_ge(kt_full, at + 1)
                        if at >= 2:
                            act.wait_ge(kt_used, at - 1)
                        act.activation(kT[:, at % 2, :], kt[:, at % 2, :], ACT.Copy).then_inc(kt_sb, 1)
                        if y == 0:
                            act.wait_ge(kcT_ps, p + 1)
                            act.activation(kcT[:], ma[:, 4 * HD:4 * HD + 32], ACT.Copy).then_inc(kcT_sb, 1)
                        if y == 5:
                            act.wait_ge(masked, p * 4 + 1)
                            act.activation(pC[:], pC[:], ACT.Exp, bias=st[:, 0:1], scale=1.0, accum_out=st[:, 4:5]).then_inc(exps, 1)
                    for x, t in enumerate((pS[:], pD[:], pW)):
                        act.wait_ge(masked, p * 4 + x + 2)
                        act.activation(t, t, ACT.Exp, bias=st[:, x + 1:x + 2], scale=1.0,
                                       accum_out=st[:, x + 5:x + 6]).then_inc(exps, 1)

                def evacuate(p):
                    i, j = p // 2, p % 2
                    act.wait_ge(pT_ps, p + 1)
                    act.activation(pT[:, 0:20, :].rearrange("p a b -> p (a b)"), mb[:, 0:20 * R], ACT.Copy).then_inc(pT_sb, 1)
                    act.activation(pT[0:32, 20, :], mb[0:32, 20 * R:21 * R], ACT.Copy).then_inc(pT_sb, 1)

                squares(0, (0, 1))
                root_compressed(0)
                for p in range(NP):
                    middle(p)
                    if p + 1 < NP:
                        squares(p + 1, (0,))
                    evacuate(p)
                    if p + 1 < NP:
                        squares(p + 1, (1,))
                        root_compressed(p + 1)

            @block.tensor
            def _(pe):

                def compress(p):
                    i, j = p // 2, p % 2
                    pe.wait_ge(ck_done, p + 1)
                    for t in range(NPAGE):
                        mm = pe.matmul(ma[0:32, 0:2 * HD], g.wcmp[:, 0, 28 - 4 * t:60 - 4 * t],
                                       ckp[:, t].rearrange("p a b -> p (a b)"), start=(t == 0), stop=(t == NPAGE - 1))
                    for t in range(NPAGE):
                        mm = pe.matmul(ma[0:32, 2 * HD:4 * HD], g.wcmp[:, 1, 28 - 4 * t:60 - 4 * t],
                                       kin[j][:, :, t, C_CV - C_CK:C_SK - C_CK], start=(t == 0), stop=(t == NPAGE - 1))
                    mm.then_inc(kc_ps, 1)

                def scores(p):
                    i, j = p // 2, p % 2
                    def transposed(y):
                        at = p * NY + y
                        if at >= 2:
                            pe.wait_ge(kt_sb, at - 1)
                        x, c = (y - 2) // 2, y % 2
                        if y < 2:
                            src = nS.rearrange("p t a b -> p t (a b)")
                            pe.wait_ge(nS_done, p + 1)
                        elif y < 10:
                            src = nD[:, :, x % 2 * P:(x % 2 + 1) * P]
                            pe.wait_ge(nD_done, p * 2 + x // 2 + 1)
                        else:
                            src = nW.rearrange("p t a b -> p t (a b)")
                            pe.wait_ge(nW_done, p + 1)
                        for q in range(4):
                            mm = pe.transpose(kt[:, at % 2, q * P:(q + 1) * P], src[:, c * 4 + q], g.ident[:])
                        mm.then_inc(kt_full, 1)

                    def score(y):
                        at = p * NY + y
                        x, c = (y - 2) // 2, y % 2
                        pe.wait_ge(kt_sb, at + 1)
                        if y < 2:
                            out, q, first, last = ss[:, c * 512:(c + 1) * 512], qc[:, 0, :], True, True
                        elif y < 10:
                            out, q, first, last = sd[:, c * 512:(c + 1) * 512], qdc[:, x * R:(x + 1) * R], x == 0, x == 3
                        else:
                            out, q, first, last = ss[:, 0:WINDOW], qc[:, 1, :], True, True
                        if y == 2 and p:
                            pe.wait_ge(o_done, p)
                        pe.matmul(out, q, kT[:, at % 2, :], start=first, stop=last, skip_group_check=True).then_inc(kt_used, 1)

                    transposed(0)
                    pe.wait_ge(kc_done, p * 3 + 3)
                    pe.matmul(ma[:, 4 * HD:4 * HD + 32], kc[:].rearrange("p a b -> p (a b)"), g.ident[0:32, 0:32], start=True,
                              stop=True).then_inc(kcT_ps, 1)
                    transposed(1)
                    pe.wait_ge(kcT_sb, p + 1)
                    pe.wait_ge(q_cur, p + 1)
                    pe.matmul(ma[0:R, 288:320], qc[:, 2, :], kcT[:], start=True, stop=True).then_inc(s_full, 1)
                    score(0)
                    for y in range(2, NY):
                        transposed(y)
                        score(y - 1)
                        if y == 7:
                            pe.wait_ge(pc_done, p + 1)
                            pe.matmul(ma[0:R, 320:321], qc[:, 0, :], knT[:, 0, p:p + 1], start=True, stop=True).then_inc(s_full, 1)
                            pe.matmul(ma[0:R, 324:356], tab[:, T_SUM:T_END], pC[:], start=True, stop=True).then_inc(imp_ps, 1)
                    pe.wait_ge(ss_read, p + 1)
                    for x in range(4):
                        mm = pe.matmul(ma[0:R, 322:323], qdc[:, x * R:(x + 1) * R], kndT[:, x % 2, p * 2 + x // 2:p * 2 + x // 2 + 1],
                                       start=(x == 0), stop=(x == 3))
                    pe.matmul(ma[0:R, 321:322], qc[:, 1, :], knT[:, 1, p:p + 1], start=True, stop=True).then_inc(s_full, 1)
                    score(NY - 1)
                    pe.wait_ge(kt_used, (p + 1) * NY)
                    pe.sem_inc(s_full, 1)

                def outputs(p):
                    i, j = p // 2, p % 2
                    idr = g.ident[0:R, 0:R]
                    for x, (src, n0, n) in enumerate(((pS, 0, 8), (pD, 8, 8), (pW, 16, 4))):
                        pe.wait_ge(exps, p * 4 + x + 2)
                        for t in range(n):
                            pe.transpose(mb[:, (n0 + t) * R:(n0 + t + 1) * R], src[:, t * P:(t + 1) * P], idr)
                    pe.transpose(mb[0:32, 20 * R:21 * R], pC[:], idr).then_inc(pT_ps, 1)
                    pe.wait_ge(pT_sb, p * 2 + 2)
                    for t in range(NPAGE):
                        pe.matmul(sd[0:R, 512:640], pT[:, t, :], kin[j][:, :, t, C_SV - C_CK:C_DK - C_CK],
                                  start=(t == 0), stop=(t == NPAGE - 1))
                    for t in range(NPAGE):
                        pe.matmul(sd[0:R, 0:512], pT[:, 8 + t, :], kin[j][:, :, t, C_DV - C_CK:CACHE_W],
                                  start=(t == 0), stop=(t == NPAGE - 1))
                    for t in range(NW):
                        pe.matmul(sd[0:R, 640:768], pT[:, 16 + t, :], win[j][:, :, t, HD:2 * HD],
                                  start=(t == 0), stop=(t == NW - 1))
                    pe.matmul(sd[0:R, 768:896], pT[0:32, 20, :], vc[j][:].rearrange("p a b -> p (a b)"), start=True, stop=True
                              ).then_inc(pv, 1)

                compress(0)
                for p in range(NP):
                    scores(p)
                    if p + 1 < NP:
                        compress(p + 1)
                    outputs(p)

            @block.vector
            def _(dve):
                n = [0]

                def link(ins):
                    n[0] += 1
                    ins.then_inc(chain2, 1)
                    dve.wait_ge(chain2, n[0])

                def norm_diff(p, x):
                    j = p % 2
                    kd = kin[j][:, x, :, C_DK - C_CK:C_DV - C_CK].rearrange("p a (b c) -> p a b c", c=HD)
                    dve.tensor_tensor(nD.rearrange("p a (b c) -> p a b c", c=HD), kd,
                                      rs[:, x, :, 2:6].unsqueeze(3).broadcast_to([P, NPAGE, 4, HD]), ALU.mult).then_inc(nD_done, 1)

                def front(p):
                    i, j = p // 2, p % 2

                    dve.tensor_copy(qc[:], qb[:, :, p * R:(p + 1) * R])
                    dve.tensor_copy(qdc[:], qdb[:, p, :]).then_inc(q_cur, 1)
                    dve.wait_ge(kin_in[j], i * 256 + 256)
                    for x in range(2):
                        ins = dve.tensor_tensor(ckp[:, :, x, :], kin[j][:, x, :, 0:HD],
                                                g.pe4[:].unsqueeze(1).broadcast_to([P, NPAGE, HD]), ALU.add)
                    ins.then_inc(ck_done, 1)
                    for x in range(2):
                        dve.wait_ge(sq_done, p * 3 + x + 1)
                        dve.tensor_reduce(rs[:, x], sq.rearrange("p a (b c) -> p a b c", c=HD), AX.X, ALU.add).then_inc(sum_done if x == 0 else chain2, 1)
                    n[0] += 1
                    dve.wait_ge(sq_done, p * 3 + 3)
                    link(dve.tensor_reduce(rw[:].rearrange("p a b -> p (a b)"), sqw, AX.X, ALU.add))
                    dve.tensor_scalar(rs[:], rs[:], 1.0 / HD, EPS, ALU.mult, ALU.add).then_inc(sum_done, 1)
                    dve.tensor_scalar(rw[:], rw[:], 1.0 / HD, EPS, ALU.mult, ALU.add).then_inc(sum_done, 1)
                    dve.wait_ge(kc_ps, p + 1)
                    link(dve.tensor_copy(kc[:], ma[0:32, 0:2 * HD].rearrange("p (a b) -> p a b", a=2)))
                    link(dve.tensor_copy(vc[j][:], ma[0:32, 2 * HD:4 * HD].rearrange("p (a b) -> p a b", a=2)))
                    link(dve.tensor_tensor(kcq[:], kc[:], kc[:], ALU.mult))
                    link(dve.tensor_reduce(kcr[:], kcq[:], AX.X, ALU.add))
                    dve.tensor_scalar(kcr[:], kcr[:], 1.0 / HD, EPS, ALU.mult, ALU.add).then_inc(kc_done, 1)
                    dve.wait_ge(root_done, p * 3 + 2)
                    link(dve.reciprocal(rs[:], rs[:]))
                    link(dve.reciprocal(rw[:], rw[:]))
                    for x in range(2):
                        ins = dve.tensor_tensor(nS[:, :, x, :], kin[j][:, x, :, C_SK - C_CK:C_SV - C_CK],
                                                rs[:, x, :, 0:1].broadcast_to([P, NPAGE, HD]), ALU.mult)
                    ins.then_inc(nS_done, 1)

                    norm_diff(p, 0)
                    for x in range(2):
                        ins = dve.tensor_tensor(nW[:, :, x, :], win[j][:, x, :, 0:HD],
                                                rw[:, x, :].unsqueeze(2).broadcast_to([P, NW, HD]), ALU.mult)
                    ins.then_inc(nW_done, 1)

                def compressed_keys(p):
                    i, j = p // 2, p % 2
                    dve.wait_ge(root_done, p * 3 + 3)
                    link(dve.reciprocal(kcr[:], kcr[:]))
                    dve.tensor_tensor(kc[:], kc[:], kcr[:].unsqueeze(2).broadcast_to([32, 2, HD]), ALU.mult).then_inc(kc_done, 1)
                    dve.wait_ge(kc_done, p * 3 + 2)
                    dve.tensor_tensor(kc[:], kc[:], g.gain[0:32, 1:2, :].broadcast_to([32, 2, HD]), ALU.mult).then_inc(kc_done, 1)

                def middle(p):
                    i, j = p // 2, p % 2
                    dve.wait_ge(s_full, p * 4 + 1)
                    link(dve.tensor_tensor(pC[:], ma[0:R, 288:320], tab[:, T_CMP:T_SN], ALU.add))
                    dve.tensor_reduce(st[:, 0:1], pC[:], AX.X, ALU.max, negate=True).then_inc(masked, 1)
                    dve.wait_ge(kt_full, p * NY + 6)
                    norm_diff(p, 1)
                    dve.wait_ge(exps, p * 4 + 1)
                    link(dve.reciprocal(st[:, 8:9], st[:, 4:5]))
                    dve.tensor_scalar(pC[:], pC[:], st[:, 8:9], None, ALU.mult).then_inc(pc_done, 1)
                    dve.wait_ge(imp_ps, p + 1)
                    link(dve.tensor_reduce(imp[:], ma[0:R, 324:356].rearrange("p (a b) -> p a b", b=2), AX.X, ALU.add))
                    link(dve.tensor_reduce(st[:, 9:10], imp[:, 1:16], AX.X, ALU.min))
                    link(dve.tensor_scalar(low[:, 1:16], imp[:, 1:16], st[:, 9:10], None, ALU.is_equal))
                    link(dve.tensor_tensor(low[:, 1:16], low[:, 1:16], tab[:, T_IDX:T_SUM], ALU.mult))
                    link(dve.tensor_reduce(st[:, 10:11], low[:, 1:16], AX.X, ALU.max))
                    link(dve.memset(low[:, 0:1], 0.0))
                    link(dve.tensor_scalar(low[:, 1:16], tab[:, T_IDX:T_SUM], st[:, 10:11], NEG, ALU.is_equal, ALU.mult))
                    dve.wait_ge(s_full, p * 4 + 2)
                    link(dve.tensor_tensor(pS[:, PAST:PAST + 1], ma[0:R, 320:321], tab[:, T_DIF - 1:T_DIF], ALU.add))
                    dve.tensor_tensor(pS[:, 0:PAST], ss[:], tab[:, T_SEL:T_DIF - 1], ALU.add).then_inc(ss_read, 1)
                    dve.wait_ge(ss_read, p + 1)
                    blk = pS[:, 0:PAST].rearrange("p (a b) -> p a b", b=HD)
                    link(dve.tensor_tensor(blk, blk, low[:].unsqueeze(2).broadcast_to([R, 16, HD]), ALU.add))
                    dve.tensor_reduce(st[:, 1:2], pS[:], AX.X, ALU.max, negate=True).then_inc(masked, 1)
                    dve.wait_ge(s_full, p * 4 + 3)
                    link(dve.tensor_tensor(pD[:, PAST:PAST + 1], ma[0:R, 322:323], tab[:, T_WIN - 1:T_WIN], ALU.add))
                    link(dve.tensor_tensor(pD[:, 0:PAST], sd[:], tab[:, T_DIF:T_WIN - 1], ALU.add))
                    dve.tensor_reduce(st[:, 2:3], pD[:], AX.X, ALU.max, negate=True).then_inc(masked, 1)
                    dve.wait_ge(s_full, p * 4 + 4)
                    link(dve.tensor_tensor(pW[:, WINDOW:WINDOW + 1], ma[0:R, 321:322], tab[:, T_CMP - 1:T_CMP], ALU.add))
                    link(dve.tensor_tensor(pW[:, 0:WINDOW], ss[:, 0:WINDOW], tab[:, T_WIN:T_CMP - 1], ALU.add))
                    dve.tensor_reduce(st[:, 3:4], pW, AX.X, ALU.max, negate=True).then_inc(masked, 1)

                def outputs(p):
                    i, j = p // 2, p % 2
                    dve.wait_ge(exps, p * 4 + 4)
                    link(dve.reciprocal(st[:, 11:14], st[:, 5:8]))
                    link(dve.tensor_tensor(st[:, 12:13], st[:, 12:13], coef[:], ALU.mult))
                    dve.wait_ge(vnew_in[j], i * 96 + 96)
                    dve.wait_ge(pv, p + 1)
                    if p:
                        dve.wait_ge(o_out, p * 16)

                    def add(o, a, sc, first=False):
                        if first:
                            link(dve.tensor_scalar(o, a, sc, None, ALU.mult))
                        else:
                            link(dve.scalar_tensor_tensor(out=o, in0=a, scalar=sc, in1=o, op0=ALU.mult, op1=ALU.add))

                    for b, c in enumerate((512, 640, 768)):
                        o = o16[:, b * HD:(b + 1) * HD]
                        for x in range(2):
                            add(o, sd[0:R, c + x * HD:c + (x + 1) * HD], tab[:, T_S + x:T_S + x + 1], x == 0)
                        if b < 2:
                            pn = pS[:, PAST:PAST + 1] if b == 0 else pW[:, WINDOW:WINDOW + 1]
                            add(o, vnew[j][:, b * HD:(b + 1) * HD], pn)
                            link(dve.tensor_scalar(o, o, st[:, 11 + 2 * b:12 + 2 * b], None, ALU.mult))
                    o = o16[:, 3 * HD:5 * HD]
                    for x in range(4):
                        add(o, sd[0:R, x * 2 * HD:(x + 1) * 2 * HD], tab[:, T_SN + x:T_SN + x + 1], x == 0)
                    for nn in range(2):
                        link(dve.tensor_tensor(st[:, 14 + nn:15 + nn], pD[:, PAST:PAST + 1], tab[:, T_N + nn:T_N + nn + 1], ALU.mult))
                        add(o, vnew[j][:, 2 * HD * (1 + nn):2 * HD * (2 + nn)], st[:, 14 + nn:15 + nn])
                    dve.tensor_scalar(o, o, st[:, 12:13], None, ALU.mult).then_inc(o_done, 1)
                    dve.sem_inc(slot_free, 1)

                front(0)
                compressed_keys(0)
                for p in range(NP):
                    middle(p)
                    if p + 1 < NP:
                        front(p + 1)
                        compressed_keys(p + 1)
                    outputs(p)

        with nc.Block() as block:
            od_in, chain3, root = s.sem("od_in"), s.sem("chain3"), s.sem("root")
            dsq = g.z[0:NDEC, TT, C_CK:C_CK + NDH * 2 * HD].rearrange("p (j v) -> p j v", j=NDH)

            @block.sync
            def _(sp):
                sp.dma_start(od, io["dec_d"].rearrange("(b r) c -> b r c", r=8)).then_inc(od_in, 16)

            @block.scalar
            def _(act):
                act.wait_ge(root, 1)
                act.activation(nrs[:, 0:NDH], nrs[:, 0:NDH], ACT.Sqrt).then_inc(root, 1)

            @block.vector
            def _(dve):
                n = [0]

                def link(ins):
                    n[0] += 1
                    ins.then_inc(chain3, 1)
                    dve.wait_ge(chain3, n[0])

                dve.wait_ge(od_in, 16)
                qo = g.z[0:NDEC, TT, C_QN:C_CK].rearrange("p (a b) -> p a b", b=HD)
                for b, gate in enumerate((1, 2, 0)):
                    gb = g.G[0:NDEC, TT, gate:24:3].unsqueeze(2).broadcast_to([NDEC, NH, HD])
                    part = od[:, :, b * HD:(b + 1) * HD]
                    if b == 0:
                        link(dve.tensor_tensor(qo, part, gb, ALU.mult))
                    else:
                        link(dve.tensor_tensor(part, part, gb, ALU.mult))
                        link(dve.tensor_tensor(qo, qo, part, ALU.add))
                do = g.z[0:NDEC, TT, C_QD:C_M].rearrange("p (j v) -> p j v", j=NDH)
                ov = od.rearrange("p (j m) c -> p j m c", m=2)
                link(dve.tensor_tensor(do, ov[:, :, 0, 3 * HD:5 * HD], ov[:, :, 1, 3 * HD:5 * HD], ALU.add))
                link(dve.tensor_tensor(dsq, do, do, ALU.mult))
                link(dve.tensor_reduce(nrs[:, 0:NDH], dsq, AX.X, ALU.add))
                dve.tensor_scalar(nrs[:, 0:NDH], nrs[:, 0:NDH], 1.0 / (2 * HD), EPS, ALU.mult, ALU.add).then_inc(root, 1)
                dve.wait_ge(root, 2)
                link(dve.reciprocal(nrs[:, 0:NDH], nrs[:, 0:NDH]))
                link(dve.tensor_tensor(do, do, nrs[:, 0:NDH].unsqueeze(2).broadcast_to([NDEC, NDH, 2 * HD]), ALU.mult))
                link(dve.tensor_tensor(do, do, g.subln[0:NDEC].unsqueeze(1).broadcast_to([NDEC, NDH, 2 * HD]), ALU.mult))


def merge_branches(nc, io, g):
    KB = NH * HD // P
    with Scope(nc, "br") as s:
        raw = [s.sb(f"raw{i}", [P, 2 * KB, P]) for i in range(2)]
        whi = [s.sb(f"whi{i}", [P, 2 * KB, P], F32R) for i in range(2)]
        wlo = [s.sb(f"wlo{i}", [P, 2 * KB, P], F32R) for i in range(2)]
        late = g.x2[:].rearrange("p t d -> p (t d)")
        gate = [late[:, i * 2 * NTOK:(i + 1) * 2 * NTOK].rearrange("p (b t) -> p b t", b=2) for i in range(2)]
        acc = [s.ps(f"acc{i}", [P, 512]) for i in range(6)]
        m_hi, m_lo = g.words_hi, g.words_lo
        w_in, gate_in = [s.sem(f"w_in{i}") for i in range(2)], [s.sem(f"gate_in{i}") for i in range(2)]
        oT_ps, oT_hi_done, oT_split = s.sem("oT_ps"), s.sem("oT_hi_done"), s.sem("oT_split")
        cols = [C_QN + k * P for k in range(KB)] + [C_QD + k * P for k in range(KB)]
        NU = 4 * KB + 1
        raw_free, w_hi, w_lo, w_free = s.sem("raw_free"), s.sem("w_hi"), s.sem("w_lo"), s.sem("w_free")
        gate_free = s.sem("gate_free")
        acc_full, prod, merged, m_hi_done, m_split = (s.sem(x) for x in ("acc_full", "prod", "merged", "m_hi_done", "m_split"))
        w_a = io["w_br_nsa"][0].rearrange("(k p) n -> p k n", p=P)
        w_b = io["w_br_diff"][0].rearrange("(k p) n -> p k n", p=P)
        wo = io["w_out"][0].rearrange("(k p) n -> p k n", p=P)
        gate_v = io["gate_d"].rearrange("(b r) t -> r b t", b=2)

        def oT(u):
            if u < NU - 1:
                half = slice(u % 2 * 512, u % 2 * 512 + 512)
                return acc[u % 6][:], g.oT_hi[:, u // 2, half], g.oT_lo[:, u // 2, half]
            return (acc[u % 6][:, 0:2 * KB * NDEC].rearrange("p (k t) -> p k t", k=2 * KB), g.oT_hi[:, :, SEQ:NTOK],
                    g.oT_lo[:, :, SEQ:NTOK])

        with nc.Block() as block:

            @block.sync
            def _(sp):
                with sp.Fori(0, KD // 2) as i:
                    for j in range(2):
                        n = i * 2 + j
                        sp.wait_ge(raw_free, n + 1)
                        sp.dma_start(raw[j][:, 0:KB, :], w_a[:, :, ds(n * P, P)]).then_inc(w_in[j], 16)
                        sp.dma_start(raw[j][:, KB:2 * KB, :], w_b[:, :, ds(n * P, P)]).then_inc(w_in[j], 16)
                        sp.wait_ge(gate_free, n + 1)
                        sp.dma_start(gate[j], gate_v[ds(n * P, P), :, :]).then_inc(gate_in[j], 16)

                for i in range(2):
                    sp.dma_start(g.wo_raw[i][:], wo[:, :, i * 256:(i + 1) * 256]).then_inc(g.wo_in[i], 16)

            @block.scalar
            def _(act):
                for u in range(NU):
                    act.wait_ge(oT_ps, u + 1)
                    act.activation(oT(u)[1], oT(u)[0], ACT.Copy).then_inc(oT_hi_done, 1)

            @block.tensor
            def _(pe):
                for u in range(NU):
                    if u >= 6:
                        pe.wait_ge(oT_split, u - 5)
                    if u < NU - 1:
                        for q in range(4):
                            mm = pe.transpose(acc[u % 6][:, q * P:(q + 1) * P], g.z[:, u % 2 * 4 + q, cols[u // 2]:cols[u // 2] + P], g.ident[:])
                    else:
                        for k in range(2 * KB):
                            mm = pe.transpose(acc[u % 6][:, k * NDEC:(k + 1) * NDEC], g.z[0:NDEC, TT, cols[k]:cols[k] + P],
                                              g.ident[0:NDEC, 0:NDEC])
                    mm.then_inc(oT_ps, 1)
                pe.wait_ge(oT_split, NU)
                with pe.Fori(0, KD // 2) as i:
                    for j in range(2):
                        n = i * 2 + j
                        pe.wait_ge(w_lo, n + 1)
                        for c in range(3):
                            tok = slice(c * TCH, (c + 1) * TCH)
                            pe.wait_ge(prod, n * 6 + c * 2 + 2)
                            for b in range(2):
                                for k in range(b * KB, (b + 1) * KB):
                                    for q, (w, o) in enumerate(((whi, g.oT_hi), (wlo, g.oT_hi), (whi, g.oT_lo))):
                                        mm = pe.matmul(acc[c * 2 + b][:, 0:TCH], w[j][:, k, :], o[:, k, tok],
                                                       start=(k == b * KB and q == 0), stop=(k == (b + 1) * KB - 1 and q == 2))
                                mm.then_inc(acc_full, 1)
                        pe.wait_ge(acc_full, n * 6 + 6)
                        pe.sem_inc(w_free, 1)

            @block.vector
            def _(dve):
                dve.sem_inc(raw_free, 2)
                dve.sem_inc(gate_free, 2)
                dve.sem_inc(prod, 6)
                dve.sem_inc(w_free, 2)

                def split_weights(n, j, round):
                    dve.wait_ge(w_in[j], round * 32 + 32)
                    dve.wait_ge(w_free, n + 1)
                    dve.tensor_copy(whi[j][:], raw[j][:]).then_inc(w_hi, 1)
                    dve.wait_ge(w_hi, n + 1)
                    dve.tensor_tensor(wlo[j][:], raw[j][:], f32(whi[j][:]), ALU.subtract).then_inc(w_lo, 1)
                    dve.wait_ge(w_lo, n + 1)
                    dve.sem_inc(raw_free, 1)

                def merge(n, j, round, more=True):
                    if more:
                        split_weights(n + 1, 1 - j, round + j)
                    dve.wait_ge(gate_in[j], round * 16 + 16)
                    for c in range(3):
                        tok = slice(c * TCH, (c + 1) * TCH)
                        for b in range(2):
                            dve.wait_ge(acc_full, n * 6 + c * 2 + b + 1)
                            gt = gate[j][:, b, tok]
                            dve.tensor_tensor(gt, acc[c * 2 + b][:, 0:TCH], gt, ALU.mult).then_inc(prod, 1)
                    dve.wait_ge(prod, n * 6 + 12)
                    row = (lambda a: a[:, n, :]) if isinstance(n, int) else (lambda a: a[:, ds(n, 1), :].rearrange("p a t -> p (a t)"))
                    hi, lo = row(m_hi), row(m_lo)
                    dve.tensor_tensor(hi, gate[j][:, 0, :], gate[j][:, 1, :], ALU.add).then_inc(m_hi_done, 1)
                    dve.wait_ge(m_hi_done, n + 1)
                    dve.tensor_tensor(gate[j][:, 0, :], gate[j][:, 0, :], gate[j][:, 1, :], ALU.add).then_inc(merged, 1)
                    dve.wait_ge(merged, n + 1)
                    dve.tensor_tensor(lo, gate[j][:, 0, :], f32(hi), ALU.subtract).then_inc(m_split, 1)
                    dve.wait_ge(m_split, n + 1)
                    dve.sem_inc(gate_free, 1)

                for u in range(NU):
                    src, hi, lo = oT(u)
                    dve.wait_ge(oT_hi_done, u + 1)
                    dve.tensor_tensor(lo, src, f32(hi), ALU.subtract).then_inc(oT_split, 1)
                    if u == 3:
                        split_weights(0, 0, 0)
                with dve.Fori(0, KD // 2 - 1) as i:
                    merge(i * 2, 0, i)
                    merge(i * 2 + 1, 1, i)
                merge(KD - 2, 0, KD // 2 - 1)
                merge(KD - 1, 1, KD // 2 - 1, more=False)


def output_and_norm(nc, io, g):
    NU = TT + 1
    with Scope(nc, "out") as s:
        raw = g.wo_raw
        whi = [s.sb(f"whi{i}", [P, KD, 512], F32R) for i in range(2)]
        wlo = [s.sb(f"wlo{i}", [P, KD, 512], F32R) for i in range(2)]
        ga = s.sb("ga", [P, D])
        gs = s.sb("gs", [NDEC, D])
        tmp = [s.sb(f"tmp{i}", [P, 512]) for i in range(2)]
        hf = [s.sb(f"hf{i}", [P, 512]) for i in range(2)]
        junk = raw[0][:, 0:4, :].rearrange("p a b -> p (a b)")
        ssq = s.sb("ssq", [P, NU])
        rstd = s.sb("rstd", [P, NU])
        aT = s.sb("aT", [P, KD, NC9])
        hs = s.sb("hs", [P, KD, NDEC])
        acc = [s.ps(f"acc{i}", [P, 512]) for i in range(4)]
        pt = [s.ps(f"pt{i}", [P, 512]) for i in range(3)]
        pc = s.ps("pc", [P, KD, NDEC])
        h_hi, h_lo = g.words_hi, g.words_lo
        w_in, x_in, ga_in = g.wo_in, [s.pool_sem(f"x_in{n}") for n in range(NU)], s.sem("ga_in")
        w_hi, w_lo, acc_full, acc_free, scaled = (s.sem(x) for x in ("w_hi", "w_lo", "acc_full", "acc_free", "scaled"))
        x2_ready, ss0, sq, mean, root, xn = (s.sem(x) for x in ("x2_ready", "ss0", "sq", "mean", "root", "xn"))
        x2_out = [s.sem(f"x2_out{n}") for n in range(NU)]
        rs_done = s.sem("rs_done")
        h_ps, h_sb, h_hi_done, h_split, coef, hs_ps = (s.sem(x) for x in ("h_ps", "h_sb", "h_hi_done", "h_split", "coef", "hs_ps"))
        w = io["w_out"][0].rearrange("(k p) n -> p k n", p=P)
        x_v = io["x_prompt"][0].rearrange("(t p) d -> p t d", p=P)
        x2_v = io["x2_d"].rearrange("(t p) d -> p t d", p=P)
        order = [0, 1, 2, 3, 4, 5, "half 0", 6, 7, TT, "half 1", "decode"]
        tiles = [t for t in order if isinstance(t, int)]
        rows = lambda t: P if t < TT else NDEC
        unit_tile = lambda u: (tiles[u % 2], u // 2) if u < 4 else (tiles[u // 2], u % 2)
        product_units = lambda n: [range(0, 3), range(3, 4)][n] if n < 2 else range(2 * n, 2 * n + 2)
        with nc.Block() as block:

            @block.sync
            def _(sp):
                for i in range(2, 4):
                    sp.wait_ge(w_lo, i - 1)
                    sp.dma_start(raw[i % 2][:], w[:, :, i * 256:(i + 1) * 256]).then_inc(w_in[i], 16)
                sp.dma_start(ga[:], io["mod_d"][NDEC:NC9, 2 * D:3 * D].broadcast_to([P, D])).then_inc(ga_in, 16)
                sp.dma_start(gs[:], io["mod_d"][0:NDEC, 2 * D:3 * D]).then_inc(ga_in, 16)
                for n, t in enumerate(tiles):
                    sp.wait_ge(x2_ready, n + 1)
                    r = rows(t)
                    sp.dma_start(x2_v[:, t, :] if t < TT else io["x2s_d"], g.x2[0:r, t, :]).then_inc(x2_out[n], 16)
                for n in range(NU):
                    sp.wait_ge(x2_out[n], 16)

            @block.gpsimd
            def _(pool):
                for n, t in enumerate(tiles):
                    pool.dma_start(g.x2[0:rows(t), t, :], x_v[:, t, :] if t < TT else io["x_sample"].rearrange("b t d -> (b t) d")
                                   ).then_inc(x_in[n], 16)

            @block.scalar
            def _(act):
                for i in range(4):
                    act.wait_ge(w_in[i], 16)
                    act.activation(whi[i // 2][:, :, i % 2 * 256:i % 2 * 256 + 256], raw[i % 2][:], ACT.Copy).then_inc(w_hi, 1)
                n = 0
                for t in order:
                    if isinstance(t, int):
                        r = rows(t)
                        act.wait_ge(x2_ready, n + 1)
                        if n == 0:
                            act.wait_ge(ss0, 1)
                            act.wait_ge(w_lo, 4)
                        else:
                            act.wait_ge(sq, n)
                        act.activation(junk[0:r], g.x2[0:r, t, :], ACT.Square, accum_out=ssq[0:r, t:t + 1]).then_inc(sq, 1)
                        act.wait_ge(mean, n + 1)
                        act.activation(rstd[0:r, t:t + 1], rstd[0:r, t:t + 1], ACT.Sqrt).then_inc(root, 1)
                        n += 1
                    elif t != "decode":
                        for k in range(KD):
                            u = int(t[-1]) * KD + k
                            act.wait_ge(h_ps, u + 1)
                            act.wait_ge(coef, 1)
                            if u >= 2:
                                act.wait_ge(h_split, u - 1)
                            act.activation(hf[u % 2][:], pt[u % 3][:], ACT.Identity, bias=g.modT[:, 3 * KD + k, NDEC:NC9],
                                           scale=aT[:, k, NDEC:NC9]).then_inc(h_sb, 1)

            @block.tensor
            def _(pe):
                pe.wait_ge(w_lo, 2)
                n = 0
                for t in order:
                    if isinstance(t, int):
                        for u in product_units(n):
                            tt, c = unit_tile(u)
                            r = rows(tt)
                            tok = slice(tt * P, tt * P + r)
                            if u == 2:
                                pe.wait_ge(w_lo, 4)
                            if u >= 4:
                                pe.wait_ge(acc_free, u - 3)
                            for k in range(KD):
                                for q, (a, b) in enumerate(((h_hi, whi), (h_lo, whi), (h_hi, wlo))):
                                    mm = pe.matmul(acc[u % 4][0:r, :], a[:, k, tok], b[c][:, k, :],
                                                   start=(k == 0 and q == 0), stop=(k == KD - 1 and q == 2))
                            mm.then_inc(acc_full, 1)
                        n += 1
                    elif t == "decode":
                        for k in range(KD):
                            mm = pe.transpose(pc[:, k, :], g.x2[0:NDEC, TT, k * P:(k + 1) * P], g.ident[0:NDEC, 0:NDEC])
                        mm.then_inc(hs_ps, 1)
                    else:
                        half = int(t[-1])
                        pe.wait_ge(xn, 4 if half == 0 else NU)
                        for k in range(KD):
                            u = half * KD + k
                            if u >= 3:
                                pe.wait_ge(h_sb, u - 2)
                            for q in range(4):
                                mm = pe.transpose(pt[u % 3][:, q * P:(q + 1) * P], g.x2[:, half * 4 + q, k * P:(k + 1) * P], g.ident[:])
                            mm.then_inc(h_ps, 1)

            @block.vector
            def _(dve):
                dve.memset(ssq[:], 0.0).then_inc(ss0, 1)
                dve.scalar_tensor_tensor(out=aT[:], in0=g.modT[:, 4 * KD:5 * KD, :], scalar=1.0,
                                         in1=g.gT[:, KD:2 * KD].unsqueeze(2).broadcast_to([P, KD, NC9]), op0=ALU.add, op1=ALU.mult).then_inc(coef, 1)
                for i in range(4):
                    hi, lo = (w[i // 2][:, :, i % 2 * 256:i % 2 * 256 + 256] for w in (whi, wlo))
                    dve.wait_ge(w_hi, i + 1)
                    dve.tensor_tensor(lo, raw[i % 2][:], f32(hi), ALU.subtract).then_inc(w_lo, 1)
                dve.wait_ge(ga_in, 32)

                def normalise(m, t):
                    r = rows(t)
                    one = rstd[0:r, t:t + 1]
                    dve.wait_ge(sq, m + 1)
                    dve.tensor_scalar(one, ssq[0:r, t:t + 1], 1.0 / D, EPS, ALU.mult, ALU.add).then_inc(mean, 1)
                    dve.wait_ge(root, m + 1)
                    dve.reciprocal(one, one).then_inc(rs_done, 1)
                    dve.wait_ge(rs_done, m + 1)
                    dve.wait_ge(x2_out[m], 16)
                    dve.tensor_scalar(g.x2[0:r, t, :], g.x2[0:r, t, :], one, None, ALU.mult).then_inc(xn, 1)

                n = 0
                for t in order:
                    if isinstance(t, int):
                        for u in product_units(n):
                            tt, c = unit_tile(u)
                            r = rows(tt)
                            cs = slice(c * 512, (c + 1) * 512)
                            gate = ga if tt < TT else gs
                            dve.wait_ge(acc_full, u + 1)
                            if c == 0:
                                dve.wait_ge(x_in[tiles.index(tt)], 16)
                            dve.tensor_tensor(tmp[u % 2][0:r], acc[u % 4][0:r, :], gate[0:r, cs], ALU.mult).then_inc(acc_free, 1)
                            dve.wait_ge(acc_free, u + 1)
                            dve.tensor_tensor(g.x2[0:r, tt, cs], g.x2[0:r, tt, cs], tmp[u % 2][0:r], ALU.add).then_inc(scaled, 1)
                        dve.wait_ge(scaled, product_units(n)[-1] + 1)
                        dve.sem_inc(x2_ready, 1)
                        if n and n != 6:
                            normalise(n - 1, tiles[n - 1])
                        if n in (5, TT):
                            normalise(n, t)
                        n += 1
                    elif t == "decode":
                        dve.wait_ge(hs_ps, 1)
                        dve.tensor_tensor(hs[:], pc[:], aT[:, :, 0:NDEC], ALU.mult).then_inc(coef, 1)
                        dve.wait_ge(coef, 2)
                        dve.tensor_tensor(hs[:], hs[:], g.modT[:, 3 * KD:4 * KD, 0:NDEC], ALU.add).then_inc(coef, 1)
                        dve.wait_ge(coef, 3)
                        dve.tensor_copy(h_hi[:, :, SEQ:NTOK], hs[:]).then_inc(coef, 1)
                        dve.wait_ge(coef, 4)
                        dve.tensor_tensor(h_lo[:, :, SEQ:NTOK], hs[:], f32(h_hi[:, :, SEQ:NTOK]), ALU.subtract).then_inc(coef, 1)
                    else:
                        half = int(t[-1])
                        for k in range(KD):
                            u = half * KD + k
                            dve.wait_ge(h_sb, u + 1)
                            hi = h_hi[:, k, half * 512:(half + 1) * 512]
                            lo = h_lo[:, k, half * 512:(half + 1) * 512]
                            dve.tensor_copy(hi, hf[u % 2][:]).then_inc(h_hi_done, 1)
                            dve.wait_ge(h_hi_done, u + 1)
                            dve.tensor_tensor(lo, hf[u % 2][:], f32(hi), ALU.subtract).then_inc(h_split, 1)


def feed_forward(nc, io, g):
    NF = D_FF // P
    NU = TT + 1
    NO = 2 * NU
    with Scope(nc, "ffn") as s:
        raw_u = [s.sb(f"raw_u{i}", [P, 2 * KD, P]) for i in range(2)]
        uhi = [s.sb(f"uhi{i}", [P, 2 * KD, P], F32R) for i in range(2)]
        ulo = [s.sb(f"ulo{i}", [P, 2 * KD, P], F32R) for i in range(2)]
        raw_o = [s.sb(f"raw_o{i}", [P, D]) for i in range(2)]
        ohi = [s.sb(f"ohi{i}", [P, D], F32R) for i in range(2)]
        olo = [s.sb(f"olo{i}", [P, D], F32R) for i in range(2)]
        sg = [s.sb(f"sg{i}", [P, TCH]) for i in range(2)]
        av = [s.sb(f"av{i}", [P, TCH]) for i in range(2)]
        a_hi = [s.sb(f"a_hi{i}", [P, NTOK], F32R) for i in range(2)]
        a_lo = [s.sb(f"a_lo{i}", [P, NTOK], F32R) for i in range(2)]
        ga, gs = raw_o[0], raw_o[1]
        xr = [raw_u[i // 2][:, i % 2 * KD:(i % 2 + 1) * KD, :].rearrange("p k n -> p (k n)") for i in range(4)]
        total = g.x2
        pg = [s.ps(f"pg{i}", [P, 512]) for i in range(2)]
        pv = [s.ps(f"pv{i}", [P, 512]) for i in range(2)]
        po = [s.ps(f"po{i}", [P, 512]) for i in range(4)]
        h_hi, h_lo = g.words_hi, g.words_lo
        u_in, o_in = [s.sem(f"u_in{i}") for i in range(2)], [s.sem(f"o_in{i}") for i in range(2)]
        raw_u_free, raw_o_free, u_hi_done, u_ready, o_hi_done, o_ready = (
            s.sem(x) for x in ("raw_u_free", "raw_o_free", "u_hi_done", "u_ready", "o_hi_done", "o_ready"))
        gate_full, val_full, silu_done, a_done, a_hi_done, a_ready = (
            s.sem(x) for x in ("gate_full", "val_full", "silu_done", "a_done", "a_hi_done", "a_ready"))
        o_full, o_read, ga_in = s.sem("o_full"), s.sem("o_read"), s.pool_sem("ga_in")
        xr_in = [s.sem(f"xr_in{t}") for t in range(NU)]
        tot0, y1, y_ready, y_out = s.sem("tot0"), s.sem("y1"), s.sem("y_ready"), s.sem("y_out")
        w_u = io["w_ffn_in"][0].rearrange("(k p) n -> p k n", p=P)
        w_o = io["w_ffn_out"][0]
        x2_v = io["x2_d"].rearrange("(t p) d -> p t d", p=P)
        y_v = io["y_p"][0].rearrange("(t p) d -> p t d", p=P)
        rows = lambda t: P if t < TT else NDEC
        with nc.Block() as block:

            @block.sync
            def _(sp):
                with sp.Fori(0, NF // 2) as i:
                    for j in range(2):
                        f = i * 2 + j
                        sp.wait_ge(raw_u_free, f + 1)
                        sp.dma_start(raw_u[j][:, 0:KD, :], w_u[:, :, ds(f * P, P)]).then_inc(u_in[j], 16)
                        sp.dma_start(raw_u[j][:, KD:2 * KD, :], w_u[:, :, ds(f * P + D_FF, P)]).then_inc(u_in[j], 16)
                        sp.wait_ge(raw_o_free, f + 1)
                        sp.dma_start(raw_o[j][:], w_o[ds(f * P, P), :]).then_inc(o_in[j], 16)
                for t in range(NU):
                    r = rows(t)
                    sp.wait_ge(y_ready, t + 1)
                    sp.dma_start(y_v[:, t, :] if t < TT else io["y_s"].rearrange("b t d -> (b t) d"),
                                 total[0:r, t, :]).then_inc(y_out, 16)
                sp.wait_ge(y_out, 16 * NU)

            @block.gpsimd
            def _(pool):
                pool.wait_ge(o_ready, NF)
                pool.dma_start(ga[:], io["mod_d"][NDEC:NC9, 5 * D:6 * D].broadcast_to([P, D])).then_inc(ga_in, 16)
                pool.dma_start(gs[0:NDEC, :], io["mod_d"][0:NDEC, 5 * D:6 * D]).then_inc(ga_in, 16)
                for t in range(NU):
                    r = rows(t)
                    pool.wait_ge(xr_in[t], 16)
                    pool.wait_ge(y1, t + 1)
                    pool.tensor_tensor(total[0:r, t, :], total[0:r, t, :], xr[t % 4][0:r], ALU.add).then_inc(y_ready, 1)

            @block.scalar
            def _(act):

                def hi_hidden(f, j):
                    act.wait_ge(u_in[j], (f - j) * 16 + 32)
                    act.activation(uhi[j][:], raw_u[j][:], ACT.Copy).then_inc(u_hi_done, 1)

                def hi_output(f, j):
                    act.wait_ge(o_in[j], (f - j) * 8 + 16)
                    act.activation(ohi[j][:], raw_o[j][:], ACT.Copy).then_inc(o_hi_done, 1)

                def silu(f, j):
                    for c in range(3):
                        n = f * 3 + c
                        act.wait_ge(gate_full, n + 1)
                        act.wait_ge(a_done, n + 1)
                        act.activation(sg[(j + c) % 2][:], pg[(j + c) % 2][:, 0:TCH], ACT.Silu).then_inc(silu_done, 1)
                        if c == 0:
                            hi_output(f, j)

                hi_hidden(0, 0)
                hi_hidden(1, 1)
                silu(0, 0)
                with act.Fori(0, NF // 2 - 1) as i:
                    for j in range(2):
                        f = i * 2 + j
                        act.wait_ge(val_full, f * 3 + 3)
                        hi_hidden(f + 2, j)
                        silu(f + 1, 1 - j)
                silu(NF - 1, 1)
                act.wait_ge(u_ready, NF)
                for t in range(NU):
                    if t >= 4:
                        act.wait_ge(y_ready, t - 3)
                    act.dma_start(xr[t % 4][0:rows(t)], x2_v[:, t, :] if t < TT else io["x2s_d"]).then_inc(xr_in[t], 16)

            def hidden(pe, f, j):
                pe.wait_ge(u_ready, f + 1)
                for c in range(3):
                    n = f * 3 + c
                    b = (j + c) % 2
                    tok = slice(c * TCH, (c + 1) * TCH)
                    pe.wait_ge(a_done, n + 1)
                    for v, (bank, full) in enumerate(((pg, gate_full), (pv, val_full))):
                        for k in range(KD):
                            for q, (w, h) in enumerate(((uhi, h_hi), (ulo, h_hi), (uhi, h_lo))):
                                mm = pe.matmul(bank[b][:, 0:TCH], w[j][:, v * KD + k, :], h[:, k, tok],
                                               start=(k == 0 and q == 0), stop=(k == KD - 1 and q == 2))
                        mm.then_inc(full, 1)

            def output(pe, f, j):
                pe.wait_ge(o_ready, f + 1)
                pe.wait_ge(a_ready, f * 3 + 3)
                for t in range(NU):
                    r = rows(t)
                    tok = slice(t * P, t * P + r)
                    for c in range(2):
                        u = t * 2 + c
                        cs = slice(c * 512, (c + 1) * 512)
                        pe.wait_ge(o_read, f * NO + u + 1)
                        for q, (a, w) in enumerate(((a_hi, ohi), (a_lo, ohi), (a_hi, olo))):
                            mm = pe.matmul(po[(j * NO + u) % 4][0:r, :], a[j][:, tok], w[j][:, cs], start=(q == 0), stop=(q == 2))
                        mm.then_inc(o_full, 1)

            @block.tensor
            def _(pe):
                hidden(pe, 0, 0)
                with pe.Fori(0, NF // 2 - 1) as i:
                    hidden(pe, i * 2 + 1, 1)
                    output(pe, i * 2, 0)
                    hidden(pe, i * 2 + 2, 0)
                    output(pe, i * 2 + 1, 1)
                hidden(pe, NF - 1, 1)
                output(pe, NF - 2, 0)
                output(pe, NF - 1, 1)

            def split_hidden(dve, f, j):
                dve.wait_ge(u_hi_done, f + 1)
                dve.tensor_tensor(ulo[j][:], raw_u[j][:], f32(uhi[j][:]), ALU.subtract).then_inc(u_ready, 1)
                dve.wait_ge(u_ready, f + 1)
                dve.sem_inc(raw_u_free, 1)

            def split_output(dve, f, j):
                dve.wait_ge(o_hi_done, f + 1)
                dve.tensor_tensor(olo[j][:], raw_o[j][:], f32(ohi[j][:]), ALU.subtract).then_inc(o_ready, 1)
                dve.wait_ge(o_ready, f + 1)
                dve.sem_inc(raw_o_free, 1)

            def gated(dve, f, j):
                for c in range(3):
                    n = f * 3 + c
                    b = (j + c) % 2
                    tok = slice(c * TCH, (c + 1) * TCH)
                    dve.wait_ge(silu_done, n + 1)
                    dve.wait_ge(val_full, n + 1)
                    dve.tensor_tensor(av[b][:], pv[b][:, 0:TCH], sg[b][:], ALU.mult).then_inc(a_done, 1)
                    dve.wait_ge(a_done, n + 3)
                    dve.tensor_copy(a_hi[j][:, tok], av[b][:]).then_inc(a_hi_done, 1)
                    dve.wait_ge(a_hi_done, n + 1)
                    dve.tensor_tensor(a_lo[j][:, tok], av[b][:], f32(a_hi[j][:, tok]), ALU.subtract).then_inc(a_ready, 1)
                    if c == 1:
                        split_output(dve, f, j)

            def accumulate(dve, f, j, last=False):
                for t in range(NU):
                    r = rows(t)
                    for c in range(2):
                        u = t * 2 + c
                        part = total[0:r, t, c * 512:(c + 1) * 512]
                        dve.wait_ge(o_full, f * NO + u + 1)
                        dve.tensor_tensor(part, part, po[(j * NO + u) % 4][0:r, :], ALU.add).then_inc(o_read, 1)
                    if last:
                        gate = ga if t < TT else gs
                        dve.wait_ge(o_read, f * NO + t * 2 + 6)
                        dve.tensor_tensor(total[0:r, t, :], total[0:r, t, :], gate[0:r, :], ALU.mult).then_inc(y1, 1)

            @block.vector
            def _(dve):
                dve.sem_inc(raw_u_free, 2)
                dve.sem_inc(raw_o_free, 2)
                dve.sem_inc(a_done, 2)
                dve.sem_inc(o_read, 4)
                split_hidden(dve, 0, 0)
                split_hidden(dve, 1, 1)
                dve.memset(total[:], 0.0).then_inc(tot0, 1)
                gated(dve, 0, 0)
                dve.wait_ge(tot0, 1)
                with dve.Fori(0, NF // 2 - 1) as i:
                    for j in range(2):
                        f = i * 2 + j
                        dve.wait_ge(val_full, f * 3 + 3)
                        split_hidden(dve, f + 2, j)
                        gated(dve, f + 1, 1 - j)
                        accumulate(dve, f, j)
                gated(dve, NF - 1, 1)
                accumulate(dve, NF - 2, 0)
                dve.wait_ge(ga_in, 32)
                accumulate(dve, NF - 1, 1, last=True)


class Globals:
    pass


def trunk_step(nc, io):
    g = Globals()
    Scope.cleared = []
    with Scope(nc, "g") as s:
        g.ident = s.sb("ident", [P, P])
        g.modT = s.sb("modT", [P, 6 * KD, NC9])
        g.gT = s.sb("gT", [P, 16])
        g.const_ready = s.sem("const_ready")
        z0 = s.sem("z0")
        zs = Scope(nc, "zs")
        g.z = zs.sb("z", [P, TT + 1, ZW], side="right")
        with nc.Block() as block:

            @block.gpsimd
            def _(pool):
                pool.memset(g.ident[:], 0.0).then_inc(g.const_ready, 1)
                pool.wait_ge(g.const_ready, 1)
                pool.affine_select(out=g.ident[:], in_=g.ident[:], compare_op=ALU.not_equal, fill=1.0, base=0,
                                   pattern=[[-1, P]], channel_multiplier=1).then_inc(g.const_ready, 1)
        h = Scope(nc, "h")
        g.hT_hi = h.sb("hT_hi", [P, KD, NTOK], F32R)
        g.hT_lo = h.sb("hT_lo", [P, KD, NTOK], F32R)
        modulation_and_h(nc, io, g)
        project_token_major(nc, io, g)
        with Scope(nc, "a", side="right") as a:
            attention_tiles(g, a)
            with Scope(nc, "at", side="right") as at:
                gates_and_constants(nc, io, g, at)
                h.__exit__(None, None, None)
                prepare_keys(nc, io, g, at)
                nsa_attention(nc, io, g)
                diff_attention(nc, io, g)
            decode_attention(nc, io, g)
        with Scope(nc, "late") as late:
            g.x2 = late.sb("x2", [P, TT + 1, D])
            wr = Scope(nc, "wo")
            g.wo_raw = [wr.sb(f"raw{i}", [P, KD, 256]) for i in range(2)]
            g.wo_in = [late.sem(f"wo_in{i}") for i in range(4)]
            with Scope(nc, "oT") as o:
                g.oT_hi = o.sb("hi", [P, KD, NTOK], F32R)
                g.oT_lo = o.sb("lo", [P, KD, NTOK], F32R)
                zs.__exit__(None, None, None)
                g.words_hi = late.sb("words_hi", [P, KD, NTOK], F32R, side="right")
                g.words_lo = late.sb("words_lo", [P, KD, NTOK], F32R, side="right")
                merge_branches(nc, io, g)
            output_and_norm(nc, io, g)
            wr.__exit__(None, None, None)
            feed_forward(nc, io, g)


_OUTS = [("y_p", (1, SEQ, D)), ("y_s", (NDEC, 1, D)), ("kv_p", (1, 1, SEQ, CACHE_W)),
         ("kv_s", (1, NDEC, 1, CACHE_W)), ("win_p", (1, 1, WINDOW, 128)), ("win_s", (1, NDEC, WINDOW, 128))]
_SCRATCH = [("mod_d", (NC9, 6 * D)), ("gate_d", (MC, NTOK)), ("x2_d", (SEQ, D)), ("x2s_d", (NDEC, D)), ("new_d", (NDEC, C_G - C_CK)), ("dec_d", (NDEC * 8, 5 * HD))]


def kernel(**inputs):
    import numpy as _np
    import concourse.bacc as _bacc
    from concourse.bass_utils import run_bass_kernel_spmd as _run

    nc = _bacc.Bacc("TRN2", target_bir_lowering=False, num_devices=1)
    arrays, io = {}, {}
    for name, a in inputs.items():
        a = _np.ascontiguousarray(a)
        arrays[f"in_{name}"] = a
        io[name] = nc.dram_tensor(f"in_{name}", a.shape, mybir.dt.from_np(a.dtype), kind="ExternalInput").ap()
    arrays["in_dec_tab"] = decode_table()
    io["dec_tab"] = nc.dram_tensor("in_dec_tab", (16, T_END), F32, kind="ExternalInput").ap()
    for name, shape in _OUTS:
        io[name] = nc.dram_tensor(f"out_{name}", shape, F32, kind="ExternalOutput").ap()
    for name, shape in _SCRATCH:
        io[name] = nc.dram_tensor(name, shape, F32).ap()
    trunk_step(nc, io)
    r = _run(nc, [arrays], core_ids=[0])
    return tuple(r.results[0][f"out_{name}"] for name, _ in _OUTS)
```
